# Optimizing a Trainium2 kernel written in Bass

```python
import jax, jax.numpy as jnp
from jax import lax
import numpy as np

D_MODEL = 4096
BATCH = 1
SEQ = 256
DEPTH = 1

CTX_LEN = 256
GRID_W = 64
MIX_WIDTH = D_MODEL
RET_WIDTH = MIX_WIDTH // 2
CONV_WIDTH = MIX_WIDTH - RET_WIDTH
RET_HEADS = 8
RET_HEAD_DIM = RET_WIDTH // RET_HEADS
RET_CHUNK = 128
CONV_KERNEL = 31
ROPE_BASE = 10000.0
NORM_EPS = 1e-6
IN_COLS = 4 * RET_WIDTH + 3 * CONV_WIDTH

kernel_name = "hymba_retention_conformer_dit_block"

def rms_norm(x, g):
    xf = x.astype(jnp.float32)
    var = jnp.mean(xf * xf, axis=-1, keepdims=True)
    return (xf * lax.rsqrt(var + NORM_EPS) * g.astype(jnp.float32)).astype(x.dtype)

def layer_norm(x, g, b):
    xf = x.astype(jnp.float32)
    mu = jnp.mean(xf, axis=-1, keepdims=True)
    var = jnp.mean(jnp.square(xf - mu), axis=-1, keepdims=True)
    y = (xf - mu) * lax.rsqrt(var + NORM_EPS) * g.astype(jnp.float32) + b.astype(jnp.float32)
    return y.astype(x.dtype)

def head_group_norm(y, g):
    mu = jnp.mean(y, axis=-1, keepdims=True)
    var = jnp.mean(jnp.square(y - mu), axis=-1, keepdims=True)
    yn = (y - mu) * lax.rsqrt(var + NORM_EPS)
    b, h, n, d = y.shape
    return yn.transpose(0, 2, 1, 3).reshape(b, n, h * d) * g.astype(jnp.float32)

def to_heads(t):
    b, n, _ = t.shape
    return t.reshape(b, n, RET_HEADS, RET_HEAD_DIM).transpose(0, 2, 1, 3)

def grid_rope_tables(n_tokens):
    rows = n_tokens // GRID_W
    pos_r = jnp.repeat(jnp.arange(rows, dtype=jnp.float32), GRID_W)
    pos_c = jnp.tile(jnp.arange(GRID_W, dtype=jnp.float32), rows)
    n_freq = RET_HEAD_DIM // 4
    inv_freq = ROPE_BASE ** (-jnp.arange(n_freq, dtype=jnp.float32) / n_freq)
    ang_r = pos_r[:, None] * inv_freq[None, :]
    ang_c = pos_c[:, None] * inv_freq[None, :]
    return (jnp.cos(ang_r), jnp.sin(ang_r), jnp.cos(ang_c), jnp.sin(ang_c))

def _rotate(xh, cos, sin):
    half = xh.shape[-1] // 2
    x1, x2 = xh[..., :half], xh[..., half:]
    cos = cos.astype(xh.dtype)
    sin = sin.astype(xh.dtype)
    return jnp.concatenate([x1 * cos - x2 * sin, x2 * cos + x1 * sin], axis=-1)

def apply_grid_rope(t, rope):
    cos_r, sin_r, cos_c, sin_c = rope
    half = t.shape[-1] // 2
    return jnp.concatenate([_rotate(t[..., :half], cos_r, sin_r),
                            _rotate(t[..., half:], cos_c, sin_c)], axis=-1)

def retention_direction(q, k, v, log_g, r0):
    q = q.astype(jnp.float32)
    k = k.astype(jnp.float32)
    v = v.astype(jnp.float32)
    b, h, n, dk = q.shape
    dv = v.shape[-1]
    nc = n // RET_CHUNK
    qc = q.reshape(b, h, nc, RET_CHUNK, dk)
    kc = k.reshape(b, h, nc, RET_CHUNK, dk)
    vc = v.reshape(b, h, nc, RET_CHUNK, dv)
    idx = jnp.arange(RET_CHUNK, dtype=jnp.float32)
    lg = log_g.astype(jnp.float32)[:, None]
    rel = idx[:, None] - idx[None, :]
    intra = jnp.where(rel >= 0, jnp.exp(lg[:, :, None] * jnp.maximum(rel, 0.0)), 0.0)
    scores = jnp.einsum('bhnid,bhnjd->bhnij', qc, kc) * intra[None, :, None]
    inner = jnp.einsum('bhnij,bhnje->bhnie', scores, vc)
    k_w = jnp.exp(lg * (RET_CHUNK - 1.0 - idx))
    chunk_kv = jnp.einsum('bhnjd,bhnje,hj->nbhde', kc, vc, k_w)
    chunk_decay = jnp.exp(lg[:, 0] * RET_CHUNK)[None, :, None, None]

    def step(r, s):
        return r * chunk_decay + s, r

    r_last, r_prev = lax.scan(step, r0.astype(jnp.float32), chunk_kv)
    q_w = jnp.exp(lg * (idx + 1.0))
    cross = jnp.einsum('bhnid,hi,nbhde->bhnie', qc, q_w, r_prev)
    return (inner + cross).reshape(b, h, n, dv), r_last

def retention_final_state(k, v, log_g, reverse):
    k = k.astype(jnp.float32)
    v = v.astype(jnp.float32)
    n = k.shape[2]
    pos = jnp.arange(n, dtype=jnp.float32)
    steps = pos if reverse else (n - 1.0 - pos)
    w = jnp.exp(log_g.astype(jnp.float32)[:, None] * steps[None, :])
    return jnp.einsum('bhnd,bhne,hn->bhde', k, v, w)

def depthwise_conv(u, w, b):
    ch = u.shape[-1]
    rhs = w.astype(u.dtype)[:, None, :]
    y = lax.conv_general_dilated(u, rhs, window_strides=(1,),
                                 padding=[(CONV_KERNEL // 2, CONV_KERNEL // 2)],
                                 dimension_numbers=('NWC', 'WIO', 'NWC'),
                                 feature_group_count=ch)
    return y + b.astype(u.dtype)

def mixer_output(ret_y, proj, conv_dw_w, conv_dw_b, conv_ln_g, conv_ln_b, w_out):
    dt = proj.dtype
    r = RET_WIDTH
    cw = CONV_WIDTH
    g_ret = proj[..., 3 * r:4 * r]
    a_conv = proj[..., 4 * r:4 * r + cw]
    b_conv = proj[..., 4 * r + cw:4 * r + 2 * cw]
    g_conv = proj[..., 4 * r + 2 * cw:]
    ret_branch = ret_y.astype(dt) * jax.nn.silu(g_ret)
    u = a_conv * jax.nn.sigmoid(b_conv)
    u = depthwise_conv(u, conv_dw_w, conv_dw_b)
    u = jax.nn.silu(layer_norm(u, conv_ln_g, conv_ln_b))
    conv_branch = u * jax.nn.silu(g_conv)
    return jnp.concatenate([ret_branch, conv_branch], axis=-1) @ w_out

def hybrid_layer(x, ctx, c, c_ctx, ada_w, ada_b, pre_g, post_g, w_in, lg_f, lg_b,
                 ret_gn_g, conv_dw_w, conv_dw_b, conv_ln_g, conv_ln_b, w_out, rope, update_ctx):
    r = RET_WIDTH
    shift, scale, gate = jnp.split(jax.nn.silu(c) @ ada_w + ada_b, 3, axis=-1)
    shift_c, scale_c, gate_c = jnp.split(jax.nn.silu(c_ctx) @ ada_w + ada_b, 3, axis=-1)
    h = rms_norm(x, pre_g) * (1.0 + scale[:, None]) + shift[:, None]
    hc = rms_norm(ctx, pre_g) * (1.0 + scale_c) + shift_c

    proj = h @ w_in
    q = apply_grid_rope(to_heads(proj[..., :r]), rope)
    k = apply_grid_rope(to_heads(proj[..., r:2 * r]), rope) * (RET_HEAD_DIM ** -0.5)
    v = to_heads(proj[..., 2 * r:3 * r])

    b = x.shape[0]
    zero_state = jnp.zeros((b, RET_HEADS, RET_HEAD_DIM, RET_HEAD_DIM), jnp.float32)
    if update_ctx:
        proj_c = hc @ w_in
        q_c = to_heads(proj_c[..., :r])
        k_c = to_heads(proj_c[..., r:2 * r]) * (RET_HEAD_DIM ** -0.5)
        v_c = to_heads(proj_c[..., 2 * r:3 * r])
        ctx_f, r_cf = retention_direction(q_c, k_c, v_c, lg_f, zero_state)
        ctx_b_rev, r_cb = retention_direction(jnp.flip(q_c, 2), jnp.flip(k_c, 2),
                                              jnp.flip(v_c, 2), lg_b, zero_state)
    else:
        kv_c = hc @ w_in[:, r:3 * r]
        k_c = to_heads(kv_c[..., :r]) * (RET_HEAD_DIM ** -0.5)
        v_c = to_heads(kv_c[..., r:])
        r_cf = retention_final_state(k_c, v_c, lg_f, reverse=False)
        r_cb = retention_final_state(k_c, v_c, lg_b, reverse=True)

    lat_f, _ = retention_direction(q, k, v, lg_f, r_cf)
    lat_b_rev, _ = retention_direction(jnp.flip(q, 2), jnp.flip(k, 2), jnp.flip(v, 2), lg_b, r_cb)
    ret = head_group_norm(lat_f + jnp.flip(lat_b_rev, 2), ret_gn_g)
    y = mixer_output(ret, proj, conv_dw_w, conv_dw_b, conv_ln_g, conv_ln_b, w_out)
    x_new = x + gate[:, None] * rms_norm(y, post_g)

    if update_ctx:
        ret_c = head_group_norm(ctx_f + jnp.flip(ctx_b_rev, 2), ret_gn_g)
        y_c = mixer_output(ret_c, proj_c, conv_dw_w, conv_dw_b, conv_ln_g, conv_ln_b, w_out)
        ctx = ctx + gate_c * rms_norm(y_c, post_g)
    return x_new, ctx

def setup_inputs(seed: int = 0) -> dict:
    key = jax.random.key(seed)
    ks = jax.random.split(key, 18)
    f32 = jnp.float32
    nrm = lambda k, s: jax.random.normal(k, s, f32)
    base_decay = jnp.log1p(-(2.0 ** (-5.0 - jnp.arange(RET_HEADS, dtype=f32))))
    return {
        "x": nrm(ks[0], (BATCH, SEQ, D_MODEL)),
        "c": nrm(ks[1], (BATCH, D_MODEL)),
        "ctx": nrm(ks[2], (BATCH, CTX_LEN, D_MODEL)),
        "c_ctx": nrm(ks[3], (D_MODEL,)),
        "ada_w": nrm(ks[4], (DEPTH, D_MODEL, 3 * D_MODEL)) * (0.5 * D_MODEL ** -0.5),
        "ada_b": 0.01 * nrm(ks[5], (DEPTH, 3 * D_MODEL)),
        "pre_norm_g": 1.0 + 0.05 * nrm(ks[6], (DEPTH, D_MODEL)),
        "post_norm_g": 1.0 + 0.05 * nrm(ks[7], (DEPTH, D_MODEL)),
        "w_in": nrm(ks[8], (DEPTH, D_MODEL, IN_COLS)) * (D_MODEL ** -0.5),
        "ret_log_decay_fwd": base_decay[None, :] * (1.0 + 0.1 * nrm(ks[9], (DEPTH, RET_HEADS))),
        "ret_log_decay_bwd": base_decay[None, :] * (1.0 + 0.1 * nrm(ks[10], (DEPTH, RET_HEADS))),
        "ret_gn_g": 1.0 + 0.05 * nrm(ks[11], (DEPTH, RET_WIDTH)),
        "conv_dw_w": nrm(ks[12], (DEPTH, CONV_KERNEL, CONV_WIDTH)) * (CONV_KERNEL ** -0.5),
        "conv_dw_b": 0.01 * nrm(ks[13], (DEPTH, CONV_WIDTH)),
        "conv_ln_g": 1.0 + 0.05 * nrm(ks[14], (DEPTH, CONV_WIDTH)),
        "conv_ln_b": 0.01 * nrm(ks[15], (DEPTH, CONV_WIDTH)),
        "w_out": nrm(ks[16], (DEPTH, MIX_WIDTH, D_MODEL)) * (MIX_WIDTH ** -0.5),
    }

def reference(x, c, ctx, c_ctx, ada_w, ada_b, pre_norm_g, post_norm_g, w_in,
              ret_log_decay_fwd, ret_log_decay_bwd, ret_gn_g, conv_dw_w, conv_dw_b,
              conv_ln_g, conv_ln_b, w_out):
    rope = grid_rope_tables(x.shape[1])
    for layer in range(DEPTH):
        x, ctx = hybrid_layer(
            x, ctx, c, c_ctx, ada_w[layer], ada_b[layer], pre_norm_g[layer], post_norm_g[layer],
            w_in[layer], ret_log_decay_fwd[layer], ret_log_decay_bwd[layer], ret_gn_g[layer],
            conv_dw_w[layer], conv_dw_b[layer], conv_ln_g[layer], conv_ln_b[layer], w_out[layer],
            rope, update_ctx=(layer < DEPTH - 1))
    return x


_drawn_inputs = setup_inputs


def setup_inputs(seed=0):
    import zlib

    import numpy as np

    out = dict(_drawn_inputs(seed))
    spreads = {}
    factors = {'ada_b': 4.012,
     'post_norm_g': 3.779,
     'ret_gn_g': 4.552,
     'conv_dw_b': 8.0,
     'conv_ln_g': 6.079,
     'conv_ln_b': 61.407}
    for name, (base, spread) in spreads.items():
        noise = np.random.default_rng([zlib.crc32(name.encode()), seed]).standard_normal(out[name].shape)
        drawn = base * np.exp(spread * noise) if base else spread * noise
        out[name] = __import__('jax').numpy.asarray(drawn.astype(out[name].dtype))
    for name, factor in factors.items():
        out[name] = (out[name] * factor).astype(out[name].dtype)
    return out
```

```python
from contextlib import ExitStack

import numpy as np

import concourse.bass as bass
from concourse import mybir

ALU = mybir.AluOpType
ACT = mybir.ActivationFunctionType
F32 = mybir.dt.float32
F32R = mybir.dt.float32r
AX = mybir.AxisListType

P = 128
D = 4096
N = 256
RET = D // 2
HD = 256
TAPS = 31
EPS = 1e-6
G = 512
KT = D // P
KH = KT // 2
PK = 2
NP = KH // PK
NPO = KT // PK
RAW = 4
ADA = 4
COLS_K, COLS_V, COLS_G, COLS_A, COLS_B, COLS_C = (RET * n for n in (1, 2, 3, 4, 5, 6))
MODEL_GROUPS = 7 * RET // G
ADA_BESIDE = [3, 3, 3, 3, 2, 2, 0, 0]
TAP_TILES = [(2, 0, 7), (3, 7, 7), (4, 14, 7), (5, 21, 7), (6, 28, 3)]
C_ID, C_SEL, C_J, C_COS, C_SIN, C_END = 0, 128, 130, 130 + 640, 130 + 640 + 512, 130 + 640 + 1024


def shape_constants():
    f = np.float32
    c = np.zeros((P, C_END), f)
    c[:, C_ID:C_ID + P] = np.eye(P, dtype=f)
    for q in range(4):
        for v in range(2):
            c[32 * q + v, C_SEL + v] = 1.0
    p = np.arange(P)[:, None]
    c[:, C_J:C_J + 640] = np.arange(640)[None, :] - p - P
    freq = f(10000.0) ** (-np.arange(64, dtype=f) / f(64))
    for t in range(2):
        tok = np.arange(P) + t * P
        for half, pos in enumerate((tok // 64, tok % 64)):
            ang = pos.astype(f)[:, None] * freq[None, :]
            at = t * 256 + half * 128
            c[:, C_COS + at:C_COS + at + 128] = np.tile(np.cos(ang), (1, 2))
            c[:, C_SIN + at:C_SIN + at + 64] = -np.sin(ang)
            c[:, C_SIN + at + 64:C_SIN + at + 128] = np.sin(ang)
    return c


class Count:

    def __init__(self, sem, start=0):
        self.sem, self.base, self.i, self.per, self.k = sem, start, 0, 0, 0

    def enter(self, i, per, first=0):
        if not self.per:
            self.base += self.k - first * per
        self.i, self.per, self.k = i, per, 0

    def landed(self, slot, slots):
        return self.i * (16 * self.per // slots) + 16 * ((self.base + self.k - slot) // slots + 1)

    def leave(self, turns):
        assert self.k == self.per, (self.sem, self.k, self.per)
        self.base += self.per * turns
        self.i = self.per = self.k = 0

    def up(self, by=1):
        self.k += by
        return self.now()

    def now(self, less=0):
        fixed = self.base + self.k - less
        return self.i * self.per + fixed if self.per else fixed


def block_kernel(nc, x, c, ctx_in, c_ctx, ada_w, ada_b, pre_norm_g, post_norm_g, w_in,
                 lg_f, lg_b, ret_gn_g, conv_dw_w, conv_dw_b, conv_ln_g, conv_ln_b, w_out, consts, out):
    with ExitStack() as ctx:
        def sem(name):
            return ctx.enter_context(nc.semaphore(name))

        def psum(name):
            return ctx.enter_context(nc.psum_tensor(name, [P, G], F32))

        START = 16512
        KB = 1024
        R_A, R_B, R_C, R_D, R_E, R_F = (START + n * KB for n in (0, 64, 96, 128, 160, 176))

        def at(name, shape, offset, dt=F32):
            return nc.alloc_sbuf_tensor_at(name, [P] + shape, dt, offset=offset)

        xs = at("x_rows", [4, D], R_A)
        h1 = [at("h1_hi", [KH, 2 * N], R_A, F32R), at("h1_lo", [KH, 2 * N], R_A + 32 * KB, F32R)]
        xT = [at("xT_first", [KH, 2 * N], R_C), at("xT_second", [KH, 2 * N], R_B)]
        h2 = [at("h2_hi", [KH, 2 * N], R_B, F32R), at("h2_lo", [KH, 2 * N], R_C, F32R)]
        raw = at("raw", [RAW, PK, G], R_D)
        whi = at("w_hi", [2, PK, G], R_D + 16 * KB, F32R)
        wlo = at("w_lo", [2, PK, G], R_D + 24 * KB, F32R)
        ada = at("ada_pieces", [ADA, PK, G], R_E)
        o = R_F
        def lasting(name, shape, dt=F32):
            nonlocal o
            t = at(name, shape, o, dt)
            o += (4 * int(np.prod(shape)) + 31) // 32 * 32
            return t
        cst = lasting("constants", [C_END])
        vt = lasting("vectors_T", [7, P])
        cT = lasting("silu_c_T", [KT, 2])
        modA = lasting("mod_scale", [KT, 2])
        modB = lasting("mod_shift", [KT, 2])
        gp = lasting("gate_post", [KT])
        stage = lasting("ada_rows", [G])
        mtmp = lasting("mod_tmp", [4, 2])
        lgrow = lasting("log_decays", [2, 8])
        lgs = lasting("decay_scales", [8, 3])
        lg4 = lasting("decay_scales_now", [2, 3])
        bst = lasting("bn", [4, 8, 6])
        mv = lasting("mean_var", [4, 2])
        rs = lasting("rstd", [4])
        half = lasting("minus_half", [4])
        last_o = o
        xtmp = at("h_tmp", [2, 2 * N], o)
        pst = at("partial_out", [2, 2 * G], o + 4 * KB)
        assert o + 12 * KB <= nc.sbuf_usable_end
        vin = at("vectors_in", [7, P], R_D)
        diag = at("rstd_diag", [4, P], o + 4 * KB)
        Y = at("y_T", [KT, N], R_A)
        a = R_A + 32 * KB
        def work(name, shape):
            nonlocal a
            t = at(name, shape, a)
            a += (4 * int(np.prod(shape)) + 31) // 32 * 32
            return t
        q_sb = work("q", [2, G])
        k_sb = work("k", [4, G])
        v_sb = work("v", [4, G])
        kT = work("k_T", [2, 2, 2 * N])
        qT = work("q_T", [2, 2, N])
        a = last_o
        Dm = work("decay", [2, 768])
        tmp = work("tmp", [1024])
        upad = work("u_padded", [2, N + TAPS - 1])
        acc = work("conv_acc", [2, N])
        ssum = work("conv_sums", [2, N])
        w4 = work("taps_now", [TAPS, 4])
        b4 = work("conv_bias_now", [4])
        gn4 = work("gn_now", [4])
        ones_c = work("ones_mean", [P])
        assert a <= nc.sbuf_usable_end, (a, nc.sbuf_usable_end)
        Pm = at("weights_T", [2, 4, N], R_A + 36 * KB)
        g_sb = at("g_T", [4, N], R_A + 36 * KB)
        bb = at("conv_b", [4, N], R_A + 32 * KB)
        ab = at("conv_a", [4, N], R_A + 44 * KB)
        lnm = at("ln_mean_rstd", [2, N], last_o)
        lnv = at("ln_var", [N], last_o + 2 * KB)
        lnh = at("ln_half", [N], last_o + 3 * KB)
        sl4 = at("silu_g", [2, 4, N], R_A + 52 * KB)
        yr = [at("y_hi", [KT, N], R_B, F32R), at("y_lo", [KT, N], R_C, F32R)]
        yo = at("y_out", [2, D], R_A + 32 * KB)
        xres = at("x_again", [2, D], R_A)
        o2 = last_o
        diag4 = at("gate_diag", [4, P], o2)
        gpb = at("gate_rows", [G], o2 + 2 * KB)
        junk = at("squares", [G], o2 + 4 * KB)
        ones = at("ones", [P], o2 + 6 * KB)
        ss = at("sums_of_squares", [2, 8], o2 + 6 * KB + 512)

        ident = cst[:, C_ID:C_ID + P]
        sel = cst[:, C_SEL:C_SEL + 2]
        Jl = cst[:, C_J:C_J + 384]
        Jc = cst[:, C_J + 256:C_J + 640]

        bank = [psum(f"bank{n}") for n in range(8)]
        ADAB, SELB = bank[4], bank[5]
        XB = [bank[2], bank[3], bank[6], bank[7]]

        part = nc.dram_tensor("partials", [MODEL_GROUPS, P, 2 * G], F32, kind="Internal").ap()
        part_c = nc.dram_tensor("partials_ctx", [8, P, 2 * G], F32, kind="Internal").ap()
        w_in_v = w_in[0].rearrange("(t p) n -> p t n", p=P)
        ada_v = ada_w[0].rearrange("(t p) n -> p t n", p=P)
        w_out_v = w_out[0].rearrange("(t p) n -> p t n", p=P)

        s_const, s_vec, s_zero, s_lg = sem("constants_in"), sem("vectors_in"), sem("vectors_zeroed"), sem("decays_in")
        s_x = [sem(f"x_in{t}") for t in range(4)]
        s_raw = [sem(f"raw_in{n}") for n in range(RAW)]
        s_ada = [sem(f"ada_in{n}") for n in range(ADA)]
        s_hi, s_lo, s_used = sem("hi_ready"), sem("lo_ready"), sem("piece_used")
        s_ada_used, s_stage, s_sel, s_modt, s_mod = (sem(n) for n in (
            "ada_piece_used", "ada_rows_ready", "ada_selected", "mod_biased", "mod_ready"))
        s_full = [sem(f"bank_full{b}") for b in range(4)]
        s_free = [sem(f"bank_free{b}") for b in range(4)]
        s_vT, s_vt, s_cT, s_clear = sem("vectors_T"), sem("vectors_T_copied"), sem("silu_c"), sem("banks_cleared")
        s_bn, s_ms, s_rstd, s_diag = sem("x_stats"), sem("x_mean_square"), sem("x_rstd"), sem("x_diag")
        s_half = sem("minus_half_set")
        s_xT, s_xe = sem("xT_unit"), [sem("xT_copied_act"), sem("xT_copied_dve")]
        s_t, s_tf, s_h1, s_h2 = sem("h_affine"), sem("h_hi"), sem("h1_ready"), sem("h2_ready")
        s_pst = [sem("partial_stored0"), sem("partial_stored1")]
        s_kept = [sem("partial_buffer_free0"), sem("partial_buffer_free1")]
        s_pin = {n: sem(f"partial_in_{n}") for n in ("k", "kc", "q", "v", "vc", "g", "b", "a", "c0", "c1")}
        s_sig, s_u = sem("conv_sigmoid"), sem("conv_u")
        s_lgs, s_prep = sem("decay_scales"), sem("turn_vectors")
        s_darg, s_dexp, s_dmask, s_dm = sem("decay_args"), sem("decay_exp"), sem("decay_masked"), sem("decay_ready")
        s_rope, s_kr, s_qr = sem("rotary_parts"), sem("k_rotated"), sem("q_rotated")
        s_tr, s_te = sem("transposed"), sem("transposed_copied")
        s_sc, s_pm = sem("scores"), sem("weights_ready")
        s_av, s_gst, s_gag, s_gnin, s_gnr, s_yn = (sem(n) for n in (
            "attended", "gn_stats", "gn_mean_var", "gn_var_eps", "gn_rstd", "yn_ready"))
        s_yt, s_ye, s_gs, s_yg = sem("yn_T"), sem("yn_T_copied"), sem("g_silu"), sem("ret_done")
        s_cu, s_tap, s_sq, s_sqd = sem("conv_padded"), sem("conv_tap"), sem("conv_squared"), sem("conv_summed")
        s_lnp, s_ln, s_lnvar, s_lnr = sem("ln_sums"), sem("ln_step"), sem("ln_var"), sem("ln_rstd")
        s_zc, s_z, s_zs, s_cg, s_cy = (sem(n) for n in (
            "ln_centred", "ln_applied", "ln_silu", "conv_gate_silu", "conv_done"))
        s_yh, s_yl = sem("y_hi"), sem("y_lo")
        s_dg, s_gb, s_gbe, s_yq = sem("gate_diag"), sem("gate_bcast"), sem("gate_rows"), sem("y_squared")
        s_fin, s_var, s_frs, s_res, s_o, s_out = (sem(n) for n in (
            "final_step", "final_var", "final_rstd", "x_again_in", "out_ready", "out_stored"))
        s_one = sem("ones_ready")

        B01, B23, B03 = (0, 1), (2, 3), (0, 1, 2, 3)
        FIRST = [(4, [("ctx", B03), ("ctx", B03)]), (4, [("tok", B01)]), (8, [("ch", B01), ("ch", B23)])]
        SECOND = [(4, [("ch", B01), ("ch", B23)]),
                  (4, [("ctx", B03), ("tok", B01), ("ctx", B03), ("ch", B23)]),
                  (2, [("ch", B01), ("ch", B23)])]
        LO0 = RAW

        def uses(groups, b):
            return sum(b in banks for _, banks in groups)

        block = ctx.enter_context(nc.Block())

        @block.sync
        def _(sp):
            sp.dma_start(cst[:, :], consts).then_inc(s_const, 16)
            sp.wait_ge(s_zero, 1)

            def rows(ap, n):
                return ap.rearrange("(r p) -> r p", r=n)
            vecs = [(0, 0, rows(c[0], 32), 32), (0, 32, rows(c_ctx[0], 32), 32), (0, 64, rows(pre_norm_g[0], 32), 32),
                    (0, 96, rows(conv_dw_b[0], 16), 16), (0, 112, rows(ret_gn_g[0], 16), 16),
                    (1, 0, rows(ada_b[0], 96), 96), (1, 96, rows(conv_ln_g[0], 16), 16),
                    (1, 112, rows(conv_ln_b[0], 16), 16), (6, 48, rows(post_norm_g[0], 32), 32)]
            taps = conv_dw_w[0].rearrange("k (c p) -> (k c) p", p=P)
            vecs += [(t, 0, taps[16 * k:16 * (k + n), :], 16 * n) for t, k, n in TAP_TILES]
            for t, r, src, n in vecs:
                sp.dma_start(vin[r:r + n, t, :], src).then_inc(s_vec, 16)
            for h, lg in enumerate((lg_f, lg_b)):
                sp.dma_start(lgrow[:, h, :], lg[0].partition_broadcast(P)).then_inc(s_lg, 16)

            raw_n = Count(None)
            ada_n = Count(None)

            def load_ada(col, piece):
                n = ada_n.now()
                if not isinstance(n, int) or n >= ADA:
                    sp.wait_ge(s_ada_used, ada_n.now(ADA - 1))
                s = piece % ADA
                sp.dma_start(ada[:, s, :, :], ada_v[:, PK * piece:PK * piece + PK, bass.ds(col, G)]).then_inc(s_ada[s], 16)
                ada_n.up()

            def load_w(view, row_tile, col, piece):
                sp.wait_ge(s_lo, raw_n.now() + 1)
                s = piece % RAW
                sp.dma_start(raw[:, s, :, :], view[:, row_tile + PK * piece:row_tile + PK * piece + PK, bass.ds(col, G)]).then_inc(s_raw[s], 16)
                raw_n.up()

            for col in (0, D):
                for j in range(NPO):
                    load_ada(col, j)
            with sp.Fori(1, 4) as i:
                ada_n.enter(i, 2 * NPO, first=1)
                for col in (0, D):
                    for j in range(NPO):
                        load_ada(i * G + col, j)
            ada_n.leave(4)

            def group(row_tile, col, ada_col=None):
                m = 0
                for j in range(NP):
                    load_w(w_in_v, row_tile, col, j)
                    if ada_col is not None:
                        for _ in range(ADA_BESIDE[j]):
                            load_ada(ada_col, m)
                            m += 1

            def loop(turns, groups):
                n, beside = len(groups(0)), sum(g[2] is not None for g in groups(0))
                with sp.Fori(0, turns) as i:
                    raw_n.enter(i, n * NP)
                    ada_n.enter(i, beside * NPO)
                    for row_tile, col, ada_col in groups(i):
                        group(row_tile, col, ada_col)
                raw_n.leave(turns)
                ada_n.leave(turns)

            loop(4, lambda i: [(0, i * G + COLS_K, i * G + D // 2), (0, i * G + COLS_V, i * G + D + D // 2)])
            loop(4, lambda i: [(0, i * G, None)])
            loop(8, lambda i: [(0, i * (2 * G) + COLS_G, None), (0, i * (2 * G) + COLS_G + G, None)])
            loop(4, lambda i: [(KH, i * G + COLS_B, None), (KH, i * G + COLS_A, None)])
            loop(4, lambda i: [(KH, i * G + COLS_K, i * (2 * G) + 2 * D), (KH, i * G, None),
                               (KH, i * G + COLS_V, i * (2 * G) + 2 * D + G), (KH, i * G + COLS_G, None)])
            loop(2, lambda i: [(KH, i * (2 * G) + COLS_C, None), (KH, i * (2 * G) + COLS_C + G, None)])
            with sp.Fori(0, 8) as i:
                raw_n.enter(i, NPO)
                for j in range(NPO):
                    load_w(w_out_v, 0, i * G, j)
            raw_n.leave(8)
            sp.wait_ge(s_yl, NPO)
            for t in range(2):
                sp.dma_start(xres[:, t, :], x[0, t * P:(t + 1) * P, :]).then_inc(s_res, 16)
            for n in range(8):
                sp.wait_ge(s_o, n + 1)
                t, q = n // 4, n % 4
                sp.dma_start(out[0, t * P:(t + 1) * P, q * 1024:(q + 1) * 1024], yo[:, t, q * 1024:(q + 1) * 1024]).then_inc(s_out, 16)
            sp.wait_ge(s_out, 8 * 16)

        @block.tensor
        def _(pe):
            piece = Count(s_used)
            ada_p = Count(s_ada_used)
            chunk = Count(None)
            bank_n = [Count(s_free[b], 1) for b in range(4)]

            def ada_piece(j, x_units=None):
                s = j % ADA
                pe.wait_ge(s_ada[s], ada_p.landed(s, ADA))
                for r in range(PK):
                    kt = PK * j + r
                    q = kt % 4
                    last = nc.tensor.matmul(ADAB[32 * q:32 * q + 2, :], cT[:, kt, :], ada[:, s, r, :],
                                            start=(kt < 4), stop=(kt >= KT - 4), tile_position=(0, 32 * q))
                last.then_inc(s_ada_used, 1)
                ada_p.up()

            def ada_select():
                pe.wait_ge(s_stage, chunk.now() + 1)
                if not isinstance(chunk.now(), int) or chunk.now() > 0:
                    pe.wait_ge(s_mod, chunk.now())
                for r in range(4):
                    last = nc.tensor.matmul(SELB[:, 2 * r:2 * r + 2], stage[:, r * P:(r + 1) * P], sel, start=True, stop=True)
                last.then_inc(s_sel, 1)
                chunk.up()

            for b in range(4):
                pe.sem_inc(s_free[b], 1)
            pe.wait_ge(s_const, 16)
            pe.wait_ge(s_vec, 14 * 16)
            for t in range(7):
                last = nc.tensor.transpose(bank[t // 4][:, (t % 4) * P:(t % 4 + 1) * P], vin[:, t, :], ident)
            last.then_inc(s_vT, 1)
            pe.wait_ge(s_cT, 1)
            pe.wait_ge(s_clear, 1)
            for j in range(NPO):
                ada_piece(j)
            ada_select()

            def x_unit(kt):
                if kt >= 4:
                    pe.wait_ge(s_xe[kt % 2], (kt - 4) // 2 + 1)
                for t in range(4):
                    if kt == 0:
                        pe.wait_ge(s_diag, t + 1)
                    last = nc.tensor.matmul(XB[kt % 4][:, t * P:(t + 1) * P], xs[:, t, kt * P:(kt + 1) * P], diag[:, t, :],
                                            start=True, stop=True)
                last.then_inc(s_xT, 1)
            for j in range(NPO):
                ada_piece(j)
                x_unit(2 * j)
                x_unit(2 * j + 1)
            ada_select()
            with pe.Fori(1, 4) as i:
                for cnt, per in ((ada_p, 2 * NPO), (chunk, 2)):
                    cnt.enter(i, per, first=1)
                for _ in range(2):
                    for j in range(NPO):
                        ada_piece(j)
                    ada_select()
            for cnt in (ada_p, chunk):
                cnt.leave(4)

            def wait_piece(j):
                pe.wait_ge(s_lo, piece.now() + 1 + LO0)

            def wait_banks(banks, j, b):
                if j == 0:
                    pe.wait_ge(s_free[b], bank_n[b].now())

            def tok_group(h, banks, beside=None, h_wait=None, with_ada=False, pieces=NP):
                m = 0
                for j in range(pieces):
                    if beside and j in beside:
                        beside[j]()
                    if h_wait is not None:
                        pe.wait_ge(h_wait[0], h_wait[1] * (j + 1))
                    wait_piece(j)
                    s = j % 2
                    for r in range(PK):
                        kt = PK * j + r
                        for t, b in enumerate(banks):
                            if r == 0:
                                wait_banks(banks, j, b)
                            hh, hl = (h[n][:, kt, t * P:(t + 1) * P] for n in range(2))
                            nc.tensor.matmul(bank[b][:, :], hh, whi[:, s, r, :], start=(kt == 0), stop=False)
                            nc.tensor.matmul(bank[b][:, :], hh, wlo[:, s, r, :], start=False, stop=False)
                            last = nc.tensor.matmul(bank[b][:, :], hl, whi[:, s, r, :], start=False, stop=(kt == PK * pieces - 1))
                            if kt == PK * pieces - 1 and t < len(banks) - 1:
                                last.then_inc(s_full[b], 1)
                    last.then_inc(s_used, 1)
                    piece.up()
                    if with_ada:
                        for _ in range(ADA_BESIDE[j]):
                            ada_piece(m)
                            m += 1
                    if with_ada and j == NP - 2:
                        ada_select()
                for b in banks:
                    bank_n[b].up()

            def ch_group(h, banks, beside=None):
                for j in range(NP):
                    if beside and j in beside:
                        beside[j]()
                    wait_piece(j)
                    s = j % 2
                    for r in range(PK):
                        kt = PK * j + r
                        for n in range(4):
                            b, co = banks[n // 2], (n % 2) * N
                            if r == 0 and n % 2 == 0:
                                wait_banks(banks, j, b)
                            to = bank[b][:, co:co + N]
                            wh, wl = (w[:, s, r, n * P:(n + 1) * P] for w in (whi, wlo))
                            end = kt == KH - 1
                            nc.tensor.matmul(to, wh, h[0][:, kt, 0:N], start=(kt == 0 and n % 2 == 0), stop=False, skip_group_check=True)
                            nc.tensor.matmul(to, wh, h[1][:, kt, 0:N], start=False, stop=False, skip_group_check=True)
                            last = nc.tensor.matmul(to, wl, h[0][:, kt, 0:N], start=False, stop=end, skip_group_check=True)
                            if end and n == 1:
                                last.then_inc(s_full[b], 1)
                    last.then_inc(s_used, 1)
                    piece.up()
                for b in banks:
                    bank_n[b].up()


            def loop(turns, kinds, body, ada_chunks=0):
                with pe.Fori(0, turns) as i:
                    piece.enter(i, NP * len(kinds))
                    ada_p.enter(i, ada_chunks * NPO)
                    chunk.enter(i, ada_chunks)
                    for b in range(4):
                        bank_n[b].enter(i, uses(kinds, b))
                    body(i)
                for cnt in (piece, ada_p, chunk, *bank_n):
                    cnt.leave(turns)

            pe.wait_ge(s_vt, 1)
            for n in range(2):
                pe.wait_ge(s_xe[n], KT // 2)
            (t1, k1), (t2, k2), (t3, k3) = FIRST
            loop(t1, k1, lambda i: (tok_group(h1, B03, h_wait=(s_h1, PK), with_ada=True), tok_group(h1, B03, with_ada=True)), ada_chunks=2)
            loop(t2, k2, lambda i: tok_group(h1, B01))
            loop(t3, k3, lambda i: (ch_group(h1, B01), ch_group(h1, B23)))
            pe.wait_ge(s_h2, KH)
            (t4, k4), (t5, k5), (t6, k6) = SECOND
            loop(t4, k4, lambda i: (ch_group(h2, B01), ch_group(h2, B23)))

            def retention(i):

                def k_units(h):
                    def go():
                        if h == 0:
                            pe.wait_ge(s_kr, i + 1)
                            pe.wait_ge(s_ye, i * 4 + 1)
                        else:
                            pe.wait_ge(s_te, i * 6 + 2)
                        for dk in range(2):
                            for t in range(4):
                                last = nc.tensor.transpose(bank[6 + dk][:, t * P:(t + 1) * P],
                                                           k_sb[:, t, h * HD + dk * P:h * HD + (dk + 1) * P], ident)
                            last.then_inc(s_tr, 1)
                    return go

                def q_units():
                    pe.wait_ge(s_qr, i + 1)
                    pe.wait_ge(s_te, i * 6 + 4)
                    for h in range(2):
                        for dk in range(2):
                            for t in range(2):
                                last = nc.tensor.transpose(bank[6 + h][:, dk * N + t * P:dk * N + (t + 1) * P],
                                                           q_sb[:, t, h * HD + dk * P:h * HD + (dk + 1) * P], ident)
                        last.then_inc(s_tr, 1)

                def scores(h):
                    def go():
                        if h == 0:
                            pe.wait_ge(s_te, i * 6 + 6)
                        else:
                            pe.wait_ge(s_pm, i * 4 + 2)
                        for pair in range(2):
                            for m in range(2):
                                key = 2 * pair + m
                                for dk in range(2):
                                    last = nc.tensor.matmul(bank[6 + pair][:, m * N:(m + 1) * N], kT[:, h, dk, key * P:(key + 1) * P],
                                                            qT[:, h, dk, :], start=(dk == 0), stop=(dk == 1))
                            last.then_inc(s_sc, 1)
                    return go

                def attend(h):
                    def go():
                        if h == 0:
                            pe.wait_ge(s_pm, i * 4 + 4)
                            pe.wait_ge(s_free[3], bank_n[3].now())
                        for t in range(2):
                            for key in range(4):
                                last = nc.tensor.matmul(bank[6 + h][:, t * HD:(t + 1) * HD], Pm[:, h, key, t * P:(t + 1) * P],
                                                        v_sb[:, key, h * HD:(h + 1) * HD], start=(key == 0), stop=(key == 3))
                        last.then_inc(s_av, 1)
                    return go

                def y_units():
                    for h in range(2):
                        pe.wait_ge(s_yn, i * 2 + h + 1)
                        for e in range(2):
                            for t in range(2):
                                last = nc.tensor.transpose(bank[6 + h][:, e * N + t * P:e * N + (t + 1) * P],
                                                           q_sb[:, t, h * HD + e * P:h * HD + (e + 1) * P], ident)
                        last.then_inc(s_yt, 1)

                tok_group(h2, B03, with_ada=True)
                tok_group(h2, B01)
                tok_group(h2, B03, beside={1: k_units(0), 2: k_units(1), 3: q_units, 4: scores(0), 5: scores(1)}, with_ada=True)
                ch_group(h2, B23, beside={1: attend(0), 2: attend(1), 5: y_units})

            loop(t5, k5, retention, ada_chunks=2)

            def ln_sums():
                pe.wait_ge(s_sqd, 8)
                pe.wait_ge(s_one, 1)
                pe.wait_ge(s_ye, 16 + 1)
                for n in range(2):
                    last = nc.tensor.matmul(bank[6][:, n * N:(n + 1) * N], ones_c[:, :], ssum[:, n, :], start=True, stop=True)
                last.then_inc(s_lnp, 1)
            ln_sums()
            loop(t6, k6, lambda i: (ch_group(h2, B01), ch_group(h2, B23)))

            def gate_rows(i, n):
                pe.wait_ge(s_dg, i * 2 + n + 1)
                nc.tensor.matmul(bank[7][:, :], ones[:, :], diag4[:, :, :].rearrange("p a b -> p (a b)"), start=True, stop=True).then_inc(s_gb, 1)

            def out_turn(i):
                for n, banks in enumerate((B01, B23)):
                    tok_group(yr, banks, beside={NPO - 2: lambda n=n: gate_rows(i, n)}, h_wait=(s_yl, 1), pieces=NPO)
            with pe.Fori(0, 4) as i:
                piece.enter(i, 2 * NPO)
                for b in range(4):
                    bank_n[b].enter(i, 1)
                out_turn(i)

        def full_waits(eng):
            n = {b: Count(s_full[b]) for b in range(4)}
            done = Count(s_used)

            def enter(i, groups, pieces=NP):
                for b in range(4):
                    n[b].enter(i, sum(b in banks[:-1] for _, banks in groups))
                done.enter(i, len(groups) * pieces)

            def leave(turns):
                for cnt in (done, *n.values()):
                    cnt.leave(turns)

            def wait(banks, b):
                if b == banks[-1]:
                    eng.wait_ge(s_used, done.now())
                else:
                    eng.wait_ge(s_full[b], n[b].now())

            def group(banks, pieces=NP):
                for b in banks[:-1]:
                    n[b].up()
                done.up(pieces)
            return enter, leave, wait, group

        @block.scalar
        def _(act):
            n_split = Count(None)

            def split(j):
                n = n_split.now()
                act.wait_ge(s_raw[j % RAW], n_split.landed(j % RAW, RAW))
                if not isinstance(n, int) or n >= 2:
                    act.wait_ge(s_used, n_split.now(1))
                nc.scalar.activation(whi[:, j % 2, :, :], raw[:, j % RAW, :, :], ACT.Copy).then_inc(s_hi, 1)
                n_split.up()

            enter, leave, wait_full, group_done = full_waits(act)
            free_n = [Count(s_free[b], 1) for b in range(4)]
            stored = [Count(s_kept[n], 1) for n in range(2)]
            chunk = Count(None)

            def group(banks, extras=None, evict=None, pieces=NP, last=False):
                for j in range(2, pieces if last else pieces + 2):
                    split(j)
                    if extras and j in extras:
                        extras[j]()
                group_done(banks, pieces)
                for b in banks:
                    free_n[b].up()
                if evict:
                    evict()

            def rows():
                act.wait_ge(s_ada_used, chunk.i * (chunk.per * NPO) + (chunk.base + chunk.k + 1) * NPO)
                nc.scalar.activation(stage[:, :], ADAB[:, :], ACT.Copy).then_inc(s_stage, 1)
                chunk.up()

            def affine(hf, kt, gkt, ready):
                s = kt % 2
                act.wait_ge(ready[0], ready[1])
                for v in range(2):
                    if isinstance(gkt, int):
                        src, m = xT[hf][:, kt, v * N:(v + 1) * N], slice(gkt, gkt + 1)
                        sc_, bi_ = modA[:, gkt, v:v + 1], modB[:, gkt, v:v + 1]
                    last = nc.scalar.activation(xtmp[:, s, v * N:(v + 1) * N], src, ACT.Identity, scale=sc_, bias=bi_)
                last.then_inc(s_t, 1)

            for t in range(4):
                src = x[0, t * P:(t + 1) * P, :] if t < 2 else ctx_in[0, (t - 2) * P:(t - 1) * P, :]
                act.dma_start(xs[:, t, :], src).then_inc(s_x[t], 16)
            act.wait_ge(s_vt, 1)
            for v in range(2):
                last = nc.scalar.activation(cT[:, :, v], vt[:, 0, 32 * v:32 * v + 32], ACT.Silu)
            last.then_inc(s_cT, 1)
            rows()
            for kt in range(0, KT, 2):
                act.wait_ge(s_xT, kt + 1)
                nc.scalar.activation(xT[kt // KH][:, kt % KH, :], XB[kt % 4][:, :], ACT.Copy).then_inc(s_xe[0], 1)
            rows()
            act.wait_ge(s_xe[0], KT // 2)
            act.wait_ge(s_xe[1], KT // 2)
            for i in range(4):
                if i:
                    rows()
                    rows()
                if i == 3:
                    split(0)
                    split(1)
                act.wait_ge(s_mod, 2 * i + 2)
                for kt in range(4 * i, 4 * i + 4):
                    affine(0, kt, kt, (s_h1, kt - 1) if kt >= 2 else (s_mod, 2 * i + 2))

            def keep(h, banks):
                act.wait_ge(s_kept[h], stored[h].now())
                wait_full(banks, 2 * h)
                nc.scalar.activation(pst[:, h, 0:G], bank[2 * h][:, :], ACT.Copy).then_inc(s_free[2 * h], 1)
                stored[h].up()

            def loop(turns, kinds, body, chunks=0, halves=(0, 0)):
                with act.Fori(0, turns) as i:
                    n_split.enter(i, NP * len(kinds))
                    chunk.enter(i, chunks)
                    enter(i, kinds)
                    for b in range(4):
                        free_n[b].enter(i, uses(kinds, b))
                    for h in range(2):
                        stored[h].enter(i, halves[h])
                    body(i)
                leave(turns)
                for cnt in (n_split, chunk, *free_n, *stored):
                    cnt.leave(turns)

            loop(4, FIRST[0][1], lambda i: [group(B03, {7: rows}, lambda: (keep(0, B03), keep(1, B03))) for _ in range(2)],
                 chunks=2, halves=(2, 2))

            def q_body(i):
                def affines(r):
                    def go():
                        kt = i * 4 + r
                        act.wait_ge(s_h1, KH) if r < 0 else None
                        if r == 0:
                            act.wait_ge(s_mod, 16)
                        act.wait_ge(s_h2, kt - 1 + 2)
                        for v in range(2):
                            last = nc.scalar.activation(xtmp[:, r % 2, v * N:(v + 1) * N], xT[1][:, bass.ds(kt, 1), v * N:(v + 1) * N],
                                                        ACT.Identity, scale=modA[:, bass.ds(kt + KH, 1), v], bias=modB[:, bass.ds(kt + KH, 1), v])
                        last.then_inc(s_t, 1)
                    return go
                group(B01, {2 + r: affines(r) for r in range(4)}, lambda: keep(0, B01))
            loop(4, FIRST[1][1], q_body, halves=(1, 0))
            loop(8, FIRST[2][1], lambda i: (group(B01, None, lambda: keep(0, B01)), group(B23, None, lambda: keep(1, B23))), halves=(1, 1))

            def d_body(i):
                def sigmoid():
                    act.wait_ge(s_free[1], free_n[1].now())
                    nc.scalar.activation(bb[:, :, :], bb[:, :, :], ACT.Sigmoid).then_inc(s_sig, 1)
                group(B01, None, sigmoid)
                group(B23)
            loop(4, SECOND[0][1], d_body)

            def e_body(i):
                def exps(h):
                    def go():
                        act.wait_ge(s_darg, i * 2 + h + 1)
                        f, b, cb = (lg4[:, h, n:n + 1] for n in range(3))
                        nc.scalar.activation(Dm[:, h, 0:384], Dm[:, h, 0:384], ACT.Exp, scale=f)
                        nc.scalar.activation(Dm[:, h, 384:768], Jc, ACT.Exp, scale=f)
                        nc.scalar.activation(tmp[:, 0:384], tmp[:, 0:384], ACT.Exp, scale=b)
                        nc.scalar.activation(tmp[:, 384:768], Jc, ACT.Exp, scale=b, bias=cb).then_inc(s_dexp, 1)
                    return go

                def square(pair):
                    def go():
                        act.wait_ge(s_tap, i * 128 + 64 * (pair + 1))
                        nc.scalar.activation(acc[:, :, :], Y[:, bass.ds(i * 4 + (16 + 2 * pair), 2), :], ACT.Square).then_inc(s_sq, 1)
                    return go

                def copy_T(n):
                    def go():
                        for u in (n, n + 1):
                            act.wait_ge(s_tr, i * 6 + u + 1)
                            if u < 4:
                                nc.scalar.activation(kT[:, u // 2, u % 2, :], bank[6 + u % 2][:, :], ACT.Copy, scale=float(HD) ** -0.5).then_inc(s_te, 1)
                            else:
                                nc.scalar.activation(qT[:, u - 4, :, :], bank[6 + u % 2][:, :], ACT.Copy).then_inc(s_te, 1)
                    return go

                def copy_y():
                    for h in range(2):
                        act.wait_ge(s_yt, i * 2 + h + 1)
                        for e in range(2):
                            nc.scalar.activation(Y[:, bass.ds(i * 4 + (2 * h + e), 1), :], bank[6 + h][:, e * N:(e + 1) * N],
                                                 ACT.Copy, scale=gn4[:, 2 * h + e:2 * h + e + 1]).then_inc(s_ye, 1)

                def silu_g():
                    act.wait_ge(s_free[3], free_n[3].now())
                    nc.scalar.activation(g_sb[:, :, :], g_sb[:, :, :], ACT.Silu).then_inc(s_gs, 1)
                group(B03, {3: exps(0), 4: exps(1), 7: rows})
                group(B01, {2: square(0)})
                group(B03, {2: copy_T(0), 3: copy_T(2), 4: copy_T(4), 7: rows, 8: square(1)})
                group(B23, {6: copy_y}, silu_g)
            act.sem_inc(s_ye, 1)
            loop(4, SECOND[1][1], e_body, chunks=2)

            def split_y(m):
                if m == 0:
                    act.wait_ge(s_used, 56 * NP)
                nc.scalar.activation(yr[0][:, PK * m:PK * m + PK, :], Y[:, PK * m:PK * m + PK, :], ACT.Copy).then_inc(s_yh, 1)

            def z_silu(g):
                def go():
                    act.wait_ge(s_z, g + 1)
                    for n in range(4):
                        ct = 4 * g + n
                        last = nc.scalar.activation(Y[:, 16 + ct, :], Y[:, 16 + ct, :], ACT.Silu, scale=vt[:, 1, 96 + ct:97 + ct], bias=vt[:, 1, 112 + ct:113 + ct])
                    last.then_inc(s_zs, 1)
                return go

            def gate_silu(g):
                def go():
                    if g == 3:
                        for m in range(4):
                            split_y(m)
                    b = 1 + 2 * (g % 2)
                    act.wait_ge(s_free[b], free_n[b].now())
                    buf = (bb, ab)[g % 2]
                    nc.scalar.activation(buf[:, :, :], buf[:, :, :], ACT.Silu).then_inc(s_cg, 1)
                return go
            for i in range(2):
                n_split.enter(i, 2 * NP)
                enter(i, SECOND[2][1])
                for b in range(4):
                    free_n[b].enter(i, 1)
                for n, banks in enumerate((B01, B23)):
                    group(banks, {7: z_silu(2 * i + n)}, gate_silu(2 * i + n))
            leave(2)
            for cnt in (n_split, *free_n):
                cnt.leave(2)

            def out_turn(i, first=False, end=False):
                n_split.enter(i, 2 * NPO)
                enter(i, SECOND[2][1], NPO)
                for b in range(4):
                    free_n[b].enter(i, 1)
                for n, banks in enumerate((B01, B23)):
                    def copy_gate():
                        act.wait_ge(s_gb, i * 2 + n + 1)
                        nc.scalar.activation(gpb[:, :], bank[7][:, :], ACT.Copy).then_inc(s_gbe, 1)

                    def squares():
                        for t, b in enumerate(banks):
                            wait_full(banks, b)
                            if not (first and n == 0 and t == 0):
                                act.wait_ge(s_yq, i * 4 + 2 * n + t)
                            nc.scalar.activation(junk[:, :], bank[b][:, :], ACT.Square,
                                                 accum_out=ss[:, t, bass.ds(i * 2 + n, 1)]).then_inc(s_yq, 1)
                    extras = {}
                    if first and n == 0:
                        extras = {j: (lambda m=j + 2: split_y(m)) for j in range(2, NPO - 2)}
                    extras[NPO - 1] = copy_gate
                    group(banks, extras, squares, NPO, last=end and n == 1)
            out_turn(0, first=True)
            with act.Fori(1, 3) as i:
                out_turn(i)
            out_turn(3, end=True)

        @block.vector
        def _(dve):
            n_split = Count(None)

            def split(j):
                dve.wait_ge(s_raw[j % RAW], n_split.landed(j % RAW, RAW))
                dve.wait_ge(s_hi, n_split.now() + 1)
                n = n_split.now()
                if not isinstance(n, int) or n >= 2:
                    dve.wait_ge(s_used, n_split.now(1))
                nc.vector.tensor_tensor(wlo[:, j % 2, :, :], raw[:, j % RAW, :, :], whi[:, j % 2, :, :].bitcast(F32), ALU.subtract).then_inc(s_lo, 1)
                n_split.up()

            enter, leave, wait_full, group_done = full_waits(dve)
            free_n = [Count(s_free[b], 1) for b in range(4)]
            stored = [Count(s_kept[n], 1) for n in range(2)]
            chunk, biased = Count(None), Count(s_modt)

            def group(banks, extras=None, evict=None, pieces=NP, last=False):
                for j in range(2, pieces if last else pieces + 2):
                    split(j)
                    if extras and j in extras:
                        extras[j]()
                group_done(banks, pieces)
                for b in banks:
                    free_n[b].up()
                if evict:
                    evict()

            def modulation(kind, kt):
                dve.wait_ge(s_sel, chunk.now() + 1)
                got = SELB[:, 0:8].rearrange("p (a v) -> p a v", v=2)
                def cols(t, at_):
                    v = vt[:, t, at_ + kt:at_ + kt + 4] if isinstance(kt, int) else vt[:, t, bass.ds(kt + at_, 4)]
                    return v
                def both(v):
                    return v.unsqueeze(2).broadcast_to([P, 4, 2])
                def kts(m):
                    return m[:, kt:kt + 4, :] if isinstance(kt, int) else m[:, bass.ds(kt, 4), :]
                if kind == "shift":
                    nc.vector.tensor_tensor(kts(modB), got, both(cols(1, 0)), ALU.add).then_inc(s_mod, 1)
                else:
                    nc.vector.tensor_tensor(mtmp[:, :, :], got, both(cols(1, 32 if kind == "scale" else 64)), ALU.add).then_inc(s_modt, 1)
                    dve.wait_ge(s_modt, biased.up())
                    if kind == "scale":
                        nc.vector.scalar_tensor_tensor(out=kts(modA), in0=mtmp[:, :, :], scalar=1.0, in1=both(cols(0, 64)),
                                                       op0=ALU.add, op1=ALU.mult).then_inc(s_mod, 1)
                    else:
                        to = gp[:, bass.ds(kt, 4)]
                        nc.vector.tensor_tensor(to, mtmp[:, :, 0], cols(6, 48), ALU.mult).then_inc(s_mod, 1)
                chunk.up()

            def split_h(kt, s, n, ready, done):
                dve.wait_ge(s_t, n + 1)
                nc.vector.tensor_copy(done[0][0][:, kt, :] if isinstance(kt, int) else done[0][0][:, bass.ds(kt, 1), :], xtmp[:, s, :]).then_inc(s_tf, 1)
                dve.wait_ge(s_tf, n + 1)
                hi, lo = (h[:, kt, :] if isinstance(kt, int) else h[:, bass.ds(kt, 1), :] for h in done[0])
                nc.vector.tensor_tensor(lo, xtmp[:, s, :] if isinstance(kt, int) else xtmp[:, s:s + 1, :], hi.bitcast(F32), ALU.subtract).then_inc(done[1], 1)

            nc.vector.memset(vin[:, :, :], 0.0).then_inc(s_zero, 1)
            nc.vector.memset(ADAB[:, :], 0.0).then_inc(s_clear, 1)
            dve.sem_inc(s_lo, LO0)
            dve.sem_inc(s_h2, 1)
            dve.wait_ge(s_const, 16)
            dve.wait_ge(s_lg, 32)
            nc.vector.tensor_copy(lgs[:, :, 0], lgrow[:, 0, :])
            nc.vector.tensor_scalar(lgs[:, :, 1], lgrow[:, 1, :], -1.0, None, ALU.mult)
            nc.vector.tensor_scalar(lgs[:, :, 2], lgrow[:, 1, :], 2.0 * N, None, ALU.mult).then_inc(s_lgs, 1)
            dve.wait_ge(s_vT, 1)
            nc.vector.tensor_copy(vt[:, 0:4, :], bank[0][:, :])
            nc.vector.tensor_copy(vt[:, 4:7, :], bank[1][:, 0:3 * P]).then_inc(s_vt, 1)
            dve.wait_ge(s_vt, 1)
            for t in range(4):
                dve.wait_ge(s_x[t], 16)
                for n in range(8):
                    last = nc.vector.bn_stats(bst[:, t, n, :], xs[:, t, n * G:(n + 1) * G])
                last.then_inc(s_bn, 1)
                dve.wait_ge(s_bn, 3 * t + 1)
                nc.vector.bn_aggr(mv[:, t, :], bst[:, t, :, :]).then_inc(s_bn, 1)
                dve.wait_ge(s_bn, 3 * t + 2)
                nc.vector.scalar_tensor_tensor(out=rs[:, t:t + 1], in0=mv[:, t, 0:1], scalar=mv[:, t, 0:1], in1=mv[:, t, 1:2],
                                               op0=ALU.mult, op1=ALU.add).then_inc(s_bn, 1)
                dve.wait_ge(s_bn, 3 * t + 3)
                nc.vector.tensor_scalar(rs[:, t:t + 1], rs[:, t:t + 1], EPS, None, ALU.add).then_inc(s_ms, 1)
            for t in range(4):
                dve.wait_ge(s_rstd, t + 1)
                nc.vector.tensor_scalar(diag[:, t, :], ident, rs[:, t:t + 1], None, ALU.mult).then_inc(s_diag, 1)
            modulation("shift", 0)
            for kt in range(1, KT, 2):
                dve.wait_ge(s_xT, kt + 1)
                nc.vector.tensor_copy(xT[kt // KH][:, kt % KH, :], XB[kt % 4][:, :]).then_inc(s_xe[1], 1)
            modulation("scale", 0)
            for i in range(4):
                if i:
                    modulation("shift", 4 * i)
                    modulation("scale", 4 * i)
                if i == 3:
                    split(0)
                    split(1)
                for kt in range(4 * i, 4 * i + 4):
                    split_h(kt, kt % 2, kt, None, (h1, s_h1))

            def keep(h, banks):
                dve.wait_ge(s_kept[h], stored[h].now())
                wait_full(banks, 2 * h + 1)
                nc.vector.tensor_copy(pst[:, h, G:2 * G], bank[2 * h + 1][:, :]).then_inc(s_free[2 * h + 1], 1)
                stored[h].up()

            def loop(turns, kinds, body, chunks=0, two_step=0, halves=(0, 0)):
                with dve.Fori(0, turns) as i:
                    n_split.enter(i, NP * len(kinds))
                    chunk.enter(i, chunks)
                    biased.enter(i, two_step)
                    enter(i, kinds)
                    for b in range(4):
                        free_n[b].enter(i, uses(kinds, b))
                    for h in range(2):
                        stored[h].enter(i, halves[h])
                    body(i)
                leave(turns)
                for cnt in (n_split, chunk, biased, *free_n, *stored):
                    cnt.leave(turns)

            loop(4, FIRST[0][1], lambda i: [group(B03, {8: lambda kind=kind: modulation(kind, i * 4 + KH)},
                                                  lambda: (keep(0, B03), keep(1, B03))) for kind in ("shift", "scale")],
                 chunks=2, two_step=1, halves=(2, 2))

            def q_body(i):
                def splits(r):
                    return lambda: split_h(i * 4 + r, r % 2, i * 4 + (r + KH), None, (h2, s_h2))
                group(B01, {2 + r: splits(r) for r in range(4)}, lambda: keep(0, B01))
            loop(4, FIRST[1][1], q_body, halves=(1, 0))
            loop(8, FIRST[2][1], lambda i: (group(B01, None, lambda: keep(0, B01)), group(B23, None, lambda: keep(1, B23))), halves=(1, 1))

            def complete(buf, banks, b):
                wait_full(banks, b)
                nc.vector.tensor_tensor(buf, buf, bank[b][:, :], ALU.add).then_inc(s_free[b], 1)

            def ch_part(buf, n):
                return buf[:, 2 * n:2 * n + 2, :].rearrange("p a b -> p (a b)")

            dve.sem_inc(s_u, 1)

            def d_body(i):
                def take_b():
                    dve.wait_ge(s_pin["b"], i * 16 + 16)
                    for n in range(2):
                        complete(ch_part(bb, n), B01, n)

                def take_a():
                    dve.wait_ge(s_pin["a"], i * 16 + 16)
                    for n in range(2):
                        complete(ch_part(ab, n), B23, 2 + n)
                    dve.wait_ge(s_sig, i + 1)
                    dve.wait_ge(s_free[3], free_n[3].now())
                    nc.vector.tensor_tensor(Y[:, bass.ds(i * 4 + 16, 4), :], ab[:, :, :], bb[:, :, :], ALU.mult).then_inc(s_u, 1)
                group(B01, None, take_b)
                group(B23, None, take_a)
            loop(4, SECOND[0][1], d_body)

            dve.wait_ge(s_kept[0], 21)
            dve.wait_ge(s_kept[1], 17)
            nc.vector.memset(upad[:, :, :], 0.0)
            nc.vector.memset(ones_c[:, :], 1.0 / RET).then_inc(s_one, 1)
            nc.vector.memset(ssum[:, :, :], 0.0)
            dve.sem_inc(s_yg, 1)
            dve.wait_ge(s_u, 5)

            def e_body(i):
                tap = Count(s_tap)
                tap.enter(i, 128)

                def prepare():
                    dve.wait_ge(s_ye, i * 4 + 1)
                    for t, k, n in TAP_TILES:
                        src = vt[:, t, 0:16 * n].rearrange("p (k c) -> p k c", c=16)[:, :, bass.ds(i * 4, 4)]
                        nc.vector.tensor_copy(w4[:, k:k + n, :], src)
                    nc.vector.tensor_copy(b4[:, :], vt[:, 0, bass.ds(i * 4 + 96, 4)])
                    nc.vector.tensor_copy(gn4[:, :], vt[:, 0, bass.ds(i * 4 + 112, 4)])
                    nc.vector.tensor_copy(lg4[:, :, :], lgs[:, bass.ds(i * 2, 2), :]).then_inc(s_prep, 1)
                    dve.wait_ge(s_prep, i + 1)

                def args(h):
                    if h == 1:
                        dve.wait_ge(s_dm, i * 2 + 1)
                    nc.vector.tensor_scalar(Dm[:, h, 0:384], Jl, 0.0, None, ALU.max)
                    nc.vector.tensor_scalar(tmp[:, 0:384], Jl, 0.0, None, ALU.min).then_inc(s_darg, 1)

                def combine(h):
                    dve.wait_ge(s_dexp, i * 2 + h + 1)
                    nc.vector.scalar_tensor_tensor(out=Dm[:, h, 0:384], in0=Jl, scalar=0.0, in1=Dm[:, h, 0:384], op0=ALU.is_ge, op1=ALU.mult)
                    nc.vector.scalar_tensor_tensor(out=tmp[:, 0:384], in0=Jl, scalar=0.0, in1=tmp[:, 0:384],
                                                   op0=ALU.is_le, op1=ALU.mult).then_inc(s_dmask, 1)
                    dve.wait_ge(s_dmask, i * 2 + h + 1)
                    nc.vector.tensor_tensor(Dm[:, h, :], Dm[:, h, :], tmp[:, 0:768], ALU.add).then_inc(s_dm, 1)

                def pad(pair):
                    for n in range(2):
                        last = nc.vector.tensor_copy(upad[:, n, TAPS // 2:TAPS // 2 + N], Y[:, bass.ds(i * 4 + (16 + 2 * pair + n), 1), :])
                    last.then_inc(s_cu, 1)
                    dve.wait_ge(s_cu, i * 2 + pair + 1)

                def taps(pair, first, last_):
                    if first == 0:
                        pad(pair)
                    for k in range(first, last_):
                        for n in range(2):
                            w = w4[:, k, 2 * pair + n:2 * pair + n + 1]
                            src = upad[:, n, k:k + N]
                            if k == 0:
                                nc.vector.tensor_scalar(acc[:, n, :], src, w, b4[:, 2 * pair + n:2 * pair + n + 1], ALU.mult, ALU.add).then_inc(s_tap, 1)
                            else:
                                dve.wait_ge(s_tap, tap.now(1))
                                to = acc[:, n, :] if k < TAPS - 1 else Y[:, bass.ds(i * 4 + (16 + 2 * pair + n), 1), :]
                                in1 = acc[:, n, :]
                                nc.vector.scalar_tensor_tensor(out=to, in0=src, scalar=w, in1=in1, op0=ALU.mult, op1=ALU.add).then_inc(s_tap, 1)
                            tap.up()
                    if last_ == TAPS:
                        dve.wait_ge(s_tap, tap.now())
                        for n in range(2):
                            nc.vector.tensor_tensor(ssum[:, 0, :], ssum[:, 0, :], Y[:, bass.ds(i * 4 + (16 + 2 * pair + n), 1), :], ALU.add).then_inc(s_tap, 1)
                            tap.up()
                            dve.wait_ge(s_tap, tap.now())

                def add_squares(pair):
                    def go():
                        dve.wait_ge(s_sq, i * 2 + pair + 1)
                        for n in range(2):
                            nc.vector.tensor_tensor(ssum[:, 1, :], ssum[:, 1, :], acc[:, n, :], ALU.add).then_inc(s_sqd, 1)
                            dve.wait_ge(s_sqd, i * 4 + 2 * pair + n + 1)
                    return go

                def rotate(buf, done):
                    sin = cst[:, C_SIN:C_SIN + 512].rearrange("p (t a s f) -> p t a s f", t=2, a=2, s=2)
                    rt = tmp[:, :].rearrange("p (t h a s f) -> p t h a s f", t=2, h=2, a=2, s=2)
                    for t in range(2):
                        for h in range(2):
                            src = buf[:, t, h * HD:(h + 1) * HD].rearrange("p (a s f) -> p a s f", a=2, s=2)[:, :, ::-1, :]
                            last = nc.vector.tensor_tensor(rt[:, t, h], src, sin[:, t], ALU.mult)
                    last.then_inc(s_rope, 1)
                    step = 4 * i + (0 if done is s_kr else 2)
                    dve.wait_ge(s_rope, step + 1)
                    v = buf[:, 0:2, :].rearrange("p t (h d) -> p t h d", h=2)
                    cos = cst[:, C_COS:C_COS + 512].rearrange("p (t d) -> p t d", t=2).unsqueeze(2).broadcast_to([P, 2, 2, HD])
                    nc.vector.tensor_tensor(v, v, cos, ALU.mult).then_inc(s_rope, 1)
                    dve.wait_ge(s_rope, step + 2)
                    flat = buf[:, 0:2, :].rearrange("p t d -> p (t d)")
                    nc.vector.tensor_tensor(flat, flat, tmp[:, :], ALU.add).then_inc(done, 1)

                def take(names, buf, banks):
                    def go():
                        for name in names:
                            dve.wait_ge(s_pin[name], i * 16 + 16)
                        for t, b in enumerate(banks):
                            complete(buf[:, t, :], banks, b)
                        dve.wait_ge(s_free[banks[-1]], free_n[banks[-1]].now())
                    return go

                def weights(h):
                    def go():
                        for pair in range(2):
                            dve.wait_ge(s_sc, i * 4 + 2 * h + pair + 1)
                            for m in range(2):
                                w = pair * 384 + (P if m == 0 else 0)
                                last = nc.vector.tensor_tensor(Pm[:, h, 2 * pair + m, :], bank[6 + pair][:, m * N:(m + 1) * N], Dm[:, h, w:w + N], ALU.mult)
                            last.then_inc(s_pm, 1)
                    return go

                def gn_stats(h):
                    def go():
                        dve.wait_ge(s_av, i * 2 + h + 1)
                        for t in range(2):
                            last = nc.vector.bn_stats(bst[:, 2 * h + t, 0, :], bank[6 + h][:, t * HD:(t + 1) * HD])
                        last.then_inc(s_gst, 1)
                        dve.wait_ge(s_bn, 12)
                        dve.wait_ge(s_gst, i * 2 + h + 1)
                        for t in range(2):
                            last = nc.vector.bn_aggr(mv[:, 2 * h + t, :], bst[:, 2 * h + t, 0, :])
                        last.then_inc(s_gag, 1)
                        dve.wait_ge(s_gag, i * 2 + h + 1)
                        nc.vector.tensor_scalar(rs[:, 2 * h:2 * h + 2], mv[:, 2 * h:2 * h + 2, 1], EPS, None, ALU.add).then_inc(s_gnin, 1)
                    return go

                def gn_apply():
                    for h in range(2):
                        dve.wait_ge(s_gnr, i * 2 + h + 1)
                        for t in range(2):
                            n = 2 * h + t
                            last = nc.vector.tensor_scalar(q_sb[:, t, h * HD:(h + 1) * HD], bank[6 + h][:, t * HD:(t + 1) * HD],
                                                           mv[:, n, 0:1], rs[:, n:n + 1], ALU.subtract, ALU.mult)
                        last.then_inc(s_yn, 1)

                def take_g():
                    dve.wait_ge(s_pin["g"], i * 16 + 16)
                    for n in range(2):
                        complete(ch_part(g_sb, n), B23, 2 + n)
                    dve.wait_ge(s_gs, i + 1)
                    dve.wait_ge(s_ye, i * 4 + 5)
                    y4 = Y[:, bass.ds(i * 4, 4), :]
                    nc.vector.tensor_tensor(y4, y4, g_sb[:, :, :], ALU.mult).then_inc(s_yg, 1)

                group(B03, {2: lambda: (prepare(), args(0)), 3: lambda: (combine(0), args(1)), 4: lambda: (combine(1), taps(0, 0, 5)),
                            5: lambda: taps(0, 5, 12), 6: lambda: taps(0, 12, 19), 7: lambda: taps(0, 19, 25),
                            8: lambda: modulation("gate", i * 8), 9: lambda: taps(0, 25, TAPS)},
                      take(("k", "kc"), k_sb, B03))
                group(B01, {2: lambda: rotate(k_sb, s_kr), 5: add_squares(0), 6: lambda: taps(1, 0, 4), 7: lambda: taps(1, 4, 6)},
                      take(("q",), q_sb, B01))
                group(B03, {2: lambda: rotate(q_sb, s_qr), 3: lambda: taps(1, 6, 12), 4: lambda: taps(1, 12, 18), 5: weights(0), 6: lambda: (weights(1)(), taps(1, 18, 25)),
                            7: lambda: taps(1, 25, TAPS), 8: lambda: modulation("gate", i * 8 + 4), 9: add_squares(1)},
                      take(("v", "vc"), v_sb, B03))
                group(B23, {2: gn_stats(0), 3: gn_stats(1), 4: gn_apply}, take_g)
            loop(4, SECOND[1][1], e_body, chunks=2, two_step=2)

            def ln_stats():
                dve.wait_ge(s_lnp, 1)
                nc.vector.tensor_copy(lnm[:, 0, :], bank[6][:, 0:N]).then_inc(s_ln, 1)
                dve.wait_ge(s_ln, 1)
                nc.vector.tensor_tensor(lnv[:, :], lnm[:, 0, :], lnm[:, 0, :], ALU.mult).then_inc(s_ln, 1)
                dve.wait_ge(s_ln, 2)
                nc.vector.scalar_tensor_tensor(out=lnv[:, :], in0=bank[6][:, N:2 * N], scalar=EPS, in1=lnv[:, :],
                                               op0=ALU.add, op1=ALU.subtract).then_inc(s_lnvar, 1)
                nc.vector.memset(ones[:, :], 1.0).then_inc(s_one, 1)

            def z(g):
                def go():
                    if g == 0:
                        dve.wait_ge(s_lnr, 1)
                    u = Y[:, 16 + 4 * g:20 + 4 * g, :]
                    m, r = (lnm[:, n, :].unsqueeze(1).broadcast_to([P, 4, N]) for n in range(2))
                    nc.vector.tensor_tensor(u, u, m, ALU.subtract).then_inc(s_zc, 1)
                    dve.wait_ge(s_zc, g + 1)
                    nc.vector.tensor_tensor(u, u, r, ALU.mult).then_inc(s_z, 1)
                return go

            def split_y(m):
                dve.wait_ge(s_yh, m + 1)
                nc.vector.tensor_tensor(yr[1][:, PK * m:PK * m + PK, :], Y[:, PK * m:PK * m + PK, :],
                                        yr[0][:, PK * m:PK * m + PK, :].bitcast(F32), ALU.subtract).then_inc(s_yl, 1)

            def conv_gate(g, banks):
                def go():
                    if g == 3:
                        for m in range(4):
                            split_y(m)
                    buf = (bb, ab)[g % 2]
                    dve.wait_ge(s_pin[f"c{g % 2}"], 16 * (g // 2 + 1))
                    for n in range(2):
                        complete(ch_part(buf, n), banks, banks[n])
                    dve.wait_ge(s_zs, g + 1)
                    dve.wait_ge(s_cg, g + 1)
                    u = Y[:, 16 + 4 * g:20 + 4 * g, :]
                    nc.vector.tensor_tensor(u, u, buf[:, :, :], ALU.mult).then_inc(s_cy, 1)
                return go
            for i in range(2):
                n_split.enter(i, 2 * NP)
                enter(i, SECOND[2][1])
                for b in range(4):
                    free_n[b].enter(i, 1)
                for n, banks in enumerate((B01, B23)):
                    g = 2 * i + n
                    extras = {5: z(g)}
                    if g == 0:
                        extras[3] = ln_stats
                    group(banks, extras, conv_gate(g, banks))
            leave(2)
            for cnt in (n_split, *free_n):
                cnt.leave(2)

            def out_turn(i, first=False, end=False):
                n_split.enter(i, 2 * NPO)
                enter(i, SECOND[2][1], NPO)
                for b in range(4):
                    free_n[b].enter(i, 1)
                for n, banks in enumerate((B01, B23)):
                    def gate_diag():
                        v = gp[:, bass.ds(i * 8 + 4 * n, 4)].unsqueeze(2).broadcast_to([P, 4, P])
                        nc.vector.tensor_tensor(diag4[:, :, :], ident.unsqueeze(1).broadcast_to([P, 4, P]), v, ALU.mult).then_inc(s_dg, 1)

                    def gated():
                        dve.wait_ge(s_gbe, i * 2 + n + 1)
                        for t, b in enumerate(banks):
                            dve.wait_ge(s_yq, i * 4 + (2 * n + t + 1))
                            wait_full(banks, b)
                            nc.vector.tensor_tensor(yo[:, t, bass.ds(i * (2 * G) + n * G, G)], bank[b][:, :], gpb[:, :], ALU.mult).then_inc(s_free[b], 1)
                    extras = {}
                    if first and n == 0:
                        extras = {j: (lambda m=j + 2: split_y(m)) for j in range(2, NPO - 2)}
                        extras[2] = lambda: (dve.wait_ge(s_cy, 4), split_y(4), gate_diag())
                    else:
                        extras[2] = gate_diag
                    group(banks, extras, gated, NPO, last=end and n == 1)
            out_turn(0, first=True)
            with dve.Fori(1, 3) as i:
                out_turn(i)
            out_turn(3, end=True)

            dve.wait_ge(s_yq, 16)
            nc.vector.tensor_reduce(rs[:, 0:2], ss[:, :, :], AX.X, ALU.add).then_inc(s_fin, 1)
            dve.wait_ge(s_fin, 1)
            nc.vector.tensor_scalar(rs[:, 0:2], rs[:, 0:2], 1.0 / D, EPS, ALU.mult, ALU.add).then_inc(s_var, 1)
            dve.wait_ge(s_frs, 1)
            dve.wait_ge(s_res, 32)
            dve.wait_ge(s_free[1], free_n[1].now())
            dve.wait_ge(s_free[3], free_n[3].now())
            for t in range(2):
                for q in range(4):
                    y = yo[:, t, q * 1024:(q + 1) * 1024]
                    nc.vector.scalar_tensor_tensor(out=y, in0=y, scalar=rs[:, t:t + 1], in1=xres[:, t, q * 1024:(q + 1) * 1024],
                                                   op0=ALU.mult, op1=ALU.add).then_inc(s_o, 1)

        @block.gpsimd
        def _(pool):
            nc.gpsimd.memset(half[:, :], -0.5).then_inc(s_half, 1)
            for h in range(2):
                pool.sem_inc(s_kept[h], 1)
            pool.wait_ge(s_half, 1)
            for t in range(4):
                pool.wait_ge(s_ms, t + 1)
                nc.gpsimd.tensor_tensor(rs[:, t:t + 1], rs[:, t:t + 1], half[:, 0:1], ALU.pow).then_inc(s_rstd, 1)

            free_n = [Count(s_free[b], 1) for b in range(4)]
            kept = [Count(s_pst[h]) for h in range(2)]

            def store(h, to):
                pool.wait_ge(s_half, 1)
                for b in (2 * h, 2 * h + 1):
                    free_n[b].up()
                    pool.wait_ge(s_free[b], free_n[b].now())
                pool.dma_start(to, pst[:, h, :]).then_inc(s_pst[h], 16)
                pool.wait_ge(s_pst[h], kept[h].up(16))
                pool.sem_inc(s_kept[h], 1)

            def loop(turns, kinds, halves, body):
                with pool.Fori(0, turns) as i:
                    for b in range(4):
                        free_n[b].enter(i, uses(kinds, b))
                    for h in range(2):
                        kept[h].enter(i, 16 * halves[h])
                    body(i)
                for cnt in (*free_n, *kept):
                    cnt.leave(turns)

            def slot(t, n):
                return t[bass.ds(n, 1), :, :].rearrange("a p n -> (a p) n")
            loop(4, FIRST[0][1], (2, 2), lambda i: (store(0, slot(part, i + 4)), store(1, slot(part_c, i)),
                                            store(0, slot(part, i + 8)), store(1, slot(part_c, i + 4))))
            loop(4, FIRST[1][1], (1, 0), lambda i: store(0, slot(part, i)))
            loop(8, FIRST[2][1], (1, 1), lambda i: (store(0, slot(part, i * 2 + 12)), store(1, slot(part, i * 2 + 13))))
            pool.wait_ge(s_pst[0], 16 * 20)
            pool.wait_ge(s_pst[1], 16 * 16)
            pool.wait_ge(s_used, 28 * NP)

            def fetch(name, buf, src):
                pool.dma_start(buf, src).then_inc(s_pin[name], 16)

            def flat(t):
                return t.rearrange("p a b -> p (a b)")
            with pool.Fori(0, 4) as i:
                pool.wait_ge(s_half, 1)
                pool.wait_ge(s_u, i + 1)
                fetch("b", flat(bb[:, :, :]), slot(part, i + 20))
                fetch("a", flat(ab[:, :, :]), slot(part, i + 16))
            pool.wait_ge(s_u, 5)
            with pool.Fori(0, 4) as i:
                pool.wait_ge(s_half, 1)
                pool.wait_ge(s_yg, i + 1)
                fetch("k", flat(k_sb[:, 0:2, :]), slot(part, i + 4))
                fetch("kc", flat(k_sb[:, 2:4, :]), slot(part_c, i))
                fetch("q", flat(q_sb[:, :, :]), slot(part, i))
                fetch("v", flat(v_sb[:, 0:2, :]), slot(part, i + 8))
                fetch("vc", flat(v_sb[:, 2:4, :]), slot(part_c, i + 4))
                pool.wait_ge(s_half, 1)
                pool.wait_ge(s_av, i * 2 + 2)
                fetch("g", flat(g_sb[:, :, :]), slot(part, i + 12))
                for h in range(2):
                    pool.wait_ge(s_gnin, i * 2 + h + 1)
                    nc.gpsimd.tensor_tensor(rs[:, 2 * h:2 * h + 2], rs[:, 2 * h:2 * h + 2], half[:, 0:2], ALU.pow).then_inc(s_gnr, 1)
            pool.wait_ge(s_yg, 5)
            fetch("c0", flat(bb[:, :, :]), slot(part, 24))
            fetch("c1", flat(ab[:, :, :]), slot(part, 25))
            pool.wait_ge(s_lnvar, 1)
            nc.gpsimd.memset(lnh[:, :], -0.5).then_inc(s_half, 1)
            pool.wait_ge(s_half, 2)
            nc.gpsimd.tensor_tensor(lnm[:, 1, :], lnv[:, :], lnh[:, :], ALU.pow).then_inc(s_lnr, 1)
            for g in range(2):
                pool.wait_ge(s_cy, g + 1)
                fetch(f"c{g}", flat((bb, ab)[g][:, :, :]), slot(part, 26 + g))
            pool.wait_ge(s_var, 1)
            nc.gpsimd.tensor_tensor(rs[:, 0:2], rs[:, 0:2], half[:, 0:2], ALU.pow).then_inc(s_frs, 1)


_INS = ["x", "c", "ctx", "c_ctx", "ada_w", "ada_b", "pre_norm_g", "post_norm_g", "w_in", "ret_log_decay_fwd",
        "ret_log_decay_bwd", "ret_gn_g", "conv_dw_w", "conv_dw_b", "conv_ln_g", "conv_ln_b", "w_out"]


def kernel(**inputs):
    import concourse.bacc as bacc
    from concourse.bass_utils import run_bass_kernel_spmd

    nc = bacc.Bacc("TRN2", target_bir_lowering=False, num_devices=1)
    arrays, args = {}, []
    for name in _INS:
        a = np.ascontiguousarray(inputs[name])
        if name == "c_ctx":
            a = a.reshape(1, D)
        arrays[f"in_{name}"] = a
        args.append(nc.dram_tensor(f"in_{name}", a.shape, mybir.dt.from_np(a.dtype), kind="ExternalInput").ap())
    consts = shape_constants()
    arrays["shape_constants"] = consts
    args.append(nc.dram_tensor("shape_constants", consts.shape, F32, kind="ExternalInput").ap())
    args.append(nc.dram_tensor("out", (1, N, D), F32, kind="ExternalOutput").ap())
    block_kernel(nc, *args)
    r = run_bass_kernel_spmd(nc, [arrays], core_ids=[0])
    return r.results[0]["out"]
```

```python
from contextlib import ExitStack

import numpy as np

import concourse.bass as bass
from concourse import mybir

ALU = mybir.AluOpType
ACT = mybir.ActivationFunctionType
F32 = mybir.dt.float32
F32R = mybir.dt.float32r
AX = mybir.AxisListType

P = 128
D = 4096
N = 256
RET = D // 2
HD = 256
TAPS = 31
EPS = 1e-6
G = 512
KT = D // P
KH = KT // 2
PK = 2
NP = KH // PK
NPO = KT // PK
RAW = 4
ADA = 4
COLS_K, COLS_V, COLS_G, COLS_A, COLS_B, COLS_C = (RET * n for n in (1, 2, 3, 4, 5, 6))
MODEL_GROUPS = 7 * RET // G
BESIDE = {"first": ([2, 1, 1, 1, 1, 1, 1, 0], [2, 1, 1, 1, 1, 1, 1, 0]),
          "second": ([2, 1, 1, 1, 1, 1, 1, 0], [0, 2, 2, 2, 1, 1, 0, 0])}
TAP_TILES = [(2, 0, 7), (3, 7, 7), (4, 14, 7), (5, 21, 7), (6, 28, 3)]
C_ID, C_SEL, C_PICK, C_J, C_COS, C_SIN, C_END = 0, 128, 130, 134, 134 + 640, 134 + 640 + 512, 134 + 640 + 1024


def ada_schedule(half):
    j, out = 0, []
    for on_pe, on_dve in zip(*BESIDE[half]):
        out.append([(e, j + n) for n, e in enumerate(["pe"] * on_pe + ["dve"] * on_dve)])
        j += on_pe + on_dve
    assert j == NPO
    return out


def shape_constants():
    f = np.float32
    c = np.zeros((P, C_END), f)
    c[:, C_ID:C_ID + P] = np.eye(P, dtype=f)
    for q in range(4):
        for v in range(2):
            c[32 * q + v, C_SEL + v] = 1.0
    c[:, C_PICK:C_PICK + 4] = [1, 0, 1, 0]
    p = np.arange(P)[:, None]
    c[:, C_J:C_J + 640] = np.arange(640)[None, :] - p - P
    freq = f(10000.0) ** (-np.arange(64, dtype=f) / f(64))
    for t in range(2):
        tok = np.arange(P) + t * P
        for half, pos in enumerate((tok // 64, tok % 64)):
            ang = pos.astype(f)[:, None] * freq[None, :]
            at = t * 256 + half * 128
            c[:, C_COS + at:C_COS + at + 128] = np.tile(np.cos(ang), (1, 2))
            c[:, C_SIN + at:C_SIN + at + 64] = -np.sin(ang)
            c[:, C_SIN + at + 64:C_SIN + at + 128] = np.sin(ang)
    return c


class Count:

    def __init__(self, sem, start=0):
        self.sem, self.base, self.i, self.per, self.k = sem, start, 0, 0, 0

    def enter(self, i, per, first=0):
        if not self.per:
            self.base += self.k - first * per
        self.i, self.per, self.k = i, per, 0

    def landed(self, slot, slots):
        return self.i * (16 * self.per // slots) + 16 * ((self.base + self.k - slot) // slots + 1)

    def leave(self, turns):
        assert self.k == self.per, (self.sem, self.k, self.per)
        self.base += self.per * turns
        self.i = self.per = self.k = 0

    def up(self, by=1):
        self.k += by
        return self.now()

    def now(self, less=0):
        fixed = self.base + self.k - less
        return self.i * self.per + fixed if self.per else fixed


def block_kernel(nc, x, c, ctx_in, c_ctx, ada_w, ada_b, pre_norm_g, post_norm_g, w_in,
                 lg_f, lg_b, ret_gn_g, conv_dw_w, conv_dw_b, conv_ln_g, conv_ln_b, w_out, consts, out):
    with ExitStack() as ctx:
        def sem(name):
            return ctx.enter_context(nc.semaphore(name))

        def psum(name):
            return ctx.enter_context(nc.psum_tensor(name, [P, G], F32))

        START = 16512
        KB = 1024
        R_A, R_B, R_C, R_D, R_E, R_F = (START + n * KB for n in (0, 64, 96, 128, 160, 176))

        def at(name, shape, offset, dt=F32):
            return nc.alloc_sbuf_tensor_at(name, [P] + shape, dt, offset=offset)

        xs = at("x_rows", [4, D], R_A)
        h1 = [at("h1_hi", [KH, 2 * N], R_A, F32R), at("h1_lo", [KH, 2 * N], R_A + 32 * KB, F32R)]
        xT = [at("xT_first", [KH, 2 * N], R_C), at("xT_second", [KH, 2 * N], R_B)]
        h2 = [at("h2_hi", [KH, 2 * N], R_B, F32R), at("h2_lo", [KH, 2 * N], R_C, F32R)]
        raw = at("raw", [RAW, PK, G], R_D)
        whi = at("w_hi", [2, PK, G], R_D + 16 * KB, F32R)
        wlo = at("w_lo", [2, PK, G], R_D + 24 * KB, F32R)
        ada = at("ada_pieces", [ADA, PK, G], R_E)
        o = R_F
        def lasting(name, shape, dt=F32):
            nonlocal o
            t = at(name, shape, o, dt)
            o += (4 * int(np.prod(shape)) + 31) // 32 * 32
            return t
        cst = lasting("constants", [C_END])
        vt = lasting("vectors_T", [7, P])
        cT = lasting("silu_c_T", [KT, 2])
        modA = lasting("mod_scale", [KT, 2])
        modB = lasting("mod_shift", [KT, 2])
        gp = lasting("gate_post", [KT])
        stage = lasting("ada_rows", [G])
        mtmp = lasting("mod_tmp", [4, 2])
        lgrow = lasting("log_decays", [2, 8])
        lgs = lasting("decay_scales", [8, 3])
        lg4 = lasting("decay_scales_now", [2, 3])
        bst = lasting("bn", [4, 8, 6])
        mv = lasting("mean_var", [4, 2])
        rs = lasting("rstd", [4])
        half = lasting("minus_half", [4])
        idle = lasting("idle", [2])
        last_o = o
        xtmp = at("h_tmp", [2, 2 * N], o)
        pst = at("partial_out", [2, 2 * G], o + 4 * KB)
        ada_acc1 = at("ada_sums_first", [2, G], o + 12 * KB)
        assert o + 16 * KB <= nc.sbuf_usable_end
        vin = at("vectors_in", [7, P], R_D)
        diag = at("rstd_diag", [4, P], o + 4 * KB)
        Y = at("y_T", [KT, N], R_A)
        a = R_A + 32 * KB
        def work(name, shape):
            nonlocal a
            t = at(name, shape, a)
            a += (4 * int(np.prod(shape)) + 31) // 32 * 32
            return t
        q_sb = work("q", [2, G])
        k_sb = work("k", [4, G])
        v_sb = work("v", [4, G])
        kT = work("k_T", [2, 2, 2 * N])
        qT = work("q_T", [2, 2, N])
        a = last_o
        Dm = work("decay", [2, 768])
        tmp = work("tmp", [1024])
        upad = work("u_padded", [2, N + TAPS - 1])
        acc = work("conv_acc", [2, N])
        ssum = work("conv_sums", [2, N])
        w4 = work("taps_now", [TAPS, 4])
        b4 = work("conv_bias_now", [4])
        gn4 = work("gn_now", [4])
        ones_c = work("ones_mean", [2])
        assert a <= nc.sbuf_usable_end, (a, nc.sbuf_usable_end)
        Pm = at("weights_T", [2, 4, N], R_A + 36 * KB)
        g_sb = at("g_T", [4, N], R_A + 36 * KB)
        bb = at("conv_b", [4, N], R_A + 32 * KB)
        ab = at("conv_a", [4, N], R_A + 44 * KB)
        upad2 = at("u_padded_pool", [2, N + TAPS - 1], R_A + 44 * KB)
        prod = at("conv_product", [2, N], R_A + 48 * KB)
        lnm = at("ln_mean_rstd", [2, N], last_o + 4 * KB)
        lnt = at("ln_tokens", [4], last_o + 3 * KB)
        lnq = at("ln_mean_squared", [2], last_o + 3 * KB + 32)
        ada_acc2 = [at("ada_sums_k", [2, G], R_A + 52 * KB), at("ada_sums_v", [2, G], last_o + 6 * KB)]
        yr = [at("y_hi", [KT, N], R_B, F32R), at("y_lo", [KT, N], R_C, F32R)]
        yo = at("y_out", [2, D], R_A + 32 * KB)
        xres = at("x_again", [2, D], R_A)
        o2 = last_o
        diag4 = at("gate_diag", [4, P], o2)
        gpb = at("gate_rows", [G], o2 + 2 * KB)
        junk = at("squares", [G], o2 + 4 * KB)
        ones = at("ones", [P], o2 + 6 * KB)
        ss = at("sums_of_squares", [2, 8], o2 + 6 * KB + 512)

        ident = cst[:, C_ID:C_ID + P]
        sel = cst[:, C_SEL:C_SEL + 2]
        pick = [cst[:, C_PICK:C_PICK + 2], cst[:, C_PICK + 1:C_PICK + 3]]
        Jl = cst[:, C_J:C_J + 384]
        Jc = cst[:, C_J + 256:C_J + 640]

        bank = [psum(f"bank{n}") for n in range(8)]
        ADAB, SELB = bank[4], bank[5]
        XB = [bank[2], bank[3], bank[6], bank[7]]

        part = nc.dram_tensor("partials", [MODEL_GROUPS, P, 2 * G], F32, kind="Internal").ap()
        part_c = nc.dram_tensor("partials_ctx", [8, P, 2 * G], F32, kind="Internal").ap()
        w_in_v = w_in[0].rearrange("(t p) n -> p t n", p=P)
        ada_v = ada_w[0].rearrange("(t p) n -> p t n", p=P)
        w_out_v = w_out[0].rearrange("(t p) n -> p t n", p=P)

        s_const, s_vec, s_zero, s_lg = sem("constants_in"), sem("vectors_in"), sem("vectors_zeroed"), sem("decays_in")
        s_x = [sem(f"x_in{t}") for t in range(4)]
        s_raw = [sem(f"raw_in{n}") for n in range(RAW)]
        s_ada = [sem(f"ada_in{n}") for n in range(ADA)]
        s_hi, s_lo, s_used = sem("hi_ready"), sem("lo_ready"), sem("piece_used")
        s_ada_sum = sem("ada_vector_sums")
        s_ada_used, s_stage, s_sel, s_modt, s_mod = (sem(n) for n in (
            "ada_piece_used", "ada_rows_ready", "ada_selected", "mod_biased", "mod_ready"))
        s_full = [sem(f"bank_full{b}") for b in range(4)]
        s_free = [sem(f"bank_free{b}") for b in range(4)]
        s_vT, s_vt, s_cT, s_clear = sem("vectors_T"), sem("vectors_T_copied"), sem("silu_c"), sem("banks_cleared")
        s_bn, s_ms, s_rstd, s_diag = sem("x_stats"), sem("x_mean_square"), sem("x_rstd"), sem("x_diag")
        s_half = sem("minus_half_set")
        s_xT, s_xe = sem("xT_unit"), [sem("xT_copied_act"), sem("xT_copied_dve")]
        s_t, s_tf, s_h1, s_h2 = sem("h_affine"), sem("h_hi"), sem("h1_ready"), sem("h2_ready")
        s_pst = [sem("partial_stored0"), sem("partial_stored1")]
        s_kept = [sem("partial_buffer_free0"), sem("partial_buffer_free1")]
        s_pin = {n: sem(f"partial_in_{n}") for n in ("k", "kc", "q", "v", "vc", "g", "b", "a", "c0", "c1")}
        s_sig, s_u = sem("conv_sigmoid"), sem("conv_u")
        s_lgs, s_prep = sem("decay_scales"), sem("turn_vectors")
        s_darg, s_dexp, s_dmask, s_dm = sem("decay_args"), sem("decay_exp"), sem("decay_masked"), sem("decay_ready")
        s_rope, s_kr, s_qr = sem("rotary_parts"), sem("k_rotated"), sem("q_rotated")
        s_tr, s_te = sem("transposed"), sem("transposed_copied")
        s_sc, s_pm = sem("scores"), sem("weights_ready")
        s_av, s_gst, s_gag, s_gnin, s_gnr, s_yn = (sem(n) for n in (
            "attended", "gn_stats", "gn_mean_var", "gn_var_eps", "gn_rstd", "yn_ready"))
        s_yt, s_ye, s_gs, s_yg = sem("yn_T"), sem("yn_T_copied"), sem("g_silu"), sem("ret_done")
        s_cu, s_tap, s_sq, s_sqd = sem("conv_padded"), sem("conv_tap"), sem("conv_squared"), sem("conv_summed")
        s_pool_tap, s_tap0, s_su = sem("pool_conv_tap"), sem("pool_conv_first_tap"), sem("conv_u_summed")
        s_lnp, s_ln, s_lnvar, s_lnr = sem("ln_sums"), sem("ln_step"), sem("ln_var"), sem("ln_rstd")
        s_lnd, s_lnb, s_lnc = sem("ln_diag"), sem("ln_bcast"), sem("ln_rows_copied")
        s_zc, s_z, s_zs, s_cg, s_cy = (sem(n) for n in (
            "ln_centred", "ln_applied", "ln_silu", "conv_gate_silu", "conv_done"))
        s_yh, s_yl = sem("y_hi"), sem("y_lo")
        s_dg, s_gb, s_gbe, s_yq = sem("gate_diag"), sem("gate_bcast"), sem("gate_rows"), sem("y_squared")
        s_fin, s_var, s_frs, s_res, s_o, s_out = (sem(n) for n in (
            "final_step", "final_var", "final_rstd", "x_again_in", "out_ready", "out_stored"))
        s_one = sem("ones_ready")

        B01, B23, B03 = (0, 1), (2, 3), (0, 1, 2, 3)
        FIRST = [(4, [("ctx", B03), ("ctx", B03)]), (4, [("tok", B01)]), (8, [("ch", B01), ("ch", B23)])]
        SECOND = [(4, [("ch", B01), ("ch", B23)]),
                  (4, [("ctx", B03), ("tok", B01), ("ctx", B03), ("ch", B23)]),
                  (2, [("ch", B01), ("ch", B23)])]
        LO0 = RAW

        def uses(groups, b):
            return sum(b in banks for _, banks in groups)

        block = ctx.enter_context(nc.Block())

        @block.sync
        def _(sp):
            sp.dma_start(cst[:, :], consts).then_inc(s_const, 16)
            sp.wait_ge(s_zero, 1)

            def rows(ap, n):
                return ap.rearrange("(r p) -> r p", r=n)
            vecs = [(0, 0, rows(c[0], 32), 32), (0, 32, rows(c_ctx[0], 32), 32), (0, 64, rows(pre_norm_g[0], 32), 32),
                    (0, 96, rows(conv_dw_b[0], 16), 16), (0, 112, rows(ret_gn_g[0], 16), 16),
                    (1, 0, rows(ada_b[0], 96), 96), (1, 96, rows(conv_ln_g[0], 16), 16),
                    (1, 112, rows(conv_ln_b[0], 16), 16), (6, 48, rows(post_norm_g[0], 32), 32)]
            taps = conv_dw_w[0].rearrange("k (c p) -> (k c) p", p=P)
            vecs += [(t, 0, taps[16 * k:16 * (k + n), :], 16 * n) for t, k, n in TAP_TILES]
            for t, r, src, n in vecs:
                sp.dma_start(vin[r:r + n, t, :], src).then_inc(s_vec, 16)
            for h, lg in enumerate((lg_f, lg_b)):
                sp.dma_start(lgrow[:, h, :], lg[0].partition_broadcast(P)).then_inc(s_lg, 16)

            raw_n = Count(None)
            ada_n = Count(None)
            sums = Count(None, 8)
            dve_n = Count(None)

            def load_ada_beside(col, engine, piece, ops):
                if engine == "pe":
                    s = (ada_n.base + ada_n.k) % 2
                    sp.wait_ge(s_ada_used, ada_n.now(1))
                    ada_n.up()
                else:
                    s = 2 + (dve_n.base + dve_n.k) % 2
                    sp.wait_ge(s_ada_sum, sums.now(ops))
                    dve_n.up()
                    sums.up(ops)
                sp.dma_start(ada[:, s, :, :], ada_v[:, PK * piece:PK * piece + PK, bass.ds(col, G)]).then_inc(s_ada[s], 16)

            def load_ada(col, piece):
                n = ada_n.now()
                if not isinstance(n, int) or n >= ADA:
                    sp.wait_ge(s_ada_used, ada_n.now(ADA - 1))
                s = piece % ADA
                sp.dma_start(ada[:, s, :, :], ada_v[:, PK * piece:PK * piece + PK, bass.ds(col, G)]).then_inc(s_ada[s], 16)
                ada_n.up()

            def load_w(view, row_tile, col, piece):
                sp.wait_ge(s_lo, raw_n.now() + 1)
                s = piece % RAW
                sp.dma_start(raw[:, s, :, :], view[:, row_tile + PK * piece:row_tile + PK * piece + PK, bass.ds(col, G)]).then_inc(s_raw[s], 16)
                raw_n.up()

            for col in (0, D):
                for j in range(NPO):
                    load_ada(col, j)
            with sp.Fori(1, 4) as i:
                ada_n.enter(i, 2 * NPO, first=1)
                for col in (0, D):
                    for j in range(NPO):
                        load_ada(i * G + col, j)
            ada_n.leave(4)

            sp.wait_ge(s_ada_used, ada_n.now())

            def group(row_tile, col, ada_col=None):
                half = "first" if row_tile == 0 else "second"
                for j in range(NP):
                    load_w(w_in_v, row_tile, col, j)
                    for b in ([j - 2] if 2 <= j < NP - 1 else [j - 2, j - 1, j] if j == NP - 1 else []):
                        if ada_col is not None:
                            for engine, piece in ada_schedule(half)[b]:
                                load_ada_beside(ada_col, engine, piece, 4 if half == "first" else 2)

            def loop(turns, groups, half="first"):
                on_pe, on_dve = (sum(n) for n in BESIDE[half])
                n, beside = len(groups(0)), sum(g[2] is not None for g in groups(0))
                with sp.Fori(0, turns) as i:
                    raw_n.enter(i, n * NP)
                    ada_n.enter(i, beside * on_pe)
                    dve_n.enter(i, beside * on_dve)
                    sums.enter(i, beside * on_dve * (4 if half == "first" else 2))
                    for row_tile, col, ada_col in groups(i):
                        group(row_tile, col, ada_col)
                for cnt in (raw_n, ada_n, dve_n, sums):
                    cnt.leave(turns)

            loop(4, lambda i: [(0, i * G + COLS_K, i * G + D // 2), (0, i * G + COLS_V, i * G + D + D // 2)])
            loop(4, lambda i: [(0, i * G, None)])
            loop(8, lambda i: [(0, i * (2 * G) + COLS_G, None), (0, i * (2 * G) + COLS_G + G, None)])
            loop(4, lambda i: [(KH, i * G + COLS_B, None), (KH, i * G + COLS_A, None)], "second")
            loop(4, lambda i: [(KH, i * G + COLS_K, i * (2 * G) + 2 * D), (KH, i * G, None),
                               (KH, i * G + COLS_V, i * (2 * G) + 2 * D + G), (KH, i * G + COLS_G, None)], "second")
            loop(2, lambda i: [(KH, i * (2 * G) + COLS_C, None), (KH, i * (2 * G) + COLS_C + G, None)], "second")
            with sp.Fori(0, 8) as i:
                raw_n.enter(i, NPO)
                for j in range(NPO):
                    load_w(w_out_v, 0, i * G, j)
            raw_n.leave(8)
            sp.wait_ge(s_yl, NPO)
            for t in range(2):
                sp.dma_start(xres[:, t, :], x[0, t * P:(t + 1) * P, :]).then_inc(s_res, 16)
            for n in range(8):
                sp.wait_ge(s_o, n + 1)
                t, q = n // 4, n % 4
                sp.dma_start(out[0, t * P:(t + 1) * P, q * 1024:(q + 1) * 1024], yo[:, t, q * 1024:(q + 1) * 1024]).then_inc(s_out, 16)
            sp.wait_ge(s_out, 8 * 16)

        @block.tensor
        def _(pe):
            piece = Count(s_used)
            ada_p = Count(s_ada_used)
            beside_p = Count(None, ADA // 2 * (8 * NPO // ADA))
            sums = Count(s_ada_sum, 8)
            chunk = Count(None)
            bank_n = [Count(s_free[b], 1) for b in range(4)]

            def ada_piece(j, x_units=None):
                s = j % ADA
                pe.wait_ge(s_ada[s], ada_p.landed(s, ADA))
                for r in range(PK):
                    kt = PK * j + r
                    q = kt % 4
                    last = nc.tensor.matmul(ADAB[32 * q:32 * q + 2, :], cT[:, kt, :], ada[:, s, r, :],
                                            start=(kt < 4), stop=(kt >= KT - 4), tile_position=(0, 32 * q))
                last.then_inc(s_ada_used, 1)
                ada_p.up()

            def ada_beside(n, j, last_n):
                s = (beside_p.base + beside_p.k) % 2
                pe.wait_ge(s_ada[s], beside_p.landed(s, 2))
                for r in range(PK):
                    q = (PK * n + r) % 4
                    last = nc.tensor.matmul(ADAB[32 * q:32 * q + 2, :], cT[:, PK * j + r, :], ada[:, s, r, :],
                                            start=(n < 2), stop=(n >= last_n - 1), tile_position=(0, 32 * q))
                last.then_inc(s_ada_used, 1)
                ada_p.up()
                beside_p.up()

            def ada_select(acc=None, picks=None):
                if acc is not None:
                    pe.wait_ge(s_ada_sum, sums.now())
                pe.wait_ge(s_stage, chunk.now() + 1)
                if not isinstance(chunk.now(), int) or chunk.now() > 0:
                    pe.wait_ge(s_mod, chunk.now())
                for r in range(4):
                    last = nc.tensor.matmul(SELB[:, 2 * r:2 * r + 2], stage[:, r * P:(r + 1) * P], sel, start=True, stop=acc is None)
                    for n in range(0 if acc is None else 2):
                        last = nc.tensor.matmul(SELB[:, 2 * r:2 * r + 2], acc[:, n, r * P:(r + 1) * P], pick[picks[n]], start=False, stop=(n == 1))
                last.then_inc(s_sel, 1)
                chunk.up()

            for b in range(4):
                pe.sem_inc(s_free[b], 1)
            pe.wait_ge(s_const, 16)
            pe.wait_ge(s_vec, 14 * 16)
            for t in range(7):
                last = nc.tensor.transpose(bank[t // 4][:, (t % 4) * P:(t % 4 + 1) * P], vin[:, t, :], ident)
            last.then_inc(s_vT, 1)
            pe.wait_ge(s_cT, 1)
            pe.wait_ge(s_clear, 1)
            for j in range(NPO):
                ada_piece(j)
            ada_select()

            def x_unit(kt):
                if kt >= 4:
                    pe.wait_ge(s_xe[kt % 2], (kt - 4) // 2 + 1)
                for t in range(4):
                    if kt == 0:
                        pe.wait_ge(s_diag, t + 1)
                    last = nc.tensor.matmul(XB[kt % 4][:, t * P:(t + 1) * P], xs[:, t, kt * P:(kt + 1) * P], diag[:, t, :],
                                            start=True, stop=True)
                last.then_inc(s_xT, 1)
            for j in range(NPO):
                ada_piece(j)
                x_unit(2 * j)
                x_unit(2 * j + 1)
            ada_select()
            with pe.Fori(1, 4) as i:
                for cnt, per in ((ada_p, 2 * NPO), (chunk, 2)):
                    cnt.enter(i, per, first=1)
                for _ in range(2):
                    for j in range(NPO):
                        ada_piece(j)
                    ada_select()
            for cnt in (ada_p, chunk):
                cnt.leave(4)

            def wait_piece(j):
                pe.wait_ge(s_lo, piece.now() + 1 + LO0)

            def wait_banks(banks, j, b):
                if j == 0:
                    pe.wait_ge(s_free[b], bank_n[b].now())

            def tok_group(h, banks, beside=None, h_wait=None, with_ada=None, pieces=NP):
                n_ada = 0
                for j in range(pieces):
                    if beside and j in beside:
                        beside[j]()
                    if h_wait is not None:
                        pe.wait_ge(h_wait[0], h_wait[1] * (j + 1))
                    wait_piece(j)
                    s = j % 2
                    for r in range(PK):
                        kt = PK * j + r
                        for t, b in enumerate(banks):
                            if r == 0:
                                wait_banks(banks, j, b)
                            hh, hl = (h[n][:, kt, t * P:(t + 1) * P] for n in range(2))
                            nc.tensor.matmul(bank[b][:, :], hh, whi[:, s, r, :], start=(kt == 0), stop=False)
                            nc.tensor.matmul(bank[b][:, :], hh, wlo[:, s, r, :], start=False, stop=False)
                            last = nc.tensor.matmul(bank[b][:, :], hl, whi[:, s, r, :], start=False, stop=(kt == PK * pieces - 1))
                            if kt == PK * pieces - 1 and t < len(banks) - 1:
                                last.then_inc(s_full[b], 1)
                    last.then_inc(s_used, 1)
                    piece.up()
                    if with_ada:
                        for engine, a in ada_schedule(with_ada[0])[j]:
                            if engine == "pe":
                                ada_beside(n_ada, a, sum(BESIDE[with_ada[0]][0]) - 1)
                                n_ada += 1
                    if with_ada and j == NP - 1:
                        sums.up(sum(BESIDE[with_ada[0]][1]) * (4 if with_ada[0] == "first" else 2))
                        ada_select(*with_ada[1:])
                for b in banks:
                    bank_n[b].up()

            def ch_group(h, banks, beside=None):
                for j in range(NP):
                    if beside and j in beside:
                        beside[j]()
                    wait_piece(j)
                    s = j % 2
                    for r in range(PK):
                        kt = PK * j + r
                        for n in range(4):
                            b, co = banks[n // 2], (n % 2) * N
                            if r == 0 and n % 2 == 0:
                                wait_banks(banks, j, b)
                            to = bank[b][:, co:co + N]
                            wh, wl = (w[:, s, r, n * P:(n + 1) * P] for w in (whi, wlo))
                            end = kt == KH - 1
                            nc.tensor.matmul(to, wh, h[0][:, kt, 0:N], start=(kt == 0 and n % 2 == 0), stop=False, skip_group_check=True)
                            nc.tensor.matmul(to, wh, h[1][:, kt, 0:N], start=False, stop=False, skip_group_check=True)
                            last = nc.tensor.matmul(to, wl, h[0][:, kt, 0:N], start=False, stop=end, skip_group_check=True)
                            if end and n == 1:
                                last.then_inc(s_full[b], 1)
                    last.then_inc(s_used, 1)
                    piece.up()
                for b in banks:
                    bank_n[b].up()


            def loop(turns, kinds, body, ada_chunks=0, half="first"):
                on_pe, on_dve = (sum(n) for n in BESIDE[half])
                with pe.Fori(0, turns) as i:
                    piece.enter(i, NP * len(kinds))
                    ada_p.enter(i, ada_chunks * on_pe)
                    beside_p.enter(i, ada_chunks * on_pe)
                    sums.enter(i, ada_chunks * on_dve * (4 if half == "first" else 2))
                    chunk.enter(i, ada_chunks)
                    for b in range(4):
                        bank_n[b].enter(i, uses(kinds, b))
                    body(i)
                for cnt in (piece, ada_p, beside_p, sums, chunk, *bank_n):
                    cnt.leave(turns)

            pe.wait_ge(s_vt, 1)
            for n in range(2):
                pe.wait_ge(s_xe[n], KT // 2)
            (t1, k1), (t2, k2), (t3, k3) = FIRST
            both = ("first", ada_acc1, (0, 1))
            loop(t1, k1, lambda i: (tok_group(h1, B03, h_wait=(s_h1, PK), with_ada=both), tok_group(h1, B03, with_ada=both)), ada_chunks=2)
            loop(t2, k2, lambda i: tok_group(h1, B01))
            loop(t3, k3, lambda i: (ch_group(h1, B01), ch_group(h1, B23)))
            pe.wait_ge(s_h2, KH)
            (t4, k4), (t5, k5), (t6, k6) = SECOND
            loop(t4, k4, lambda i: (ch_group(h2, B01), ch_group(h2, B23)))

            def retention(i):

                def k_units(h):
                    def go():
                        if h == 0:
                            pe.wait_ge(s_kr, i + 1)
                            pe.wait_ge(s_ye, i * 4 + 1)
                        else:
                            pe.wait_ge(s_te, i * 6 + 2)
                        for dk in range(2):
                            for t in range(4):
                                last = nc.tensor.transpose(bank[6 + dk][:, t * P:(t + 1) * P],
                                                           k_sb[:, t, h * HD + dk * P:h * HD + (dk + 1) * P], ident)
                            last.then_inc(s_tr, 1)
                    return go

                def q_units():
                    pe.wait_ge(s_qr, i + 1)
                    pe.wait_ge(s_te, i * 6 + 4)
                    for h in range(2):
                        for dk in range(2):
                            for t in range(2):
                                last = nc.tensor.transpose(bank[6 + h][:, dk * N + t * P:dk * N + (t + 1) * P],
                                                           q_sb[:, t, h * HD + dk * P:h * HD + (dk + 1) * P], ident)
                        last.then_inc(s_tr, 1)

                def scores(h):
                    def go():
                        if h == 0:
                            pe.wait_ge(s_te, i * 6 + 6)
                        else:
                            pe.wait_ge(s_pm, i * 4 + 2)
                        for pair in range(2):
                            for m in range(2):
                                key = 2 * pair + m
                                for dk in range(2):
                                    last = nc.tensor.matmul(bank[6 + pair][:, m * N:(m + 1) * N], kT[:, h, dk, key * P:(key + 1) * P],
                                                            qT[:, h, dk, :], start=(dk == 0), stop=(dk == 1))
                            last.then_inc(s_sc, 1)
                    return go

                def attend(h):
                    def go():
                        if h == 0:
                            pe.wait_ge(s_pm, i * 4 + 4)
                            pe.wait_ge(s_free[3], bank_n[3].now())
                        for t in range(2):
                            for key in range(4):
                                last = nc.tensor.matmul(bank[6 + h][:, t * HD:(t + 1) * HD], Pm[:, h, key, t * P:(t + 1) * P],
                                                        v_sb[:, key, h * HD:(h + 1) * HD], start=(key == 0), stop=(key == 3))
                        last.then_inc(s_av, 1)
                    return go

                def y_units():
                    for h in range(2):
                        pe.wait_ge(s_yn, i * 2 + h + 1)
                        for e in range(2):
                            for t in range(2):
                                last = nc.tensor.transpose(bank[6 + h][:, e * N + t * P:e * N + (t + 1) * P],
                                                           q_sb[:, t, h * HD + e * P:h * HD + (e + 1) * P], ident)
                        last.then_inc(s_yt, 1)

                tok_group(h2, B03, with_ada=("second", ada_acc2[0], (0, 0)))
                tok_group(h2, B01)
                tok_group(h2, B03, beside={1: k_units(0), 2: k_units(1), 3: q_units, 4: scores(0), 5: scores(1)},
                          with_ada=("second", ada_acc2[1], (0, 0)))
                ch_group(h2, B23, beside={1: attend(0), 2: attend(1), 5: y_units})

            loop(t5, k5, retention, ada_chunks=2, half="second")

            def ln_sums():
                pe.wait_ge(s_sqd, 16)
                pe.wait_ge(s_one, 1)
                pe.wait_ge(s_ye, 16 + 1)
                for n in range(2):
                    for t in range(2):
                        m = 2 * (2 * n + t)
                        last = nc.tensor.matmul(bank[6][:, m:m + 2], ssum[:, n, t * P:(t + 1) * P], ones_c[:, 0:2], start=True, stop=True)
                last.then_inc(s_lnp, 1)

            def ln_rows():
                pe.wait_ge(s_lnd, 1)
                nc.tensor.matmul(bank[7][:, :], ones[:, :], diag4[:, :, :].rearrange("p a b -> p (a b)"), start=True, stop=True).then_inc(s_lnb, 1)
            ln_sums()
            for i in range(2):
                for cnt, per in ((piece, 2 * NP), *((cnt, 1) for cnt in bank_n)):
                    cnt.enter(i, per)
                ch_group(h2, B01, beside={5: ln_rows} if i == 0 else None)
                ch_group(h2, B23)
            for cnt in (piece, *bank_n):
                cnt.leave(2)

            def gate_rows(i, n):
                pe.wait_ge(s_dg, i * 2 + n + 1)
                nc.tensor.matmul(bank[7][:, :], ones[:, :], diag4[:, :, :].rearrange("p a b -> p (a b)"), start=True, stop=True).then_inc(s_gb, 1)

            def out_turn(i):
                for n, banks in enumerate((B01, B23)):
                    tok_group(yr, banks, beside={NPO - 2: lambda n=n: gate_rows(i, n)}, h_wait=(s_yl, 1), pieces=NPO)
            with pe.Fori(0, 4) as i:
                piece.enter(i, 2 * NPO)
                for b in range(4):
                    bank_n[b].enter(i, 1)
                out_turn(i)

        def full_waits(eng):
            n = {b: Count(s_full[b]) for b in range(4)}
            done = Count(s_used)

            def enter(i, groups, pieces=NP):
                for b in range(4):
                    n[b].enter(i, sum(b in banks[:-1] for _, banks in groups))
                done.enter(i, len(groups) * pieces)

            def leave(turns):
                for cnt in (done, *n.values()):
                    cnt.leave(turns)

            def wait(banks, b):
                if b == banks[-1]:
                    eng.wait_ge(s_used, done.now())
                else:
                    eng.wait_ge(s_full[b], n[b].now())

            def group(banks, pieces=NP):
                for b in banks[:-1]:
                    n[b].up()
                done.up(pieces)
            return enter, leave, wait, group

        @block.scalar
        def _(act):
            n_split = Count(None)

            def split(j):
                n = n_split.now()
                act.wait_ge(s_raw[j % RAW], n_split.landed(j % RAW, RAW))
                if not isinstance(n, int) or n >= 2:
                    act.wait_ge(s_used, n_split.now(1))
                nc.scalar.activation(whi[:, j % 2, :, :], raw[:, j % RAW, :, :], ACT.Copy).then_inc(s_hi, 1)
                n_split.up()

            enter, leave, wait_full, group_done = full_waits(act)
            free_n = [Count(s_free[b], 1) for b in range(4)]
            stored = [Count(s_kept[n], 1) for n in range(2)]
            ada_p = Count(s_ada_used)

            def group(banks, extras=None, evict=None, pieces=NP, last=False):
                for j in range(2, pieces + 1):
                    if not (last and j == pieces):
                        split(j)
                    if extras and j in extras:
                        extras[j]()
                group_done(banks, pieces)
                for b in banks:
                    free_n[b].up()
                if evict:
                    evict()
                if not last:
                    split(pieces + 1)
                if extras and pieces + 1 in extras:
                    extras[pieces + 1]()

            def rows(per_chunk=NPO):
                act.wait_ge(s_ada_used, ada_p.up(per_chunk))
                nc.scalar.activation(stage[:, :], ADAB[:, :], ACT.Copy).then_inc(s_stage, 1)

            def affine(hf, kt, gkt, ready):
                s = kt % 2
                act.wait_ge(ready[0], ready[1])
                for v in range(2):
                    if isinstance(gkt, int):
                        src, m = xT[hf][:, kt, v * N:(v + 1) * N], slice(gkt, gkt + 1)
                        sc_, bi_ = modA[:, gkt, v:v + 1], modB[:, gkt, v:v + 1]
                    last = nc.scalar.activation(xtmp[:, s, v * N:(v + 1) * N], src, ACT.Identity, scale=sc_, bias=bi_)
                last.then_inc(s_t, 1)

            act.wait_ge(s_vec, 14 * 16)
            for t in range(4):
                src = x[0, t * P:(t + 1) * P, :] if t < 2 else ctx_in[0, (t - 2) * P:(t - 1) * P, :]
                act.dma_start(xs[:, t, :], src).then_inc(s_x[t], 16)
            act.wait_ge(s_vt, 1)
            for v in range(2):
                last = nc.scalar.activation(cT[:, :, v], vt[:, 0, 32 * v:32 * v + 32], ACT.Silu)
            last.then_inc(s_cT, 1)
            rows()
            for kt in range(0, KT, 2):
                act.wait_ge(s_xT, kt + 1)
                nc.scalar.activation(xT[kt // KH][:, kt % KH, :], XB[kt % 4][:, :], ACT.Copy).then_inc(s_xe[0], 1)
            rows()
            act.wait_ge(s_xe[0], KT // 2)
            act.wait_ge(s_xe[1], KT // 2)
            for i in range(4):
                if i:
                    rows()
                    rows()
                if i == 3:
                    split(0)
                    split(1)
                act.wait_ge(s_mod, 2 * i + 2)
                for kt in range(4 * i, 4 * i + 4):
                    affine(0, kt, kt, (s_h1, kt - 1) if kt >= 2 else (s_mod, 2 * i + 2))

            def keep(h, banks):
                act.wait_ge(s_kept[h], stored[h].now())
                wait_full(banks, 2 * h)
                nc.scalar.activation(pst[:, h, 0:G], bank[2 * h][:, :], ACT.Copy).then_inc(s_free[2 * h], 1)
                stored[h].up()

            def loop(turns, kinds, body, ada_pieces=0, halves=(0, 0)):
                with act.Fori(0, turns) as i:
                    n_split.enter(i, NP * len(kinds))
                    ada_p.enter(i, ada_pieces)
                    enter(i, kinds)
                    for b in range(4):
                        free_n[b].enter(i, uses(kinds, b))
                    for h in range(2):
                        stored[h].enter(i, halves[h])
                    body(i)
                leave(turns)
                for cnt in (n_split, ada_p, *free_n, *stored):
                    cnt.leave(turns)

            on_pe = {half: sum(BESIDE[half][0]) for half in BESIDE}
            loop(4, FIRST[0][1], lambda i: [group(B03, {8: lambda: rows(on_pe["first"])}, lambda: (keep(0, B03), keep(1, B03))) for _ in range(2)],
                 ada_pieces=2 * on_pe["first"], halves=(2, 2))

            def q_body(i):
                def affines(r):
                    def go():
                        kt = i * 4 + r
                        act.wait_ge(s_h1, KH) if r < 0 else None
                        if r == 0:
                            act.wait_ge(s_mod, 16)
                        act.wait_ge(s_h2, kt - 1 + 2)
                        for v in range(2):
                            last = nc.scalar.activation(xtmp[:, r % 2, v * N:(v + 1) * N], xT[1][:, bass.ds(kt, 1), v * N:(v + 1) * N],
                                                        ACT.Identity, scale=modA[:, bass.ds(kt + KH, 1), v], bias=modB[:, bass.ds(kt + KH, 1), v])
                        last.then_inc(s_t, 1)
                    return go
                group(B01, {2 + r: affines(r) for r in range(4)}, lambda: keep(0, B01))
            loop(4, FIRST[1][1], q_body, halves=(1, 0))
            loop(8, FIRST[2][1], lambda i: (group(B01, None, lambda: keep(0, B01)), group(B23, None, lambda: keep(1, B23))), halves=(1, 1))

            def d_body(i):
                def sigmoid():
                    act.wait_ge(s_free[1], free_n[1].now())
                    nc.scalar.activation(bb[:, :, :], bb[:, :, :], ACT.Sigmoid).then_inc(s_sig, 1)
                group(B01, None, sigmoid)
                group(B23)
            loop(4, SECOND[0][1], d_body)

            def e_body(i):
                def exps(h):
                    def go():
                        act.wait_ge(s_darg, i * 2 + h + 1)
                        f, b, cb = (lg4[:, h, n:n + 1] for n in range(3))
                        nc.scalar.activation(Dm[:, h, 0:384], Dm[:, h, 0:384], ACT.Exp, scale=f)
                        nc.scalar.activation(Dm[:, h, 384:768], Jc, ACT.Exp, scale=f)
                        nc.scalar.activation(tmp[:, 0:384], tmp[:, 0:384], ACT.Exp, scale=b)
                        nc.scalar.activation(tmp[:, 384:768], Jc, ACT.Exp, scale=b, bias=cb).then_inc(s_dexp, 1)
                    return go

                def square(pair):
                    def go():
                        if pair == 0:
                            act.wait_ge(s_tap, i * 62 + 62)
                        else:
                            act.wait_ge(s_pool_tap, i * 60 + 60)
                            act.wait_ge(s_sqd, i * 4 + 2)
                        nc.scalar.activation(acc[:, :, :], Y[:, bass.ds(i * 4 + (16 + 2 * pair), 2), :], ACT.Square).then_inc(s_sq, 1)
                    return go

                def copy_T(n):
                    def go():
                        for u in (n, n + 1):
                            act.wait_ge(s_tr, i * 6 + u + 1)
                            if u < 4:
                                nc.scalar.activation(kT[:, u // 2, u % 2, :], bank[6 + u % 2][:, :], ACT.Copy, scale=float(HD) ** -0.5).then_inc(s_te, 1)
                            else:
                                nc.scalar.activation(qT[:, u - 4, :, :], bank[6 + u % 2][:, :], ACT.Copy).then_inc(s_te, 1)
                    return go

                def copy_y():
                    for h in range(2):
                        act.wait_ge(s_yt, i * 2 + h + 1)
                        for e in range(2):
                            nc.scalar.activation(Y[:, bass.ds(i * 4 + (2 * h + e), 1), :], bank[6 + h][:, e * N:(e + 1) * N],
                                                 ACT.Copy, scale=gn4[:, 2 * h + e:2 * h + e + 1]).then_inc(s_ye, 1)

                def silu_g():
                    act.wait_ge(s_free[3], free_n[3].now())
                    nc.scalar.activation(g_sb[:, :, :], g_sb[:, :, :], ACT.Silu).then_inc(s_gs, 1)
                gate_rows = lambda: rows(on_pe["second"])
                group(B03, {3: exps(0), 4: exps(1), 8: gate_rows})
                group(B01)
                group(B03, {2: copy_T(0), 3: copy_T(2), 4: copy_T(4), 7: square(0), 8: gate_rows})
                group(B23, {3: square(1), 6: copy_y}, silu_g)
            act.sem_inc(s_ye, 1)
            loop(4, SECOND[1][1], e_body, ada_pieces=2 * on_pe["second"])

            def split_y(m):
                if m == 0:
                    act.wait_ge(s_used, 56 * NP)
                nc.scalar.activation(yr[0][:, PK * m:PK * m + PK, :], Y[:, PK * m:PK * m + PK, :], ACT.Copy).then_inc(s_yh, 1)

            def ln_rows():
                act.wait_ge(s_lnb, 1)
                nc.scalar.activation(lnm[:, :, :], bank[7][:, :], ACT.Copy).then_inc(s_lnc, 1)

            def z_silu(g):
                def go():
                    act.wait_ge(s_z, g + 1)
                    for n in range(4):
                        ct = 4 * g + n
                        last = nc.scalar.activation(Y[:, 16 + ct, :], Y[:, 16 + ct, :], ACT.Silu, scale=vt[:, 1, 96 + ct:97 + ct], bias=vt[:, 1, 112 + ct:113 + ct])
                    last.then_inc(s_zs, 1)
                return go

            def gate_silu(g):
                def go():
                    if g == 3:
                        for m in range(4):
                            split_y(m)
                    b = 1 + 2 * (g % 2)
                    act.wait_ge(s_free[b], free_n[b].now())
                    buf = (bb, ab)[g % 2]
                    nc.scalar.activation(buf[:, :, :], buf[:, :, :], ACT.Silu).then_inc(s_cg, 1)
                return go
            for i in range(2):
                n_split.enter(i, 2 * NP)
                enter(i, SECOND[2][1])
                for b in range(4):
                    free_n[b].enter(i, 1)
                for n, banks in enumerate((B01, B23)):
                    group(banks, {6: ln_rows if i + n == 0 else (lambda: None), 8: z_silu(2 * i + n)}, gate_silu(2 * i + n))
            leave(2)
            for cnt in (n_split, *free_n):
                cnt.leave(2)

            def out_turn(i, first=False, end=False):
                n_split.enter(i, 2 * NPO)
                enter(i, SECOND[2][1], NPO)
                for b in range(4):
                    free_n[b].enter(i, 1)
                for n, banks in enumerate((B01, B23)):
                    def copy_gate():
                        act.wait_ge(s_gb, i * 2 + n + 1)
                        nc.scalar.activation(gpb[:, :], bank[7][:, :], ACT.Copy).then_inc(s_gbe, 1)

                    def squares():
                        for t, b in enumerate(banks):
                            wait_full(banks, b)
                            if not (first and n == 0 and t == 0):
                                act.wait_ge(s_yq, i * 4 + 2 * n + t)
                            nc.scalar.activation(junk[:, :], bank[b][:, :], ACT.Square,
                                                 accum_out=ss[:, t, bass.ds(i * 2 + n, 1)]).then_inc(s_yq, 1)
                    extras = {}
                    if first and n == 0:
                        extras = {j: (lambda m=j + 2: split_y(m)) for j in range(2, NPO - 2)}
                    extras[NPO - 1] = copy_gate
                    group(banks, extras, squares, NPO, last=end and n == 1)
            out_turn(0, first=True)
            with act.Fori(1, 3) as i:
                out_turn(i)
            out_turn(3, end=True)

        @block.vector
        def _(dve):
            n_split = Count(None)

            def split(j):
                dve.wait_ge(s_raw[j % RAW], n_split.landed(j % RAW, RAW))
                dve.wait_ge(s_hi, n_split.now() + 1)
                n = n_split.now()
                if not isinstance(n, int) or n >= 2:
                    dve.wait_ge(s_used, n_split.now(1))
                nc.vector.tensor_tensor(wlo[:, j % 2, :, :], raw[:, j % RAW, :, :], whi[:, j % 2, :, :].bitcast(F32), ALU.subtract).then_inc(s_lo, 1)
                n_split.up()

            enter, leave, wait_full, group_done = full_waits(dve)
            free_n = [Count(s_free[b], 1) for b in range(4)]
            stored = [Count(s_kept[n], 1) for n in range(2)]
            chunk, biased = Count(None), Count(s_modt)
            beside_n = Count(None, ADA // 2 * (8 * NPO // ADA))
            sums = Count(s_ada_sum, 8)

            def ada_sums(acc, half, b):
                first = next(j for tiles in ada_schedule(half) for e, j in tiles if e == "dve")
                for engine, j in ada_schedule(half)[b]:
                    if engine == "pe":
                        continue
                    s = (beside_n.base + beside_n.k) % 2
                    dve.wait_ge(s_ada[2 + s], beside_n.landed(s, 2))
                    for n, (r, v) in enumerate([(0, 0), (0, 1), (1, 0), (1, 1)] if half == "first" else [(0, 0), (1, 0)]):
                        to = acc[:, n % 2, :]
                        if j == first and n < 2:
                            nc.vector.tensor_scalar(to, ada[:, 2 + s, r, :], cT[:, PK * j + r, v:v + 1], None, ALU.mult).then_inc(s_ada_sum, 1)
                        else:
                            dve.wait_ge(s_ada_sum, sums.now(1))
                            nc.vector.scalar_tensor_tensor(out=to, in0=ada[:, 2 + s, r, :], scalar=cT[:, PK * j + r, v:v + 1], in1=to,
                                                           op0=ALU.mult, op1=ALU.add).then_inc(s_ada_sum, 1)
                        sums.up()
                    beside_n.up()

            def group(banks, extras=None, evict=None, pieces=NP, last=False):
                for j in range(2, pieces + 1):
                    if not (last and j == pieces):
                        split(j)
                    if extras and j in extras:
                        extras[j]()
                group_done(banks, pieces)
                for b in banks:
                    free_n[b].up()
                if evict:
                    evict()
                if not last:
                    split(pieces + 1)
                if extras and pieces + 1 in extras:
                    extras[pieces + 1]()

            def modulation(kind, kt):
                dve.wait_ge(s_sel, chunk.now() + 1)
                got = SELB[:, 0:8].rearrange("p (a v) -> p a v", v=2)
                def cols(t, at_):
                    v = vt[:, t, at_ + kt:at_ + kt + 4] if isinstance(kt, int) else vt[:, t, bass.ds(kt + at_, 4)]
                    return v
                def both(v):
                    return v.unsqueeze(2).broadcast_to([P, 4, 2])
                def kts(m):
                    return m[:, kt:kt + 4, :] if isinstance(kt, int) else m[:, bass.ds(kt, 4), :]
                if kind == "shift":
                    nc.vector.tensor_tensor(kts(modB), got, both(cols(1, 0)), ALU.add).then_inc(s_mod, 1)
                else:
                    nc.vector.tensor_tensor(mtmp[:, :, :], got, both(cols(1, 32 if kind == "scale" else 64)), ALU.add).then_inc(s_modt, 1)
                    dve.wait_ge(s_modt, biased.up())
                    if kind == "scale":
                        nc.vector.scalar_tensor_tensor(out=kts(modA), in0=mtmp[:, :, :], scalar=1.0, in1=both(cols(0, 64)),
                                                       op0=ALU.add, op1=ALU.mult).then_inc(s_mod, 1)
                    else:
                        to = gp[:, bass.ds(kt, 4)]
                        nc.vector.tensor_tensor(to, mtmp[:, :, 0], cols(6, 48), ALU.mult).then_inc(s_mod, 1)
                chunk.up()

            def split_h(kt, s, n, ready, done):
                dve.wait_ge(s_t, n + 1)
                nc.vector.tensor_copy(done[0][0][:, kt, :] if isinstance(kt, int) else done[0][0][:, bass.ds(kt, 1), :], xtmp[:, s, :]).then_inc(s_tf, 1)
                dve.wait_ge(s_tf, n + 1)
                hi, lo = (h[:, kt, :] if isinstance(kt, int) else h[:, bass.ds(kt, 1), :] for h in done[0])
                nc.vector.tensor_tensor(lo, xtmp[:, s, :] if isinstance(kt, int) else xtmp[:, s:s + 1, :], hi.bitcast(F32), ALU.subtract).then_inc(done[1], 1)

            nc.vector.memset(vin[:, :, :], 0.0).then_inc(s_zero, 1)
            nc.vector.memset(ADAB[:, :], 0.0).then_inc(s_clear, 1)
            dve.sem_inc(s_lo, LO0)
            dve.sem_inc(s_h2, 1)
            dve.sem_inc(s_ada_sum, 8)
            dve.wait_ge(s_const, 16)
            dve.wait_ge(s_lg, 32)
            nc.vector.tensor_copy(lgs[:, :, 0], lgrow[:, 0, :])
            nc.vector.tensor_scalar(lgs[:, :, 1], lgrow[:, 1, :], -1.0, None, ALU.mult)
            nc.vector.tensor_scalar(lgs[:, :, 2], lgrow[:, 1, :], 2.0 * N, None, ALU.mult).then_inc(s_lgs, 1)
            dve.wait_ge(s_vT, 1)
            nc.vector.tensor_copy(vt[:, 0:4, :], bank[0][:, :])
            nc.vector.tensor_copy(vt[:, 4:7, :], bank[1][:, 0:3 * P]).then_inc(s_vt, 1)
            dve.wait_ge(s_vt, 1)
            for t in range(4):
                dve.wait_ge(s_x[t], 16)
                for n in range(8):
                    last = nc.vector.bn_stats(bst[:, t, n, :], xs[:, t, n * G:(n + 1) * G])
                last.then_inc(s_bn, 1)
                dve.wait_ge(s_bn, 3 * t + 1)
                nc.vector.bn_aggr(mv[:, t, :], bst[:, t, :, :]).then_inc(s_bn, 1)
                dve.wait_ge(s_bn, 3 * t + 2)
                nc.vector.scalar_tensor_tensor(out=rs[:, t:t + 1], in0=mv[:, t, 0:1], scalar=mv[:, t, 0:1], in1=mv[:, t, 1:2],
                                               op0=ALU.mult, op1=ALU.add).then_inc(s_bn, 1)
                dve.wait_ge(s_bn, 3 * t + 3)
                nc.vector.tensor_scalar(rs[:, t:t + 1], rs[:, t:t + 1], EPS, None, ALU.add).then_inc(s_ms, 1)
            for t in range(4):
                dve.wait_ge(s_rstd, t + 1)
                nc.vector.tensor_scalar(diag[:, t, :], ident, rs[:, t:t + 1], None, ALU.mult).then_inc(s_diag, 1)
            modulation("shift", 0)
            for kt in range(1, KT, 2):
                dve.wait_ge(s_xT, kt + 1)
                nc.vector.tensor_copy(xT[kt // KH][:, kt % KH, :], XB[kt % 4][:, :]).then_inc(s_xe[1], 1)
            modulation("scale", 0)
            for i in range(4):
                if i:
                    modulation("shift", 4 * i)
                    modulation("scale", 4 * i)
                if i == 3:
                    split(0)
                    split(1)
                for kt in range(4 * i, 4 * i + 4):
                    split_h(kt, kt % 2, kt, None, (h1, s_h1))

            def keep(h, banks):
                dve.wait_ge(s_kept[h], stored[h].now())
                wait_full(banks, 2 * h + 1)
                nc.vector.tensor_copy(pst[:, h, G:2 * G], bank[2 * h + 1][:, :]).then_inc(s_free[2 * h + 1], 1)
                stored[h].up()

            def loop(turns, kinds, body, chunks=0, two_step=0, halves=(0, 0), half="first"):
                with dve.Fori(0, turns) as i:
                    n_split.enter(i, NP * len(kinds))
                    on_dve = chunks * sum(BESIDE[half][1])
                    beside_n.enter(i, on_dve)
                    sums.enter(i, on_dve * (4 if half == "first" else 2))
                    chunk.enter(i, chunks)
                    biased.enter(i, two_step)
                    enter(i, kinds)
                    for b in range(4):
                        free_n[b].enter(i, uses(kinds, b))
                    for h in range(2):
                        stored[h].enter(i, halves[h])
                    body(i)
                leave(turns)
                for cnt in (n_split, chunk, biased, beside_n, sums, *free_n, *stored):
                    cnt.leave(turns)

            in_first = {b + 2: lambda b=b: ada_sums(ada_acc1, "first", b) for b in range(7)}
            loop(4, FIRST[0][1], lambda i: [group(B03, {**in_first, 9: lambda kind=kind: modulation(kind, i * 4 + KH)},
                                                  lambda: (keep(0, B03), keep(1, B03))) for kind in ("shift", "scale")],
                 chunks=2, two_step=1, halves=(2, 2))

            def q_body(i):
                def splits(r):
                    return lambda: split_h(i * 4 + r, r % 2, i * 4 + (r + KH), None, (h2, s_h2))
                group(B01, {2 + r: splits(r) for r in range(4)}, lambda: keep(0, B01))
            loop(4, FIRST[1][1], q_body, halves=(1, 0))
            loop(8, FIRST[2][1], lambda i: (group(B01, None, lambda: keep(0, B01)), group(B23, None, lambda: keep(1, B23))), halves=(1, 1))

            def complete(buf, banks, b):
                wait_full(banks, b)
                nc.vector.tensor_tensor(buf, buf, bank[b][:, :], ALU.add).then_inc(s_free[b], 1)

            def ch_part(buf, n):
                return buf[:, 2 * n:2 * n + 2, :].rearrange("p a b -> p (a b)")

            dve.sem_inc(s_u, 1)

            def d_body(i):
                def take_b():
                    dve.wait_ge(s_pin["b"], i * 16 + 16)
                    for n in range(2):
                        complete(ch_part(bb, n), B01, n)

                def take_a():
                    dve.wait_ge(s_pin["a"], i * 16 + 16)
                    for n in range(2):
                        complete(ch_part(ab, n), B23, 2 + n)
                    dve.wait_ge(s_sig, i + 1)
                    dve.wait_ge(s_free[3], free_n[3].now())
                    nc.vector.tensor_tensor(Y[:, bass.ds(i * 4 + 16, 4), :], ab[:, :, :], bb[:, :, :], ALU.mult).then_inc(s_u, 1)
                group(B01, None, take_b)
                group(B23, None, take_a)
            loop(4, SECOND[0][1], d_body)

            dve.wait_ge(s_kept[0], 21)
            dve.wait_ge(s_kept[1], 17)
            nc.vector.memset(upad[:, :, :], 0.0)
            nc.vector.memset(ones_c[:, :], 1.0 / RET).then_inc(s_one, 1)
            nc.vector.memset(ssum[:, :, :], 0.0)
            dve.wait_ge(s_u, 5)

            def e_body(i):
                tap = Count(s_tap)
                tap.enter(i, 62)

                def prepare():
                    dve.wait_ge(s_ye, i * 4 + 1)
                    for t, k, n in TAP_TILES:
                        src = vt[:, t, 0:16 * n].rearrange("p (k c) -> p k c", c=16)[:, :, bass.ds(i * 4, 4)]
                        nc.vector.tensor_copy(w4[:, k:k + n, :], src)
                    nc.vector.tensor_copy(b4[:, :], vt[:, 0, bass.ds(i * 4 + 96, 4)])
                    nc.vector.tensor_copy(gn4[:, :], vt[:, 0, bass.ds(i * 4 + 112, 4)])
                    nc.vector.tensor_copy(lg4[:, :, :], lgs[:, bass.ds(i * 2, 2), :]).then_inc(s_prep, 1)
                    dve.wait_ge(s_prep, i + 1)

                def args(h):
                    if h == 1:
                        dve.wait_ge(s_dm, i * 2 + 1)
                    nc.vector.tensor_scalar(Dm[:, h, 0:384], Jl, 0.0, None, ALU.max)
                    nc.vector.tensor_scalar(tmp[:, 0:384], Jl, 0.0, None, ALU.min).then_inc(s_darg, 1)

                def combine(h):
                    dve.wait_ge(s_dexp, i * 2 + h + 1)
                    nc.vector.scalar_tensor_tensor(out=Dm[:, h, 0:384], in0=Jl, scalar=0.0, in1=Dm[:, h, 0:384], op0=ALU.is_ge, op1=ALU.mult)
                    nc.vector.scalar_tensor_tensor(out=tmp[:, 0:384], in0=Jl, scalar=0.0, in1=tmp[:, 0:384],
                                                   op0=ALU.is_le, op1=ALU.mult).then_inc(s_dmask, 1)
                    dve.wait_ge(s_dmask, i * 2 + h + 1)
                    nc.vector.tensor_tensor(Dm[:, h, :], Dm[:, h, :], tmp[:, 0:768], ALU.add).then_inc(s_dm, 1)

                def pad(to, pair):
                    for n in range(2):
                        last = nc.vector.tensor_copy(to[:, n, TAPS // 2:TAPS // 2 + N], Y[:, bass.ds(i * 4 + (16 + 2 * pair + n), 1), :])
                    last.then_inc(s_cu, 1)

                def start_pool_taps():
                    for edge in (0, TAPS // 2 + N):
                        nc.vector.memset(upad2[:, :, edge:edge + TAPS // 2], 0.0)
                    pad(upad2, 1)
                    dve.wait_ge(s_cu, i * 2 + 1)
                    for n in range(2):
                        last = nc.vector.tensor_scalar(Y[:, bass.ds(i * 4 + (18 + n), 1), :], upad2[:, n:n + 1, 0:N],
                                                       w4[:, 0, 2 + n:3 + n], b4[:, 2 + n:3 + n], ALU.mult, ALU.add)
                    last.then_inc(s_tap0, 1)
                    pad(upad, 0)
                    dve.wait_ge(s_cu, i * 2 + 2)

                def taps(first, last_):
                    for k in range(first, last_):
                        for n in range(2):
                            w = w4[:, k, n:n + 1]
                            src = upad[:, n, k:k + N]
                            if k == 0:
                                nc.vector.tensor_scalar(acc[:, n, :], src, w, b4[:, n:n + 1], ALU.mult, ALU.add).then_inc(s_tap, 1)
                            else:
                                dve.wait_ge(s_tap, tap.now(1))
                                to = acc[:, n, :] if k < TAPS - 1 else Y[:, bass.ds(i * 4 + (16 + n), 1), :]
                                nc.vector.scalar_tensor_tensor(out=to, in0=src, scalar=w, in1=acc[:, n, :], op0=ALU.mult, op1=ALU.add).then_inc(s_tap, 1)
                            tap.up()
                    if last_ == TAPS:
                        dve.wait_ge(s_tap, tap.now())
                        add_u(0)

                def add_u(pair):
                    for n in range(2):
                        nc.vector.tensor_tensor(ssum[:, 0:1, :], ssum[:, 0:1, :], Y[:, bass.ds(i * 4 + (16 + 2 * pair + n), 1), :], ALU.add).then_inc(s_su, 1)
                        dve.wait_ge(s_su, i * 4 + 2 * pair + n + 1)

                def add_squares(pair):
                    def go():
                        if pair == 1:
                            dve.wait_ge(s_pool_tap, i * 60 + 60)
                            add_u(1)
                        dve.wait_ge(s_sq, i * 2 + pair + 1)
                        for n in range(2):
                            nc.vector.tensor_tensor(ssum[:, 1, :], ssum[:, 1, :], acc[:, n, :], ALU.add).then_inc(s_sqd, 1)
                            dve.wait_ge(s_sqd, i * 4 + 2 * pair + n + 1)
                    return go

                def rotate(buf, done):
                    sin = cst[:, C_SIN:C_SIN + 512].rearrange("p (t a s f) -> p t a s f", t=2, a=2, s=2)
                    rt = tmp[:, :].rearrange("p (t h a s f) -> p t h a s f", t=2, h=2, a=2, s=2)
                    for t in range(2):
                        for h in range(2):
                            src = buf[:, t, h * HD:(h + 1) * HD].rearrange("p (a s f) -> p a s f", a=2, s=2)[:, :, ::-1, :]
                            last = nc.vector.tensor_tensor(rt[:, t, h], src, sin[:, t], ALU.mult)
                    last.then_inc(s_rope, 1)
                    step = 4 * i + (0 if done is s_kr else 2)
                    dve.wait_ge(s_rope, step + 1)
                    v = buf[:, 0:2, :].rearrange("p t (h d) -> p t h d", h=2)
                    cos = cst[:, C_COS:C_COS + 512].rearrange("p (t d) -> p t d", t=2).unsqueeze(2).broadcast_to([P, 2, 2, HD])
                    nc.vector.tensor_tensor(v, v, cos, ALU.mult).then_inc(s_rope, 1)
                    dve.wait_ge(s_rope, step + 2)
                    flat = buf[:, 0:2, :].rearrange("p t d -> p (t d)")
                    nc.vector.tensor_tensor(flat, flat, tmp[:, :], ALU.add).then_inc(done, 1)

                def take(names, buf, banks):
                    def go():
                        for name in names:
                            dve.wait_ge(s_pin[name], i * 16 + 16)
                        for t, b in enumerate(banks):
                            complete(buf[:, t, :], banks, b)
                        dve.wait_ge(s_free[banks[-1]], free_n[banks[-1]].now())
                    return go

                def weights(h):
                    def go():
                        for pair in range(2):
                            dve.wait_ge(s_sc, i * 4 + 2 * h + pair + 1)
                            for m in range(2):
                                w = pair * 384 + (P if m == 0 else 0)
                                last = nc.vector.tensor_tensor(Pm[:, h, 2 * pair + m, :], bank[6 + pair][:, m * N:(m + 1) * N], Dm[:, h, w:w + N], ALU.mult)
                            last.then_inc(s_pm, 1)
                    return go

                def gn_stats(h):
                    def go():
                        dve.wait_ge(s_av, i * 2 + h + 1)
                        for t in range(2):
                            last = nc.vector.bn_stats(bst[:, 2 * h + t, 0, :], bank[6 + h][:, t * HD:(t + 1) * HD])
                        last.then_inc(s_gst, 1)
                        dve.wait_ge(s_bn, 12)
                        dve.wait_ge(s_gst, i * 2 + h + 1)
                        for t in range(2):
                            last = nc.vector.bn_aggr(mv[:, 2 * h + t, :], bst[:, 2 * h + t, 0, :])
                        last.then_inc(s_gag, 1)
                        dve.wait_ge(s_gag, i * 2 + h + 1)
                        nc.vector.tensor_scalar(rs[:, 2 * h:2 * h + 2], mv[:, 2 * h:2 * h + 2, 1], EPS, None, ALU.add).then_inc(s_gnin, 1)
                    return go

                def gn_apply():
                    for h in range(2):
                        dve.wait_ge(s_gnr, i * 2 + h + 1)
                        for t in range(2):
                            n = 2 * h + t
                            last = nc.vector.tensor_scalar(q_sb[:, t, h * HD:(h + 1) * HD], bank[6 + h][:, t * HD:(t + 1) * HD],
                                                           mv[:, n, 0:1], rs[:, n:n + 1], ALU.subtract, ALU.mult)
                        last.then_inc(s_yn, 1)

                def take_g():
                    dve.wait_ge(s_pin["g"], i * 16 + 16)
                    for n in range(2):
                        complete(ch_part(g_sb, n), B23, 2 + n)

                def ada_k(b):
                    ada_sums(ada_acc2[0], "second", b)

                def ada_v(b):
                    dve.wait_ge(s_qr, i + 1)
                    ada_sums(ada_acc2[1], "second", b)

                group(B03, {2: lambda: (prepare(), args(0), start_pool_taps()), 3: lambda: (combine(0), args(1), ada_k(1)),
                            4: lambda: (combine(1), ada_k(2)), 5: lambda: (ada_k(3), taps(0, 4)), 6: lambda: (ada_k(4), taps(4, 8)),
                            7: lambda: (ada_k(5), taps(8, 12)), 9: lambda: modulation("gate", i * 8)},
                      take(("k", "kc"), k_sb, B03))
                group(B01, {2: lambda: rotate(k_sb, s_kr), **{j: lambda j=j: taps(9 + j, 10 + j) for j in range(3, 8)}},
                      take(("q",), q_sb, B01))
                group(B03, {2: lambda: rotate(q_sb, s_qr), 3: lambda: (ada_v(1), taps(17, 21)), 4: lambda: (ada_v(2), taps(21, 25)),
                            5: lambda: (weights(0)(), ada_v(3)), 6: lambda: (weights(1)(), ada_v(4), taps(25, 28)),
                            7: lambda: (ada_v(5), taps(28, TAPS)), 9: lambda: modulation("gate", i * 8 + 4)},
                      take(("v", "vc"), v_sb, B03))
                group(B23, {2: lambda: (gn_stats(0)(), add_squares(0)()), 3: gn_stats(1), 4: gn_apply, 6: add_squares(1)}, take_g)
            loop(4, SECOND[1][1], e_body, chunks=2, two_step=2, half="second")

            def ln_stats():
                dve.wait_ge(s_yg, 5)
                nc.vector.memset(ones[:, :], 1.0).then_inc(s_one, 1)
                dve.wait_ge(s_lnp, 1)
                nc.vector.tensor_copy(lnt[:, :], bank[6][:, 0:8:2]).then_inc(s_ln, 1)
                dve.wait_ge(s_ln, 1)
                nc.vector.tensor_tensor(lnq[:, :], lnt[:, 0:2], lnt[:, 0:2], ALU.mult).then_inc(s_ln, 1)
                dve.wait_ge(s_ln, 2)
                nc.vector.scalar_tensor_tensor(out=lnt[:, 2:4], in0=lnt[:, 2:4], scalar=EPS, in1=lnq[:, :],
                                               op0=ALU.add, op1=ALU.subtract).then_inc(s_lnvar, 1)

            def ln_diag():
                dve.wait_ge(s_lnr, 1)
                nc.vector.tensor_tensor(diag4[:, :, :], ident.unsqueeze(1).broadcast_to([P, 4, P]),
                                        lnt[:, :].unsqueeze(2).broadcast_to([P, 4, P]), ALU.mult).then_inc(s_lnd, 1)

            def z(g):
                def go():
                    dve.wait_ge(s_lnc, 1)
                    u = Y[:, 16 + 4 * g:20 + 4 * g, :]
                    m, r = (lnm[:, n, :].unsqueeze(1).broadcast_to([P, 4, N]) for n in range(2))
                    nc.vector.tensor_tensor(u, u, m, ALU.subtract).then_inc(s_zc, 1)
                    dve.wait_ge(s_zc, g + 1)
                    nc.vector.tensor_tensor(u, u, r, ALU.mult).then_inc(s_z, 1)
                return go

            def split_y(m):
                dve.wait_ge(s_yh, m + 1)
                nc.vector.tensor_tensor(yr[1][:, PK * m:PK * m + PK, :], Y[:, PK * m:PK * m + PK, :],
                                        yr[0][:, PK * m:PK * m + PK, :].bitcast(F32), ALU.subtract).then_inc(s_yl, 1)

            def conv_gate(g, banks):
                def go():
                    if g == 3:
                        for m in range(4):
                            split_y(m)
                    buf = (bb, ab)[g % 2]
                    dve.wait_ge(s_pin[f"c{g % 2}"], 16 * (g // 2 + 1))
                    for n in range(2):
                        complete(ch_part(buf, n), banks, banks[n])
                    dve.wait_ge(s_zs, g + 1)
                    dve.wait_ge(s_cg, g + 1)
                    u = Y[:, 16 + 4 * g:20 + 4 * g, :]
                    nc.vector.tensor_tensor(u, u, buf[:, :, :], ALU.mult).then_inc(s_cy, 1)
                return go
            for i in range(2):
                n_split.enter(i, 2 * NP)
                enter(i, SECOND[2][1])
                for b in range(4):
                    free_n[b].enter(i, 1)
                for n, banks in enumerate((B01, B23)):
                    g = 2 * i + n
                    extras = {7: z(g)}
                    if g == 0:
                        extras[2], extras[4] = ln_stats, ln_diag
                    group(banks, extras, conv_gate(g, banks))
            leave(2)
            for cnt in (n_split, *free_n):
                cnt.leave(2)

            def out_turn(i, first=False, end=False):
                n_split.enter(i, 2 * NPO)
                enter(i, SECOND[2][1], NPO)
                for b in range(4):
                    free_n[b].enter(i, 1)
                for n, banks in enumerate((B01, B23)):
                    def gate_diag():
                        v = gp[:, bass.ds(i * 8 + 4 * n, 4)].unsqueeze(2).broadcast_to([P, 4, P])
                        nc.vector.tensor_tensor(diag4[:, :, :], ident.unsqueeze(1).broadcast_to([P, 4, P]), v, ALU.mult).then_inc(s_dg, 1)

                    def gated():
                        dve.wait_ge(s_gbe, i * 2 + n + 1)
                        for t, b in enumerate(banks):
                            dve.wait_ge(s_yq, i * 4 + (2 * n + t + 1))
                            wait_full(banks, b)
                            nc.vector.tensor_tensor(yo[:, t, bass.ds(i * (2 * G) + n * G, G)], bank[b][:, :], gpb[:, :], ALU.mult).then_inc(s_free[b], 1)
                    extras = {}
                    if first and n == 0:
                        extras = {j: (lambda m=j + 2: split_y(m)) for j in range(2, NPO - 2)}
                        extras[2] = lambda: (dve.wait_ge(s_cy, 4), split_y(4), gate_diag())
                    else:
                        extras[2] = gate_diag
                    group(banks, extras, gated, NPO, last=end and n == 1)
            out_turn(0, first=True)
            with dve.Fori(1, 3) as i:
                out_turn(i)
            out_turn(3, end=True)

            dve.wait_ge(s_yq, 16)
            nc.vector.tensor_reduce(rs[:, 0:2], ss[:, :, :], AX.X, ALU.add).then_inc(s_fin, 1)
            dve.wait_ge(s_fin, 1)
            nc.vector.tensor_scalar(rs[:, 0:2], rs[:, 0:2], 1.0 / D, EPS, ALU.mult, ALU.add).then_inc(s_var, 1)
            dve.wait_ge(s_frs, 1)
            dve.wait_ge(s_res, 32)
            dve.wait_ge(s_free[1], free_n[1].now())
            dve.wait_ge(s_free[3], free_n[3].now())
            for t in range(2):
                for q in range(4):
                    y = yo[:, t, q * 1024:(q + 1) * 1024]
                    nc.vector.scalar_tensor_tensor(out=y, in0=y, scalar=rs[:, t:t + 1], in1=xres[:, t, q * 1024:(q + 1) * 1024],
                                                   op0=ALU.mult, op1=ALU.add).then_inc(s_o, 1)

        @block.gpsimd
        def _(pool):
            nc.gpsimd.memset(half[:, :], -0.5).then_inc(s_half, 1)
            for h in range(2):
                pool.sem_inc(s_kept[h], 1)
            pool.wait_ge(s_half, 1)
            for t in range(4):
                pool.wait_ge(s_ms, t + 1)
                nc.gpsimd.tensor_tensor(rs[:, t:t + 1], rs[:, t:t + 1], half[:, 0:1], ALU.pow).then_inc(s_rstd, 1)

            free_n = [Count(s_free[b], 1) for b in range(4)]
            kept = [Count(s_pst[h]) for h in range(2)]

            def store(h, to):
                pool.wait_ge(s_half, 1)
                for b in (2 * h, 2 * h + 1):
                    free_n[b].up()
                    pool.wait_ge(s_free[b], free_n[b].now())
                pool.dma_start(to, pst[:, h, :]).then_inc(s_pst[h], 16)
                pool.wait_ge(s_pst[h], kept[h].up(16))
                pool.sem_inc(s_kept[h], 1)

            def loop(turns, kinds, halves, body):
                with pool.Fori(0, turns) as i:
                    for b in range(4):
                        free_n[b].enter(i, uses(kinds, b))
                    for h in range(2):
                        kept[h].enter(i, 16 * halves[h])
                    body(i)
                for cnt in (*free_n, *kept):
                    cnt.leave(turns)

            def slot(t, n):
                return t[bass.ds(n, 1), :, :].rearrange("a p n -> (a p) n")
            loop(4, FIRST[0][1], (2, 2), lambda i: (store(0, slot(part, i + 4)), store(1, slot(part_c, i)),
                                            store(0, slot(part, i + 8)), store(1, slot(part_c, i + 4))))
            loop(4, FIRST[1][1], (1, 0), lambda i: store(0, slot(part, i)))
            loop(8, FIRST[2][1], (1, 1), lambda i: (store(0, slot(part, i * 2 + 12)), store(1, slot(part, i * 2 + 13))))
            pool.wait_ge(s_pst[0], 16 * 20)
            pool.wait_ge(s_pst[1], 16 * 16)
            pool.wait_ge(s_used, 28 * NP)

            def fetch(name, buf, src):
                pool.dma_start(buf, src).then_inc(s_pin[name], 16)

            def flat(t):
                return t.rearrange("p a b -> p (a b)")
            with pool.Fori(0, 4) as i:
                pool.wait_ge(s_half, 1)
                pool.wait_ge(s_u, i + 1)
                fetch("b", flat(bb[:, :, :]), slot(part, i + 20))
                fetch("a", flat(ab[:, :, :]), slot(part, i + 16))
            pool.wait_ge(s_u, 5)
            pool.sem_inc(s_yg, 1)
            with pool.Fori(0, 4) as i:
                pool.wait_ge(s_half, 1)
                pool.wait_ge(s_yg, i + 1)
                fetch("k", flat(k_sb[:, 0:2, :]), slot(part, i + 4))
                fetch("kc", flat(k_sb[:, 2:4, :]), slot(part_c, i))
                fetch("q", flat(q_sb[:, :, :]), slot(part, i))
                pool.wait_ge(s_tap0, i + 1)
                for k in range(1, TAPS):
                    w = w4[:, k, 2:4].unsqueeze(2).broadcast_to([P, 2, N])
                    if k > 1:
                        pool.wait_ge(s_pool_tap, i * 60 + 2 * (k - 1))
                    nc.gpsimd.tensor_tensor(prod[:, :, :], upad2[:, :, k:k + N], w, ALU.mult).then_inc(s_pool_tap, 1)
                    pool.wait_ge(s_pool_tap, i * 60 + 2 * k - 1)
                    nc.gpsimd.tensor_tensor(idle[:, :], half[:, 0:2], half[:, 0:2], ALU.add)
                    y2 = Y[:, bass.ds(i * 4 + 18, 2), :]
                    nc.gpsimd.tensor_tensor(y2, y2, prod[:, :, :], ALU.add).then_inc(s_pool_tap, 1)
                pool.wait_ge(s_half, 1)
                pool.wait_ge(s_pool_tap, i * 60 + 60)
                fetch("v", flat(v_sb[:, 0:2, :]), slot(part, i + 8))
                fetch("vc", flat(v_sb[:, 2:4, :]), slot(part_c, i + 4))
                pool.wait_ge(s_half, 1)
                pool.wait_ge(s_av, i * 2 + 2)
                fetch("g", flat(g_sb[:, :, :]), slot(part, i + 12))
                for h in range(2):
                    pool.wait_ge(s_gnin, i * 2 + h + 1)
                    nc.gpsimd.tensor_tensor(rs[:, 2 * h:2 * h + 2], rs[:, 2 * h:2 * h + 2], half[:, 0:2], ALU.pow).then_inc(s_gnr, 1)
                pool.wait_ge(s_gs, i + 1)
                pool.wait_ge(s_ye, i * 4 + 5)
                nc.gpsimd.tensor_tensor(idle[:, :], half[:, 0:2], half[:, 0:2], ALU.add)
                y4 = Y[:, bass.ds(i * 4, 4), :]
                nc.gpsimd.tensor_tensor(y4, y4, g_sb[:, :, :], ALU.mult).then_inc(s_yg, 1)
            pool.wait_ge(s_yg, 5)
            fetch("c0", flat(bb[:, :, :]), slot(part, 24))
            fetch("c1", flat(ab[:, :, :]), slot(part, 25))
            pool.wait_ge(s_lnvar, 1)
            nc.gpsimd.tensor_tensor(lnt[:, 2:4], lnt[:, 2:4], half[:, 0:2], ALU.pow).then_inc(s_lnr, 1)
            for g in range(2):
                pool.wait_ge(s_cy, g + 1)
                fetch(f"c{g}", flat((bb, ab)[g][:, :, :]), slot(part, 26 + g))
            pool.wait_ge(s_var, 1)
            nc.gpsimd.tensor_tensor(rs[:, 0:2], rs[:, 0:2], half[:, 0:2], ALU.pow).then_inc(s_frs, 1)


_INS = ["x", "c", "ctx", "c_ctx", "ada_w", "ada_b", "pre_norm_g", "post_norm_g", "w_in", "ret_log_decay_fwd",
        "ret_log_decay_bwd", "ret_gn_g", "conv_dw_w", "conv_dw_b", "conv_ln_g", "conv_ln_b", "w_out"]


def kernel(**inputs):
    import concourse.bacc as bacc
    from concourse.bass_utils import run_bass_kernel_spmd

    nc = bacc.Bacc("TRN2", target_bir_lowering=False, num_devices=1)
    arrays, args = {}, []
    for name in _INS:
        a = np.ascontiguousarray(inputs[name])
        if name == "c_ctx":
            a = a.reshape(1, D)
        arrays[f"in_{name}"] = a
        args.append(nc.dram_tensor(f"in_{name}", a.shape, mybir.dt.from_np(a.dtype), kind="ExternalInput").ap())
    consts = shape_constants()
    arrays["shape_constants"] = consts
    args.append(nc.dram_tensor("shape_constants", consts.shape, F32, kind="ExternalInput").ap())
    args.append(nc.dram_tensor("out", (1, N, D), F32, kind="ExternalOutput").ap())
    block_kernel(nc, *args)
    r = run_bass_kernel_spmd(nc, [arrays], core_ids=[0])
    return r.results[0]["out"]
```

```python
from contextlib import ExitStack

import numpy as np

import concourse.bass as bass
from concourse import mybir

ALU = mybir.AluOpType
ACT = mybir.ActivationFunctionType
F32 = mybir.dt.float32
F32R = mybir.dt.float32r
AX = mybir.AxisListType

P = 128
D = 4096
N = 256
RET = D // 2
HD = 256
TAPS = 31
EPS = 1e-6
G = 512
KT = D // P
K1, K2 = 12, 20
PK = 2
NP1, NP2 = K1 // PK, K2 // PK
NPO = KT // PK
RAW = 4
SPLIT = 4
ADA = 4
COLS_K, COLS_V, COLS_G, COLS_A, COLS_B, COLS_C = (RET * n for n in (1, 2, 3, 4, 5, 6))
MODEL_GROUPS = 7 * RET // G
BESIDE = {"first": ([2, 2, 2, 2, 1, 0], [2, 1, 2, 1, 1, 0]),
          "second": ([1, 1, 1, 1, 1, 1, 0, 0, 0, 0], [0, 1, 1, 2, 2, 2, 1, 1, 0, 0])}
LATE = (1, 3)
LATE_TURNS = NPO // (2 * len(LATE))
PER_Q = K2 // 4
TAP_TILES = [(2, 0, 7), (3, 7, 7), (4, 14, 7), (5, 21, 7), (6, 28, 3)]
C_ID, C_SEL, C_PICK, C_J, C_COS, C_SIN, C_END = 0, 128, 130, 134, 134 + 640, 134 + 640 + 512, 134 + 640 + 1024


def ada_schedule(half):
    j, out = 0, []
    for on_pe, on_dve in zip(*BESIDE[half]):
        out.append([(e, j + n) for n, e in enumerate(["pe"] * on_pe + ["dve"] * on_dve)])
        j += on_pe + on_dve
    assert j == NPO
    return out


def shape_constants():
    f = np.float32
    c = np.zeros((P, C_END), f)
    c[:, C_ID:C_ID + P] = np.eye(P, dtype=f)
    for q in range(4):
        for v in range(2):
            c[32 * q + v, C_SEL + v] = 1.0
    c[:, C_PICK:C_PICK + 4] = [1, 0, 1, 0]
    p = np.arange(P)[:, None]
    c[:, C_J:C_J + 640] = np.arange(640)[None, :] - p - P
    freq = f(10000.0) ** (-np.arange(64, dtype=f) / f(64))
    for t in range(2):
        tok = np.arange(P) + t * P
        for half, pos in enumerate((tok // 64, tok % 64)):
            ang = pos.astype(f)[:, None] * freq[None, :]
            at = t * 256 + half * 128
            c[:, C_COS + at:C_COS + at + 128] = np.tile(np.cos(ang), (1, 2))
            c[:, C_SIN + at:C_SIN + at + 64] = -np.sin(ang)
            c[:, C_SIN + at + 64:C_SIN + at + 128] = np.sin(ang)
    return c


class Count:

    def __init__(self, sem, start=0):
        self.sem, self.base, self.i, self.per, self.k = sem, start, 0, 0, 0

    def enter(self, i, per, first=0):
        if not self.per:
            self.base += self.k - first * per
        self.i, self.per, self.k = i, per, 0

    def landed(self, slot, slots, size=1):
        return self.i * (16 * self.per // (slots * size)) + 16 * (((self.base + self.k) // size - slot) // slots + 1)

    def leave(self, turns):
        assert self.k == self.per, (self.sem, self.k, self.per)
        self.base += self.per * turns
        self.i = self.per = self.k = 0

    def up(self, by=1):
        self.k += by
        return self.now()

    def now(self, less=0):
        fixed = self.base + self.k - less
        return self.i * self.per + fixed if self.per else fixed


def block_kernel(nc, x, c, ctx_in, c_ctx, ada_w, ada_b, pre_norm_g, post_norm_g, w_in,
                 lg_f, lg_b, ret_gn_g, conv_dw_w, conv_dw_b, conv_ln_g, conv_ln_b, w_out, consts, out):
    with ExitStack() as ctx:
        def sem(name):
            return ctx.enter_context(nc.semaphore(name))

        def psum(name):
            return ctx.enter_context(nc.psum_tensor(name, [P, G], F32))

        START = 16512
        KB = 1024
        R_A, R_L, R_H, R_D, R_E, R_F = (START + n * KB for n in (0, 48, 88, 128, 160, 176))

        def at(name, shape, offset, dt=F32):
            return nc.alloc_sbuf_tensor_at(name, [P] + shape, dt, offset=offset)

        xs = at("x_rows", [4, D], R_A)
        h1 = [at("h1_hi", [K1, 2 * N], R_A, F32R), at("h1_lo", [K1, 2 * N], R_A + 2 * K1 * KB, F32R)]
        xT = [at("xT_first", [K1, 2 * N], R_A + 64 * KB), at("xT_second", [K2, 2 * N], R_H)]
        h2 = [at("h2_hi", [K2, 2 * N], R_H, F32R), at("h2_lo", [K2, 2 * N], R_L, F32R)]
        raw = at("raw", [RAW, PK, G], R_D)
        whi = at("w_hi", [SPLIT, G], R_D + 16 * KB, F32R)
        wlo = at("w_lo", [SPLIT, G], R_D + 24 * KB, F32R)
        ada = at("ada_pieces", [ADA, PK, G], R_E)
        o = R_F
        def lasting(name, shape, dt=F32):
            nonlocal o
            t = at(name, shape, o, dt)
            o += (4 * int(np.prod(shape)) + 31) // 32 * 32
            return t
        cst = lasting("constants", [C_END])
        vt = lasting("vectors_T", [7, P])
        cT = lasting("silu_c_T", [KT, 2])
        modA = lasting("mod_scale", [KT, 2])
        modB = lasting("mod_shift", [KT, 2])
        gp = lasting("gate_post", [KT])
        stage = lasting("ada_rows", [G])
        mtmp = lasting("mod_tmp", [4, 2])
        lgrow = lasting("log_decays", [2, 8])
        lgs = lasting("decay_scales", [8, 3])
        lg4 = lasting("decay_scales_now", [2, 3])
        bst = lasting("bn", [4, 8, 6])
        mv = lasting("mean_var", [4, 2])
        rs = lasting("rstd", [4])
        half = lasting("minus_half", [4])
        idle = lasting("idle", [2])
        last_o = o
        xtmp = at("h_tmp", [2, 2 * N], o)
        pst = at("partial_out", [2, 2 * G], o + 4 * KB)
        ada_acc1 = at("ada_sums_first", [2, G], o + 12 * KB)
        assert o + 16 * KB <= nc.sbuf_usable_end
        vin = at("vectors_in", [7, P], R_D)
        diag = at("rstd_diag", [4, P], o + 4 * KB)
        Yc = at("y_conv_T", [KT // 2, N], R_A)
        Yr = at("y_ret_T", [KT // 2, N], R_E)
        W = a = R_A + 16 * KB
        def work(name, shape):
            nonlocal a
            t = at(name, shape, a)
            a += (4 * int(np.prod(shape)) + 31) // 32 * 32
            return t
        q_sb = work("q", [2, G])
        k_sb = work("k", [4, G])
        v_sb = work("v", [4, G])
        kT = work("k_T", [2, 2, 2 * N])
        qT = work("q_T", [2, 2, N])
        a = last_o
        Dm = work("decay", [2, 768])
        tmp = work("tmp", [1024])
        upad = work("u_padded", [2, N + TAPS - 1])
        acc = work("conv_acc", [2, N])
        ssum = work("conv_sums", [2, N])
        w4 = work("taps_now", [TAPS, 4])
        b4 = work("conv_bias_now", [4])
        gn4 = work("gn_now", [4])
        ones_c = work("ones_mean", [2])
        assert a <= nc.sbuf_usable_end, (a, nc.sbuf_usable_end)
        Pm = at("weights_T", [2, 4, N], W + 4 * KB)
        g_sb = at("g_T", [4, N], W + 4 * KB)
        bb = at("conv_b", [4, N], W)
        ab = at("conv_a", [4, N], W + 12 * KB)
        upad2 = at("u_padded_pool", [2, N + TAPS - 1], W + 12 * KB)
        prod = at("conv_product", [2, N], W + 16 * KB)
        lnm = at("ln_mean_rstd", [2, N], last_o + 4 * KB)
        lnt = at("ln_tokens", [4], last_o + 3 * KB)
        lnq = at("ln_mean_squared", [2], last_o + 3 * KB + 32)
        y_now = at("y_ret_now", [4, N], W + 24 * KB)
        ada_acc2 = [at("ada_sums_k", [2, G], W + 20 * KB), at("ada_sums_v", [2, G], last_o + 6 * KB)]
        ys = [at("y_hi", [KT, N], R_L, F32R), at("y_lo", [KT, N], R_L + 32 * KB, F32R)]
        yo = at("y_out", [2, D], W)
        xres = [at("x_again0", [D], R_L + 64 * KB), at("x_again1", [D], R_A)]
        o2 = last_o
        diag4 = at("gate_diag", [4, P], o2)
        gpb = at("gate_rows", [G], o2 + 2 * KB)
        junk = at("squares", [G], o2 + 4 * KB)
        ones = at("ones", [P], o2 + 6 * KB)
        ss = at("sums_of_squares", [2, 8], o2 + 6 * KB + 512)

        def y_tiles(m):
            n = PK * m
            return Yr[:, n:n + PK, :] if n < KT // 2 else Yc[:, n - KT // 2:n - KT // 2 + PK, :]

        ident = cst[:, C_ID:C_ID + P]
        sel = cst[:, C_SEL:C_SEL + 2]
        pick = [cst[:, C_PICK:C_PICK + 2], cst[:, C_PICK + 1:C_PICK + 3]]
        Jl = cst[:, C_J:C_J + 384]
        Jc = cst[:, C_J + 256:C_J + 640]

        bank = [psum(f"bank{n}") for n in range(8)]
        ADAB, SELB = bank[4], bank[5]
        XB = [bank[2], bank[3], bank[6], bank[7]]

        part = nc.dram_tensor("partials", [MODEL_GROUPS, P, 2 * G], F32, kind="Internal").ap()
        part_c = nc.dram_tensor("partials_ctx", [8, P, 2 * G], F32, kind="Internal").ap()
        y_ret = nc.dram_tensor("y_ret", [4, P, 4 * N], F32, kind="Internal").ap()
        w_in_v = w_in[0].rearrange("(t p) n -> p t n", p=P)
        ada_v = ada_w[0].rearrange("(t p) n -> p t n", p=P)
        w_out_v = w_out[0].rearrange("(t p) n -> p t n", p=P)

        s_const, s_vec, s_zero, s_lg = sem("constants_in"), sem("vectors_in"), sem("vectors_zeroed"), sem("decays_in")
        s_x = [sem(f"x_in{t}") for t in range(4)]
        s_raw = [sem(f"raw_in{n}") for n in range(RAW)]
        s_ada = [sem(f"ada_in{n}") for n in range(ADA)]
        s_hi, s_lo, s_used = sem("hi_ready"), sem("lo_ready"), sem("k_tile_used")
        s_ada_sum = sem("ada_vector_sums")
        s_ada_used, s_stage, s_sel, s_modt, s_mod = (sem(n) for n in (
            "ada_piece_used", "ada_rows_ready", "ada_selected", "mod_biased", "mod_ready"))
        s_full = [sem(f"bank_full{b}") for b in range(4)]
        s_free = [sem(f"bank_free{b}") for b in range(4)]
        s_vT, s_vt, s_cT, s_clear = sem("vectors_T"), sem("vectors_T_copied"), sem("silu_c"), sem("banks_cleared")
        s_bn, s_ms, s_rstd, s_diag = sem("x_stats"), sem("x_mean_square"), sem("x_rstd"), sem("x_diag")
        s_half = sem("minus_half_set")
        s_xT, s_xe = sem("xT_unit"), [sem("xT_copied_act"), sem("xT_copied_dve")]
        s_t, s_tf, s_h1, s_h2 = sem("h_affine"), sem("h_hi"), sem("h1_ready"), sem("h2_ready")
        s_pst = [sem("partial_stored0"), sem("partial_stored1")]
        s_kept = [sem("partial_buffer_free0"), sem("partial_buffer_free1")]
        s_pin = {n: sem(f"partial_in_{n}") for n in ("k", "kc", "q", "v", "vc", "g", "b", "a", "c0", "c1")}
        s_sig, s_u = sem("conv_sigmoid"), sem("conv_u")
        s_lgs, s_prep = sem("decay_scales"), sem("turn_vectors")
        s_darg, s_dexp, s_dmask, s_dm = sem("decay_args"), sem("decay_exp"), sem("decay_masked"), sem("decay_ready")
        s_rope, s_kr, s_qr = sem("rotary_parts"), sem("k_rotated"), sem("q_rotated")
        s_tr, s_te = sem("transposed"), sem("transposed_copied")
        s_sc, s_pm = sem("scores"), sem("weights_ready")
        s_av, s_gst, s_gag, s_gnin, s_gnr, s_yn = (sem(n) for n in (
            "attended", "gn_stats", "gn_mean_var", "gn_var_eps", "gn_rstd", "yn_ready"))
        s_yt, s_ye, s_gs, s_yg = sem("yn_T"), sem("yn_T_copied"), sem("g_silu"), sem("ret_done")
        s_cu, s_tap, s_sq, s_sqd = sem("conv_padded"), sem("conv_tap"), sem("conv_squared"), sem("conv_summed")
        s_pool_tap, s_tap0, s_su = sem("pool_conv_tap"), sem("pool_conv_first_tap"), sem("conv_u_summed")
        s_lnp, s_ln, s_lnvar, s_lnr = sem("ln_sums"), sem("ln_step"), sem("ln_var"), sem("ln_rstd")
        s_lnd, s_lnb, s_lnc = sem("ln_diag"), sem("ln_bcast"), sem("ln_rows_copied")
        s_zc, s_z, s_zs, s_cg, s_cy = (sem(n) for n in (
            "ln_centred", "ln_applied", "ln_silu", "conv_gate_silu", "conv_done"))
        s_yh, s_yl = sem("y_hi"), sem("y_lo")
        s_yst, s_yin, s_late = sem("y_ret_stored"), sem("y_ret_in"), sem("late_sums_zeroed")
        s_gy = sem("ret_gated")
        s_dg, s_gb, s_gbe, s_yq = sem("gate_diag"), sem("gate_bcast"), sem("gate_rows"), sem("y_squared")
        s_fin, s_var, s_frs, s_res, s_o, s_out = (sem(n) for n in (
            "final_step", "final_var", "final_rstd", "x_again_in", "out_ready", "out_stored"))
        s_one = sem("ones_ready")

        B01, B23, B03 = (0, 1), (2, 3), (0, 1, 2, 3)
        FIRST = [(4, [("ctx", B03), ("ctx", B03)]), (LATE_TURNS, [("ch", B01), ("ch", B23)]),
                 (LATE_TURNS, [("ch", B01), ("ch", B23)]), (2, [("tok", B01), ("tok", B01)])]
        SECOND = [(4, [("ch", B01), ("ch", B23)]),
                  (4, [("ctx", B03), ("tok", B01), ("ctx", B03), ("ch", B23)]),
                  (2, [("ch", B01), ("ch", B23)])]
        LO0 = RAW * PK

        def uses(groups, b):
            return sum(b in banks for _, banks in groups)

        block = ctx.enter_context(nc.Block())

        @block.sync
        def _(sp):
            sp.dma_start(cst[:, :], consts).then_inc(s_const, 16)
            sp.wait_ge(s_zero, 1)

            def rows(ap, n):
                return ap.rearrange("(r p) -> r p", r=n)
            vecs = [(0, 0, rows(c[0], 32), 32), (0, 32, rows(c_ctx[0], 32), 32), (0, 64, rows(pre_norm_g[0], 32), 32),
                    (0, 96, rows(conv_dw_b[0], 16), 16), (0, 112, rows(ret_gn_g[0], 16), 16),
                    (1, 0, rows(ada_b[0], 96), 96), (1, 96, rows(conv_ln_g[0], 16), 16),
                    (1, 112, rows(conv_ln_b[0], 16), 16), (6, 48, rows(post_norm_g[0], 32), 32)]
            taps = conv_dw_w[0].rearrange("k (c p) -> (k c) p", p=P)
            vecs += [(t, 0, taps[16 * k:16 * (k + n), :], 16 * n) for t, k, n in TAP_TILES]
            for t, r, src, n in vecs:
                sp.dma_start(vin[r:r + n, t, :], src).then_inc(s_vec, 16)
            for h, lg in enumerate((lg_f, lg_b)):
                sp.dma_start(lgrow[:, h, :], lg[0].partition_broadcast(P)).then_inc(s_lg, 16)

            raw_n = Count(None)
            ada_n = Count(None)
            sums = Count(None, 8)
            dve_n = Count(None)

            def load_ada_beside(col, engine, piece, ops):
                if engine == "pe":
                    s = (ada_n.base + ada_n.k) % 2
                    sp.wait_ge(s_ada_used, ada_n.now(1))
                    ada_n.up()
                else:
                    s = 2 + (dve_n.base + dve_n.k) % 2
                    sp.wait_ge(s_ada_sum, sums.now(ops))
                    dve_n.up()
                    sums.up(ops)
                tiles = slice(PK * piece, PK * piece + PK) if isinstance(piece, int) else bass.ds(piece * PK, PK)
                sp.dma_start(ada[:, s, :, :], ada_v[:, tiles, bass.ds(col, G)]).then_inc(s_ada[s], 16)

            def load_ada(col, piece):
                n = ada_n.now()
                if not isinstance(n, int) or n >= ADA:
                    sp.wait_ge(s_ada_used, ada_n.now(ADA - 1))
                s = piece % ADA
                sp.dma_start(ada[:, s, :, :], ada_v[:, PK * piece:PK * piece + PK, bass.ds(col, G)]).then_inc(s_ada[s], 16)
                ada_n.up()

            def load_w(view, row_tile, col, piece):
                sp.wait_ge(s_lo, raw_n.now() * PK + PK)
                s = (raw_n.base + raw_n.k) % RAW
                sp.dma_start(raw[:, s, :, :], view[:, row_tile + PK * piece:row_tile + PK * piece + PK, bass.ds(col, G)]).then_inc(s_raw[s], 16)
                raw_n.up()

            for col in (0, D):
                for j in range(NPO):
                    load_ada(col, j)
            with sp.Fori(1, K1 // 4) as i:
                ada_n.enter(i, 2 * NPO, first=1)
                for col in (0, D):
                    for j in range(NPO):
                        load_ada(i * G + col, j)
            ada_n.leave(K1 // 4)

            sp.wait_ge(s_ada_used, ada_n.now())

            def group(half, col, ada_col=None, late=None):
                row_tile, pieces = (0, NP1) if half == "first" else (K1, NP2)
                for j in range(pieces):
                    load_w(w_in_v, row_tile, col, j)
                    for b in ([j - 2] if 2 <= j < pieces - 1 else [j - 2, j - 1, j] if j == pieces - 1 else []):
                        if ada_col is not None:
                            for engine, piece in ada_schedule(half)[b]:
                                load_ada_beside(ada_col, engine, piece, 4 if half == "first" else 2)
                        if late is not None and b in LATE:
                            load_ada_beside(late[0], "dve", late[1] + LATE.index(b), 4)

            def loop(turns, half, groups, late=0):
                on_pe, on_dve = (sum(n) for n in BESIDE[half])
                gs = groups(0)
                beside = sum(g[1] is not None for g in gs)
                with sp.Fori(0, turns) as i:
                    raw_n.enter(i, len(gs) * (NP1 if half == "first" else NP2))
                    ada_n.enter(i, beside * on_pe)
                    dve_n.enter(i, beside * on_dve + late)
                    sums.enter(i, (beside * on_dve + late) * (4 if half == "first" else 2))
                    for g in groups(i):
                        group(half, *g)
                for cnt in (raw_n, ada_n, dve_n, sums):
                    cnt.leave(turns)

            loop(4, "first", lambda i: [(i * G + COLS_K, i * G + K1 * P), (i * G + COLS_V, i * G + D + K1 * P)])
            for n, col in enumerate((D - G, 2 * D - G)):
                at_ = COLS_G + n * LATE_TURNS * 2 * G
                loop(LATE_TURNS, "first", lambda i: [(i * (2 * G) + at_, None, (col, i * 4)),
                                                     (i * (2 * G) + (at_ + G), None, (col, i * 4 + 2))], late=2 * len(LATE))
            loop(2, "first", lambda i: [(i * (2 * G), None), (i * (2 * G) + G, None)])
            loop(4, "second", lambda i: [(i * G + COLS_B, None), (i * G + COLS_A, None)])
            loop(4, "second", lambda i: [(i * G + COLS_K, i * (2 * G) + 2 * D), (i * G, None),
                                         (i * G + COLS_V, i * (2 * G) + 2 * D + G), (i * G + COLS_G, None)])
            loop(2, "second", lambda i: [(i * (2 * G) + COLS_C, None), (i * (2 * G) + COLS_C + G, None)])
            with sp.Fori(0, 8) as i:
                raw_n.enter(i, NPO)
                for j in range(NPO):
                    load_w(w_out_v, 0, i * G, j)
            raw_n.leave(8)
            sp.wait_ge(s_yl, NPO)
            for t in range(2):
                sp.dma_start(xres[t][:, :], x[0, t * P:(t + 1) * P, :]).then_inc(s_res, 16)
            for n in range(8):
                sp.wait_ge(s_o, n + 1)
                t, q = n // 4, n % 4
                sp.dma_start(out[0, t * P:(t + 1) * P, q * 1024:(q + 1) * 1024], yo[:, t, q * 1024:(q + 1) * 1024]).then_inc(s_out, 16)
            sp.wait_ge(s_out, 8 * 16)

        @block.tensor
        def _(pe):
            tile = Count(s_used)
            ada_p = Count(s_ada_used)
            beside_p = Count(None, 2 * K1 // 4 * NPO // 2)
            sums = Count(s_ada_sum, 8)
            chunk, staged = Count(None), Count(s_stage)
            bank_n = [Count(s_free[b], 1) for b in range(4)]

            def ada_piece(j, x_units=None):
                s = j % ADA
                pe.wait_ge(s_ada[s], ada_p.landed(s, ADA))
                for r in range(PK):
                    kt = PK * j + r
                    q = kt % 4
                    last = nc.tensor.matmul(ADAB[32 * q:32 * q + 2, :], cT[:, kt, :], ada[:, s, r, :],
                                            start=(kt < 4), stop=(kt >= KT - 4), tile_position=(0, 32 * q))
                last.then_inc(s_ada_used, 1)
                ada_p.up()

            def ada_beside(n, j, last_n):
                s = (beside_p.base + beside_p.k) % 2
                pe.wait_ge(s_ada[s], beside_p.landed(s, 2))
                for r in range(PK):
                    q = (PK * n + r) % 4
                    last = nc.tensor.matmul(ADAB[32 * q:32 * q + 2, :], cT[:, PK * j + r, :], ada[:, s, r, :],
                                            start=(n < 2), stop=(n >= last_n - 1), tile_position=(0, 32 * q))
                last.then_inc(s_ada_used, 1)
                ada_p.up()
                beside_p.up()

            def ada_select(acc=None, picks=None, rows=True):
                if acc is not None:
                    pe.wait_ge(s_ada_sum, sums.now())
                if rows:
                    pe.wait_ge(s_stage, staged.up())
                if not isinstance(chunk.now(), int) or chunk.now() > 0:
                    pe.wait_ge(s_mod, chunk.now())
                for r in range(4):
                    to = SELB[:, 2 * r:2 * r + 2]
                    if rows:
                        last = nc.tensor.matmul(to, stage[:, r * P:(r + 1) * P], sel, start=True, stop=acc is None)
                    for n in range(0 if acc is None else 2):
                        last = nc.tensor.matmul(to, acc[:, n, r * P:(r + 1) * P], pick[picks[n]], start=not rows and n == 0, stop=(n == 1))
                last.then_inc(s_sel, 1)
                chunk.up()

            for b in range(4):
                pe.sem_inc(s_free[b], 1)
            pe.wait_ge(s_const, 16)
            pe.wait_ge(s_vec, 14 * 16)
            for t in range(7):
                last = nc.tensor.transpose(bank[t // 4][:, (t % 4) * P:(t % 4 + 1) * P], vin[:, t, :], ident)
            last.then_inc(s_vT, 1)
            pe.wait_ge(s_cT, 1)
            pe.wait_ge(s_clear, 1)
            for j in range(NPO):
                ada_piece(j)
            ada_select()

            def x_unit(kt):
                if kt >= 4:
                    pe.wait_ge(s_xe[kt % 2], (kt - 4) // 2 + 1)
                for t in range(4):
                    if kt == 0:
                        pe.wait_ge(s_diag, t + 1)
                    last = nc.tensor.matmul(XB[kt % 4][:, t * P:(t + 1) * P], xs[:, t, kt * P:(kt + 1) * P], diag[:, t, :],
                                            start=True, stop=True)
                last.then_inc(s_xT, 1)
            for j in range(NPO):
                ada_piece(j)
                x_unit(2 * j)
                x_unit(2 * j + 1)
            ada_select()
            with pe.Fori(1, K1 // 4) as i:
                for cnt, per in ((ada_p, 2 * NPO), (chunk, 2), (staged, 2)):
                    cnt.enter(i, per, first=1)
                for _ in range(2):
                    for j in range(NPO):
                        ada_piece(j)
                    ada_select()
            for cnt in (ada_p, chunk, staged):
                cnt.leave(K1 // 4)

            def wait_tile():
                pe.wait_ge(s_lo, tile.now() + 1 + LO0)

            def wait_banks(banks, j, b):
                if j == 0:
                    pe.wait_ge(s_free[b], bank_n[b].now())

            def tok_group(h, banks, beside=None, h_wait=None, with_ada=None, pieces=NP2):
                n_ada = 0
                for j in range(pieces):
                    if beside and j in beside:
                        beside[j]()
                    if h_wait is not None:
                        pe.wait_ge(h_wait[0], h_wait[1] * (j + 1))
                    for r in range(PK):
                        kt = PK * j + r
                        wait_tile()
                        for t, b in enumerate(banks):
                            if r == 0:
                                wait_banks(banks, j, b)
                            hh, hl = (h[n][:, kt, t * P:(t + 1) * P] for n in range(2))
                            nc.tensor.matmul(bank[b][:, :], hh, whi[:, kt % SPLIT, :], start=(kt == 0), stop=False)
                            nc.tensor.matmul(bank[b][:, :], hh, wlo[:, kt % SPLIT, :], start=False, stop=False)
                            last = nc.tensor.matmul(bank[b][:, :], hl, whi[:, kt % SPLIT, :], start=False, stop=(kt == PK * pieces - 1))
                            if kt == PK * pieces - 1 and t < len(banks) - 1:
                                last.then_inc(s_full[b], 1)
                        last.then_inc(s_used, 1)
                        tile.up()
                    if with_ada:
                        for engine, a in ada_schedule(with_ada[0])[j]:
                            if engine == "pe":
                                ada_beside(n_ada, a, sum(BESIDE[with_ada[0]][0]) - 1)
                                n_ada += 1
                    if with_ada and j == pieces - 1:
                        sums.up(sum(BESIDE[with_ada[0]][1]) * (4 if with_ada[0] == "first" else 2))
                        ada_select(*with_ada[1:])
                for b in banks:
                    bank_n[b].up()

            def ch_group(h, banks, beside=None, pieces=NP2):
                for j in range(pieces):
                    if beside and j in beside:
                        beside[j]()
                    for r in range(PK):
                        kt = PK * j + r
                        wait_tile()
                        for n in range(4):
                            b, co = banks[n // 2], (n % 2) * N
                            if r == 0 and n % 2 == 0:
                                wait_banks(banks, j, b)
                            to = bank[b][:, co:co + N]
                            wh, wl = (w[:, kt % SPLIT, n * P:(n + 1) * P] for w in (whi, wlo))
                            end = kt == PK * pieces - 1
                            nc.tensor.matmul(to, wh, h[0][:, kt, 0:N], start=(kt == 0 and n % 2 == 0), stop=False, skip_group_check=True)
                            nc.tensor.matmul(to, wh, h[1][:, kt, 0:N], start=False, stop=False, skip_group_check=True)
                            last = nc.tensor.matmul(to, wl, h[0][:, kt, 0:N], start=False, stop=end, skip_group_check=True)
                            if end and n == 1:
                                last.then_inc(s_full[b], 1)
                        last.then_inc(s_used, 1)
                        tile.up()
                for b in banks:
                    bank_n[b].up()


            def loop(turns, kinds, body, ada_chunks=0, half="first"):
                on_pe, on_dve = (sum(n) for n in BESIDE[half])
                with pe.Fori(0, turns) as i:
                    tile.enter(i, (K1 if half == "first" else K2) * len(kinds))
                    ada_p.enter(i, ada_chunks * on_pe)
                    beside_p.enter(i, ada_chunks * on_pe)
                    sums.enter(i, ada_chunks * on_dve * (4 if half == "first" else 2))
                    chunk.enter(i, ada_chunks)
                    staged.enter(i, ada_chunks)
                    for b in range(4):
                        bank_n[b].enter(i, uses(kinds, b))
                    body(i)
                for cnt in (tile, ada_p, beside_p, sums, chunk, staged, *bank_n):
                    cnt.leave(turns)

            pe.wait_ge(s_vt, 1)
            for n in range(2):
                pe.wait_ge(s_xe[n], KT // 2)
            (t1, k1), (t2, k2), (t3, k3), (t4, k4) = FIRST
            both = ("first", ada_acc1, (0, 1))
            loop(t1, k1, lambda i: (tok_group(h1, B03, h_wait=(s_h1, PK), with_ada=both, pieces=NP1),
                                    tok_group(h1, B03, with_ada=both, pieces=NP1)), ada_chunks=2)
            for turns, kinds in ((t2, k2), (t3, k3)):
                loop(turns, kinds, lambda i: (ch_group(h1, B01, pieces=NP1), ch_group(h1, B23, pieces=NP1)))
                sums.up(4 * NPO)
                ada_select(ada_acc1, (0, 1), rows=False)

            loop(t4, k4, lambda i: (tok_group(h1, B01, pieces=NP1), tok_group(h1, B01, pieces=NP1)))
            pe.wait_ge(s_h2, K2 + 1)
            (t5, k5), (t6, k6), (t7, k7) = SECOND
            loop(t5, k5, lambda i: (ch_group(h2, B01), ch_group(h2, B23)), half="second")

            def retention(i):

                def k_units(h):
                    def go():
                        if h == 0:
                            pe.wait_ge(s_kr, i + 1)
                            pe.wait_ge(s_ye, i * 4 + 1)
                        else:
                            pe.wait_ge(s_te, i * 6 + 2)
                        for dk in range(2):
                            for t in range(4):
                                last = nc.tensor.transpose(bank[6 + dk][:, t * P:(t + 1) * P],
                                                           k_sb[:, t, h * HD + dk * P:h * HD + (dk + 1) * P], ident)
                            last.then_inc(s_tr, 1)
                    return go

                def q_units():
                    pe.wait_ge(s_qr, i + 1)
                    pe.wait_ge(s_te, i * 6 + 4)
                    for h in range(2):
                        for dk in range(2):
                            for t in range(2):
                                last = nc.tensor.transpose(bank[6 + h][:, dk * N + t * P:dk * N + (t + 1) * P],
                                                           q_sb[:, t, h * HD + dk * P:h * HD + (dk + 1) * P], ident)
                        last.then_inc(s_tr, 1)

                def scores(h):
                    def go():
                        if h == 0:
                            pe.wait_ge(s_te, i * 6 + 6)
                        else:
                            pe.wait_ge(s_pm, i * 4 + 2)
                        for pair in range(2):
                            for m in range(2):
                                key = 2 * pair + m
                                for dk in range(2):
                                    last = nc.tensor.matmul(bank[6 + pair][:, m * N:(m + 1) * N], kT[:, h, dk, key * P:(key + 1) * P],
                                                            qT[:, h, dk, :], start=(dk == 0), stop=(dk == 1))
                            last.then_inc(s_sc, 1)
                    return go

                def attend(h):
                    def go():
                        if h == 0:
                            pe.wait_ge(s_pm, i * 4 + 4)
                            pe.wait_ge(s_free[3], bank_n[3].now())
                        for t in range(2):
                            for key in range(4):
                                last = nc.tensor.matmul(bank[6 + h][:, t * HD:(t + 1) * HD], Pm[:, h, key, t * P:(t + 1) * P],
                                                        v_sb[:, key, h * HD:(h + 1) * HD], start=(key == 0), stop=(key == 3))
                        last.then_inc(s_av, 1)
                    return go

                def y_units():
                    for h in range(2):
                        pe.wait_ge(s_yn, i * 2 + h + 1)
                        for e in range(2):
                            for t in range(2):
                                last = nc.tensor.transpose(bank[6 + h][:, e * N + t * P:e * N + (t + 1) * P],
                                                           q_sb[:, t, h * HD + e * P:h * HD + (e + 1) * P], ident)
                        last.then_inc(s_yt, 1)

                tok_group(h2, B03, with_ada=("second", ada_acc2[0], (0, 0)))
                tok_group(h2, B01)
                tok_group(h2, B03, beside={1: k_units(0), 2: k_units(1), 3: q_units, 4: scores(0), 5: scores(1)},
                          with_ada=("second", ada_acc2[1], (0, 0)))
                ch_group(h2, B23, beside={1: attend(0), 2: attend(1), 5: y_units})

            loop(t6, k6, retention, ada_chunks=2, half="second")

            def ln_sums():
                pe.wait_ge(s_sqd, 16)
                pe.wait_ge(s_one, 1)
                pe.wait_ge(s_ye, 16 + 1)
                for n in range(2):
                    for t in range(2):
                        m = 2 * (2 * n + t)
                        last = nc.tensor.matmul(bank[6][:, m:m + 2], ssum[:, n, t * P:(t + 1) * P], ones_c[:, 0:2], start=True, stop=True)
                last.then_inc(s_lnp, 1)

            def ln_rows():
                pe.wait_ge(s_lnd, 1)
                nc.tensor.matmul(bank[7][:, :], ones[:, :], diag4[:, :, :].rearrange("p a b -> p (a b)"), start=True, stop=True).then_inc(s_lnb, 1)
            ln_sums()
            for i in range(2):
                for cnt, per in ((tile, 2 * K2), *((cnt, 1) for cnt in bank_n)):
                    cnt.enter(i, per)
                ch_group(h2, B01, beside={5: ln_rows} if i == 0 else None)
                ch_group(h2, B23)
            for cnt in (tile, *bank_n):
                cnt.leave(2)

            def gate_rows(i, n):
                pe.wait_ge(s_dg, i * 2 + n + 1)
                nc.tensor.matmul(bank[7][:, :], ones[:, :], diag4[:, :, :].rearrange("p a b -> p (a b)"), start=True, stop=True).then_inc(s_gb, 1)

            def out_turn(i):
                for n, banks in enumerate((B01, B23)):
                    tok_group(ys, banks, beside={NPO - 2: lambda n=n: gate_rows(i, n)}, h_wait=(s_yl, 1), pieces=NPO)
            with pe.Fori(0, 4) as i:
                tile.enter(i, 2 * KT)
                for b in range(4):
                    bank_n[b].enter(i, 1)
                out_turn(i)

        def full_waits(eng):
            n = {b: Count(s_full[b]) for b in range(4)}
            done = Count(s_used)

            def enter(i, groups, pieces=NP2):
                for b in range(4):
                    n[b].enter(i, sum(b in banks[:-1] for _, banks in groups))
                done.enter(i, len(groups) * pieces * PK)

            def leave(turns):
                for cnt in (done, *n.values()):
                    cnt.leave(turns)

            def wait(banks, b):
                if b == banks[-1]:
                    eng.wait_ge(s_used, done.now())
                else:
                    eng.wait_ge(s_full[b], n[b].now())

            def group(banks, pieces=NP2):
                for b in banks[:-1]:
                    n[b].up()
                done.up(pieces * PK)
            return enter, leave, wait, group

        @block.scalar
        def _(act):
            n_split = Count(None)

            def split():
                n, fixed = n_split.now(), n_split.base + n_split.k
                s, to = fixed // PK % RAW, fixed % SPLIT
                act.wait_ge(s_raw[s], n_split.landed(s, RAW, PK))
                if not isinstance(n, int) or n >= SPLIT:
                    act.wait_ge(s_used, n_split.now(SPLIT - 1))
                nc.scalar.activation(whi[:, to, :], raw[:, s, fixed % PK, :], ACT.Copy).then_inc(s_hi, 1)
                n_split.up()

            enter, leave, wait_full, group_done = full_waits(act)
            free_n = [Count(s_free[b], 1) for b in range(4)]
            stored = [Count(s_kept[n], 1) for n in range(2)]
            ada_p = Count(s_ada_used)

            def group(banks, extras=None, evict=None, pieces=NP2, last=False):
                for j in range(2, pieces + 1):
                    if not (last and j == pieces):
                        for _ in range(PK):
                            split()
                    if extras and j in extras:
                        extras[j]()
                group_done(banks, pieces)
                for b in banks:
                    free_n[b].up()
                if evict:
                    evict()
                if not last:
                    for _ in range(PK):
                        split()
                if extras and pieces + 1 in extras:
                    extras[pieces + 1]()

            def rows(per_chunk=NPO):
                act.wait_ge(s_ada_used, ada_p.up(per_chunk))
                nc.scalar.activation(stage[:, :], ADAB[:, :], ACT.Copy).then_inc(s_stage, 1)

            def affine(kt, ready):
                s = kt % 2
                act.wait_ge(ready[0], ready[1])
                for v in range(2):
                    last = nc.scalar.activation(xtmp[:, s, v * N:(v + 1) * N], xT[0][:, kt, v * N:(v + 1) * N],
                                                ACT.Identity, scale=modA[:, kt, v:v + 1], bias=modB[:, kt, v:v + 1])
                last.then_inc(s_t, 1)

            for t in range(4):
                if t == 1:
                    act.wait_ge(s_vec, 14 * 16)
                src = x[0, t * P:(t + 1) * P, :] if t < 2 else ctx_in[0, (t - 2) * P:(t - 1) * P, :]
                act.dma_start(xs[:, t, :], src).then_inc(s_x[t], 16)
            act.wait_ge(s_vt, 1)
            for v in range(2):
                last = nc.scalar.activation(cT[:, :, v], vt[:, 0, 32 * v:32 * v + 32], ACT.Silu)
            last.then_inc(s_cT, 1)
            rows()
            for kt in range(0, KT, 2):
                act.wait_ge(s_xT, kt + 1)
                nc.scalar.activation((xT[0][:, kt, :] if kt < K1 else xT[1][:, kt - K1, :]), XB[kt % 4][:, :], ACT.Copy).then_inc(s_xe[0], 1)
            rows()
            act.wait_ge(s_xe[0], KT // 2)
            act.wait_ge(s_xe[1], KT // 2)
            for i in range(K1 // 4):
                if i:
                    rows()
                    rows()
                if i == K1 // 4 - 1:
                    for _ in range(SPLIT):
                        split()
                act.wait_ge(s_mod, 2 * i + 2)
                for kt in range(4 * i, 4 * i + 4):
                    affine(kt, (s_h1, kt - 1) if kt >= 2 else (s_mod, 2 * i + 2))

            def keep(h, banks):
                act.wait_ge(s_kept[h], stored[h].now())
                wait_full(banks, 2 * h)
                nc.scalar.activation(pst[:, h, 0:G], bank[2 * h][:, :], ACT.Copy).then_inc(s_free[2 * h], 1)
                stored[h].up()

            def loop(turns, kinds, body, ada_pieces=0, halves=(0, 0), pieces=NP2):
                with act.Fori(0, turns) as i:
                    n_split.enter(i, pieces * PK * len(kinds))
                    ada_p.enter(i, ada_pieces)
                    enter(i, kinds, pieces)
                    for b in range(4):
                        free_n[b].enter(i, uses(kinds, b))
                    for h in range(2):
                        stored[h].enter(i, halves[h])
                    body(i)
                leave(turns)
                for cnt in (n_split, ada_p, *free_n, *stored):
                    cnt.leave(turns)

            on_pe = {half: sum(BESIDE[half][0]) for half in BESIDE}
            loop(4, FIRST[0][1], lambda i: [group(B03, {NP1: lambda: rows(on_pe["first"])}, lambda: (keep(0, B03), keep(1, B03)), NP1)
                                            for _ in range(2)],
                 ada_pieces=2 * on_pe["first"], halves=(2, 2), pieces=NP1)

            for turns, kinds in FIRST[1:3]:
                loop(turns, kinds, lambda i: (group(B01, None, lambda: keep(0, B01), NP1), group(B23, None, lambda: keep(1, B23), NP1)),
                     halves=(1, 1), pieces=NP1)

            def affines(kt, r):
                def go():
                    if r == 0:
                        act.wait_ge(s_mod, 2 * (KT // 4))
                    act.wait_ge(s_h2, kt + 1)
                    for v in range(2):
                        last = nc.scalar.activation(xtmp[:, r % 2, v * N:(v + 1) * N], xT[1][:, bass.ds(kt, 1), v * N:(v + 1) * N],
                                                    ACT.Identity, scale=modA[:, bass.ds(kt + K1, 1), v], bias=modB[:, bass.ds(kt + K1, 1), v])
                    last.then_inc(s_t, 1)
                return go

            def q_body(i):
                for g in range(2):
                    group(B01, {2 + r: affines(i * (2 * PER_Q) + (PER_Q * g + r), PER_Q * g + r) for r in range(PER_Q)}, lambda: keep(0, B01), NP1)
            loop(2, FIRST[3][1], q_body, halves=(2, 0), pieces=NP1)

            def d_body(i):
                def sigmoid():
                    act.wait_ge(s_free[1], free_n[1].now())
                    nc.scalar.activation(bb[:, :, :], bb[:, :, :], ACT.Sigmoid).then_inc(s_sig, 1)
                group(B01, None, sigmoid)
                group(B23)
            loop(4, SECOND[0][1], d_body)

            def e_body(i):
                def exps(h):
                    def go():
                        act.wait_ge(s_darg, i * 2 + h + 1)
                        f, b, cb = (lg4[:, h, n:n + 1] for n in range(3))
                        nc.scalar.activation(Dm[:, h, 0:384], Dm[:, h, 0:384], ACT.Exp, scale=f)
                        nc.scalar.activation(Dm[:, h, 384:768], Jc, ACT.Exp, scale=f)
                        nc.scalar.activation(tmp[:, 0:384], tmp[:, 0:384], ACT.Exp, scale=b)
                        nc.scalar.activation(tmp[:, 384:768], Jc, ACT.Exp, scale=b, bias=cb).then_inc(s_dexp, 1)
                    return go

                def square(pair):
                    def go():
                        if pair == 0:
                            act.wait_ge(s_tap, i * 62 + 62)
                        else:
                            act.wait_ge(s_pool_tap, i * 60 + 60)
                            act.wait_ge(s_sqd, i * 4 + 2)
                        nc.scalar.activation(acc[:, :, :], Yc[:, bass.ds(i * 4 + 2 * pair, 2), :], ACT.Square).then_inc(s_sq, 1)
                    return go

                def copy_T(n):
                    def go():
                        for u in (n, n + 1):
                            act.wait_ge(s_tr, i * 6 + u + 1)
                            if u < 4:
                                nc.scalar.activation(kT[:, u // 2, u % 2, :], bank[6 + u % 2][:, :], ACT.Copy, scale=float(HD) ** -0.5).then_inc(s_te, 1)
                            else:
                                nc.scalar.activation(qT[:, u - 4, :, :], bank[6 + u % 2][:, :], ACT.Copy).then_inc(s_te, 1)
                    return go

                def copy_y():
                    for h in range(2):
                        act.wait_ge(s_yt, i * 2 + h + 1)
                        for e in range(2):
                            nc.scalar.activation(y_now[:, 2 * h + e, :], bank[6 + h][:, e * N:(e + 1) * N],
                                                 ACT.Copy, scale=gn4[:, 2 * h + e:2 * h + e + 1]).then_inc(s_ye, 1)

                def silu_g():
                    act.wait_ge(s_free[3], free_n[3].now())
                    nc.scalar.activation(g_sb[:, :, :], g_sb[:, :, :], ACT.Silu).then_inc(s_gs, 1)
                gate_rows = lambda: rows(on_pe["second"])
                group(B03, {3: exps(0), 4: exps(1), NP2: gate_rows})
                group(B01)
                group(B03, {2: copy_T(0), 3: copy_T(2), 4: copy_T(4), 9: square(0), NP2: gate_rows})
                group(B23, {3: square(1), 6: copy_y}, silu_g)
            act.sem_inc(s_ye, 1)
            loop(4, SECOND[1][1], e_body, ada_pieces=2 * on_pe["second"])

            def split_y(m):
                if m == 0:
                    act.wait_ge(s_used, 28 * KT)
                    act.wait_ge(s_yin, 16)
                nc.scalar.activation(ys[0][:, PK * m:PK * m + PK, :], y_tiles(m), ACT.Copy).then_inc(s_yh, 1)

            def ln_rows():
                act.wait_ge(s_lnb, 1)
                nc.scalar.activation(lnm[:, :, :], bank[7][:, :], ACT.Copy).then_inc(s_lnc, 1)

            def z_silu(g):
                def go():
                    act.wait_ge(s_z, g + 1)
                    for n in range(4):
                        ct = 4 * g + n
                        last = nc.scalar.activation(Yc[:, ct, :], Yc[:, ct, :], ACT.Silu, scale=vt[:, 1, 96 + ct:97 + ct], bias=vt[:, 1, 112 + ct:113 + ct])
                    last.then_inc(s_zs, 1)
                return go

            def gate_silu(g):
                def go():
                    if g == 3:
                        for m in range(4):
                            split_y(m)
                    b = 1 + 2 * (g % 2)
                    act.wait_ge(s_free[b], free_n[b].now())
                    buf = (bb, ab)[g % 2]
                    nc.scalar.activation(buf[:, :, :], buf[:, :, :], ACT.Silu).then_inc(s_cg, 1)
                return go
            for i in range(2):
                n_split.enter(i, 2 * K2)
                enter(i, SECOND[2][1])
                for b in range(4):
                    free_n[b].enter(i, 1)
                for n, banks in enumerate((B01, B23)):
                    group(banks, {6: ln_rows if i + n == 0 else (lambda: None), 8: z_silu(2 * i + n)}, gate_silu(2 * i + n))
            leave(2)
            for cnt in (n_split, *free_n):
                cnt.leave(2)

            def out_turn(i, first=False, end=False):
                n_split.enter(i, 2 * KT)
                enter(i, SECOND[2][1], NPO)
                for b in range(4):
                    free_n[b].enter(i, 1)
                for n, banks in enumerate((B01, B23)):
                    def copy_gate():
                        act.wait_ge(s_gb, i * 2 + n + 1)
                        nc.scalar.activation(gpb[:, :], bank[7][:, :], ACT.Copy).then_inc(s_gbe, 1)

                    def squares():
                        for t, b in enumerate(banks):
                            wait_full(banks, b)
                            if not (first and n == 0 and t == 0):
                                act.wait_ge(s_yq, i * 4 + 2 * n + t)
                            nc.scalar.activation(junk[:, :], bank[b][:, :], ACT.Square,
                                                 accum_out=ss[:, t, bass.ds(i * 2 + n, 1)]).then_inc(s_yq, 1)
                    extras = {}
                    if first and n == 0:
                        extras = {j: (lambda m=j + 2: split_y(m)) for j in range(2, NPO - 2)}
                    extras[NPO - 1] = copy_gate
                    group(banks, extras, squares, NPO, last=end and n == 1)
            out_turn(0, first=True)
            with act.Fori(1, 3) as i:
                out_turn(i)
            out_turn(3, end=True)

        @block.vector
        def _(dve):
            n_split = Count(None)

            def split():
                n, fixed = n_split.now(), n_split.base + n_split.k
                s, to = fixed // PK % RAW, fixed % SPLIT
                dve.wait_ge(s_raw[s], n_split.landed(s, RAW, PK))
                dve.wait_ge(s_hi, n + 1)
                if not isinstance(n, int) or n >= SPLIT:
                    dve.wait_ge(s_used, n_split.now(SPLIT - 1))
                nc.vector.tensor_tensor(wlo[:, to, :], raw[:, s, fixed % PK, :], whi[:, to, :].bitcast(F32), ALU.subtract).then_inc(s_lo, 1)
                n_split.up()

            enter, leave, wait_full, group_done = full_waits(dve)
            free_n = [Count(s_free[b], 1) for b in range(4)]
            stored = [Count(s_kept[n], 1) for n in range(2)]
            chunk, biased = Count(None), Count(s_modt)
            beside_n = Count(None, 2 * K1 // 4 * NPO // 2)
            sums = Count(s_ada_sum, 8)

            def ada_sum(acc, j, terms, start=False):
                s = (beside_n.base + beside_n.k) % 2
                dve.wait_ge(s_ada[2 + s], beside_n.landed(s, 2))
                for n, (r, v) in enumerate(terms):
                    to = acc[:, n % 2, :]
                    by = cT[:, PK * j + r, v:v + 1] if isinstance(j, int) else cT[:, bass.ds(j * PK + r, 1), v]
                    if start and n < 2:
                        nc.vector.tensor_scalar(to, ada[:, 2 + s, r, :], by, None, ALU.mult).then_inc(s_ada_sum, 1)
                    else:
                        dve.wait_ge(s_ada_sum, sums.now(1))
                        nc.vector.scalar_tensor_tensor(out=to, in0=ada[:, 2 + s, r, :], scalar=by, in1=to,
                                                       op0=ALU.mult, op1=ALU.add).then_inc(s_ada_sum, 1)
                    sums.up()
                beside_n.up()

            BOTH = [(0, 0), (0, 1), (1, 0), (1, 1)]
            GATE = [(0, 0), (1, 0)]

            def ada_sums(acc, half, b):
                first = next(j for tiles in ada_schedule(half) for e, j in tiles if e == "dve")
                for engine, j in ada_schedule(half)[b]:
                    if engine == "dve":
                        ada_sum(acc, j, BOTH if half == "first" else GATE, start=j == first)

            def group(banks, extras=None, evict=None, pieces=NP2, last=False):
                for j in range(2, pieces + 1):
                    if not (last and j == pieces):
                        for _ in range(PK):
                            split()
                    if extras and j in extras:
                        extras[j]()
                group_done(banks, pieces)
                for b in banks:
                    free_n[b].up()
                if evict:
                    evict()
                if not last:
                    for _ in range(PK):
                        split()
                if extras and pieces + 1 in extras:
                    extras[pieces + 1]()

            def modulation(kind, kt):
                dve.wait_ge(s_sel, chunk.now() + 1)
                got = SELB[:, 0:8].rearrange("p (a v) -> p a v", v=2)
                def cols(t, at_):
                    v = vt[:, t, at_ + kt:at_ + kt + 4] if isinstance(kt, int) else vt[:, t, bass.ds(kt + at_, 4)]
                    return v
                def both(v):
                    return v.unsqueeze(2).broadcast_to([P, 4, 2])
                def kts(m):
                    return m[:, kt:kt + 4, :] if isinstance(kt, int) else m[:, bass.ds(kt, 4), :]
                if kind == "shift":
                    nc.vector.tensor_tensor(kts(modB), got, both(cols(1, 0)), ALU.add).then_inc(s_mod, 1)
                else:
                    nc.vector.tensor_tensor(mtmp[:, :, :], got, both(cols(1, 32 if kind == "scale" else 64)), ALU.add).then_inc(s_modt, 1)
                    dve.wait_ge(s_modt, biased.up())
                    if kind == "scale":
                        nc.vector.scalar_tensor_tensor(out=kts(modA), in0=mtmp[:, :, :], scalar=1.0, in1=both(cols(0, 64)),
                                                       op0=ALU.add, op1=ALU.mult).then_inc(s_mod, 1)
                    else:
                        to = gp[:, bass.ds(kt, 4)]
                        nc.vector.tensor_tensor(to, mtmp[:, :, 0], cols(6, 48), ALU.mult).then_inc(s_mod, 1)
                chunk.up()

            def split_h(kt, s, n, ready, done):
                dve.wait_ge(s_t, n + 1)
                nc.vector.tensor_copy(done[0][0][:, kt, :] if isinstance(kt, int) else done[0][0][:, bass.ds(kt, 1), :], xtmp[:, s, :]).then_inc(s_tf, 1)
                dve.wait_ge(s_tf, n + 1)
                hi, lo = (h[:, kt, :] if isinstance(kt, int) else h[:, bass.ds(kt, 1), :] for h in done[0])
                nc.vector.tensor_tensor(lo, xtmp[:, s, :] if isinstance(kt, int) else xtmp[:, s:s + 1, :], hi.bitcast(F32), ALU.subtract).then_inc(done[1], 1)

            nc.vector.memset(vin[:, :, :], 0.0).then_inc(s_zero, 1)
            nc.vector.memset(ADAB[:, :], 0.0).then_inc(s_clear, 1)
            dve.sem_inc(s_lo, LO0)
            dve.sem_inc(s_h2, 1)
            dve.sem_inc(s_ada_sum, 8)
            dve.wait_ge(s_const, 16)
            dve.wait_ge(s_lg, 32)
            nc.vector.tensor_copy(lgs[:, :, 0], lgrow[:, 0, :])
            nc.vector.tensor_scalar(lgs[:, :, 1], lgrow[:, 1, :], -1.0, None, ALU.mult)
            nc.vector.tensor_scalar(lgs[:, :, 2], lgrow[:, 1, :], 2.0 * N, None, ALU.mult).then_inc(s_lgs, 1)
            dve.wait_ge(s_vT, 1)
            nc.vector.tensor_copy(vt[:, 0:4, :], bank[0][:, :])
            nc.vector.tensor_copy(vt[:, 4:7, :], bank[1][:, 0:3 * P]).then_inc(s_vt, 1)
            dve.wait_ge(s_vt, 1)
            for t in range(4):
                dve.wait_ge(s_x[t], 16)
                for n in range(8):
                    last = nc.vector.bn_stats(bst[:, t, n, :], xs[:, t, n * G:(n + 1) * G])
                last.then_inc(s_bn, 1)
                dve.wait_ge(s_bn, 3 * t + 1)
                nc.vector.bn_aggr(mv[:, t, :], bst[:, t, :, :]).then_inc(s_bn, 1)
                dve.wait_ge(s_bn, 3 * t + 2)
                nc.vector.scalar_tensor_tensor(out=rs[:, t:t + 1], in0=mv[:, t, 0:1], scalar=mv[:, t, 0:1], in1=mv[:, t, 1:2],
                                               op0=ALU.mult, op1=ALU.add).then_inc(s_bn, 1)
                dve.wait_ge(s_bn, 3 * t + 3)
                nc.vector.tensor_scalar(rs[:, t:t + 1], rs[:, t:t + 1], EPS, None, ALU.add).then_inc(s_ms, 1)
            for t in range(4):
                dve.wait_ge(s_rstd, t + 1)
                nc.vector.tensor_scalar(diag[:, t, :], ident, rs[:, t:t + 1], None, ALU.mult).then_inc(s_diag, 1)
            modulation("shift", 0)
            for kt in range(1, KT, 2):
                dve.wait_ge(s_xT, kt + 1)
                nc.vector.tensor_copy((xT[0][:, kt, :] if kt < K1 else xT[1][:, kt - K1, :]), XB[kt % 4][:, :]).then_inc(s_xe[1], 1)
            modulation("scale", 0)
            for i in range(K1 // 4):
                if i:
                    modulation("shift", 4 * i)
                    modulation("scale", 4 * i)
                if i == K1 // 4 - 1:
                    for _ in range(SPLIT):
                        split()
                for kt in range(4 * i, 4 * i + 4):
                    split_h(kt, kt % 2, kt, None, (h1, s_h1))

            def keep(h, banks):
                dve.wait_ge(s_kept[h], stored[h].now())
                wait_full(banks, 2 * h + 1)
                nc.vector.tensor_copy(pst[:, h, G:2 * G], bank[2 * h + 1][:, :]).then_inc(s_free[2 * h + 1], 1)
                stored[h].up()

            def loop(turns, kinds, body, chunks=0, two_step=0, halves=(0, 0), half="first", late=0):
                pieces = NP1 if half == "first" else NP2
                with dve.Fori(0, turns) as i:
                    n_split.enter(i, pieces * PK * len(kinds))
                    on_dve = chunks * sum(BESIDE[half][1]) + late
                    beside_n.enter(i, on_dve)
                    sums.enter(i, on_dve * (4 if half == "first" else 2))
                    chunk.enter(i, chunks)
                    biased.enter(i, two_step)
                    enter(i, kinds, pieces)
                    for b in range(4):
                        free_n[b].enter(i, uses(kinds, b))
                    for h in range(2):
                        stored[h].enter(i, halves[h])
                    body(i)
                leave(turns)
                for cnt in (n_split, chunk, biased, beside_n, sums, *free_n, *stored):
                    cnt.leave(turns)

            in_first = {b + 2: lambda b=b: ada_sums(ada_acc1, "first", b) for b in range(NP1 - 1)}
            loop(4, FIRST[0][1], lambda i: [group(B03, {**in_first, NP1 + 1: lambda kind=kind: modulation(kind, i * 4 + K1)},
                                                  lambda: (keep(0, B03), keep(1, B03)), NP1) for kind in ("shift", "scale")],
                 chunks=2, two_step=1, halves=(2, 2))

            for n, (turns, kinds) in enumerate(FIRST[1:3]):
                nc.vector.memset(ada_acc1[:, :, :], 0.0).then_inc(s_late, 1)
                dve.wait_ge(s_late, n + 1)

                def late_body(i):
                    for g, h in ((0, 0), (1, 1)):
                        banks = (B01, B23)[g]
                        extras = {b + 2: lambda m=m: ada_sum(ada_acc1, i * 4 + (2 * g + m), BOTH) for m, b in enumerate(LATE)}
                        group(banks, extras, lambda: keep(h, banks), NP1)
                loop(turns, kinds, late_body, halves=(1, 1), late=2 * len(LATE))
                modulation(("shift", "scale")[n], KT - 4)

            def q_body(i):
                def splits(m):
                    kt = i * (2 * PER_Q) + m
                    return lambda: split_h(kt, m % 2, kt + K1, None, (h2, s_h2))
                for g in range(2):
                    group(B01, {2 + r: splits(PER_Q * g + r) for r in range(PER_Q)}, lambda: keep(0, B01), NP1)
            loop(2, FIRST[3][1], q_body, halves=(2, 0))

            def complete(buf, banks, b):
                wait_full(banks, b)
                nc.vector.tensor_tensor(buf, buf, bank[b][:, :], ALU.add).then_inc(s_free[b], 1)

            def ch_part(buf, n):
                return buf[:, 2 * n:2 * n + 2, :].rearrange("p a b -> p (a b)")

            dve.sem_inc(s_u, 1)

            def d_body(i):
                def take_b():
                    dve.wait_ge(s_pin["b"], i * 16 + 16)
                    for n in range(2):
                        complete(ch_part(bb, n), B01, n)

                def take_a():
                    dve.wait_ge(s_pin["a"], i * 16 + 16)
                    for n in range(2):
                        complete(ch_part(ab, n), B23, 2 + n)
                    dve.wait_ge(s_sig, i + 1)
                    dve.wait_ge(s_free[3], free_n[3].now())
                    nc.vector.tensor_tensor(Yc[:, bass.ds(i * 4, 4), :], ab[:, :, :], bb[:, :, :], ALU.mult).then_inc(s_u, 1)
                group(B01, None, take_b)
                group(B23, None, take_a)
            loop(4, SECOND[0][1], d_body, half="second")

            dve.wait_ge(s_kept[0], 21)
            dve.wait_ge(s_kept[1], 17)
            nc.vector.memset(upad[:, :, :], 0.0)
            nc.vector.memset(ones_c[:, :], 1.0 / RET).then_inc(s_one, 1)
            nc.vector.memset(ssum[:, :, :], 0.0)
            dve.wait_ge(s_u, 5)

            def e_body(i):
                tap = Count(s_tap)
                tap.enter(i, 62)

                def prepare():
                    dve.wait_ge(s_ye, i * 4 + 1)
                    for t, k, n in TAP_TILES:
                        src = vt[:, t, 0:16 * n].rearrange("p (k c) -> p k c", c=16)[:, :, bass.ds(i * 4, 4)]
                        nc.vector.tensor_copy(w4[:, k:k + n, :], src)
                    nc.vector.tensor_copy(b4[:, :], vt[:, 0, bass.ds(i * 4 + 96, 4)])
                    nc.vector.tensor_copy(gn4[:, :], vt[:, 0, bass.ds(i * 4 + 112, 4)])
                    nc.vector.tensor_copy(lg4[:, :, :], lgs[:, bass.ds(i * 2, 2), :]).then_inc(s_prep, 1)
                    dve.wait_ge(s_prep, i + 1)

                def args(h):
                    if h == 1:
                        dve.wait_ge(s_dm, i * 2 + 1)
                    nc.vector.tensor_scalar(Dm[:, h, 0:384], Jl, 0.0, None, ALU.max)
                    nc.vector.tensor_scalar(tmp[:, 0:384], Jl, 0.0, None, ALU.min).then_inc(s_darg, 1)

                def combine(h):
                    dve.wait_ge(s_dexp, i * 2 + h + 1)
                    nc.vector.scalar_tensor_tensor(out=Dm[:, h, 0:384], in0=Jl, scalar=0.0, in1=Dm[:, h, 0:384], op0=ALU.is_ge, op1=ALU.mult)
                    nc.vector.scalar_tensor_tensor(out=tmp[:, 0:384], in0=Jl, scalar=0.0, in1=tmp[:, 0:384],
                                                   op0=ALU.is_le, op1=ALU.mult).then_inc(s_dmask, 1)
                    dve.wait_ge(s_dmask, i * 2 + h + 1)
                    nc.vector.tensor_tensor(Dm[:, h, :], Dm[:, h, :], tmp[:, 0:768], ALU.add).then_inc(s_dm, 1)

                def pad(to, pair):
                    for n in range(2):
                        last = nc.vector.tensor_copy(to[:, n, TAPS // 2:TAPS // 2 + N], Yc[:, bass.ds(i * 4 + (2 * pair + n), 1), :])
                    last.then_inc(s_cu, 1)

                def start_pool_taps():
                    for edge in (0, TAPS // 2 + N):
                        nc.vector.memset(upad2[:, :, edge:edge + TAPS // 2], 0.0)
                    pad(upad2, 1)
                    dve.wait_ge(s_cu, i * 2 + 1)
                    for n in range(2):
                        last = nc.vector.tensor_scalar(Yc[:, bass.ds(i * 4 + (2 + n), 1), :], upad2[:, n:n + 1, 0:N],
                                                       w4[:, 0, 2 + n:3 + n], b4[:, 2 + n:3 + n], ALU.mult, ALU.add)
                    last.then_inc(s_tap0, 1)
                    pad(upad, 0)
                    dve.wait_ge(s_cu, i * 2 + 2)

                def taps(first, last_):
                    for k in range(first, last_):
                        for n in range(2):
                            w = w4[:, k, n:n + 1]
                            src = upad[:, n, k:k + N]
                            if k == 0:
                                nc.vector.tensor_scalar(acc[:, n, :], src, w, b4[:, n:n + 1], ALU.mult, ALU.add).then_inc(s_tap, 1)
                            else:
                                dve.wait_ge(s_tap, tap.now(1))
                                to = acc[:, n, :] if k < TAPS - 1 else Yc[:, bass.ds(i * 4 + n, 1), :]
                                nc.vector.scalar_tensor_tensor(out=to, in0=src, scalar=w, in1=acc[:, n, :], op0=ALU.mult, op1=ALU.add).then_inc(s_tap, 1)
                            tap.up()
                    if last_ == TAPS:
                        dve.wait_ge(s_tap, tap.now())
                        add_u(0)

                def add_u(pair):
                    for n in range(2):
                        nc.vector.tensor_tensor(ssum[:, 0:1, :], ssum[:, 0:1, :], Yc[:, bass.ds(i * 4 + (2 * pair + n), 1), :], ALU.add).then_inc(s_su, 1)
                        dve.wait_ge(s_su, i * 4 + 2 * pair + n + 1)

                def add_squares(pair):
                    def go():
                        if pair == 1:
                            dve.wait_ge(s_pool_tap, i * 60 + 60)
                            add_u(1)
                        dve.wait_ge(s_sq, i * 2 + pair + 1)
                        for n in range(2):
                            nc.vector.tensor_tensor(ssum[:, 1, :], ssum[:, 1, :], acc[:, n, :], ALU.add).then_inc(s_sqd, 1)
                            dve.wait_ge(s_sqd, i * 4 + 2 * pair + n + 1)
                    return go

                def rotate(buf, done):
                    sin = cst[:, C_SIN:C_SIN + 512].rearrange("p (t a s f) -> p t a s f", t=2, a=2, s=2)
                    rt = tmp[:, :].rearrange("p (t h a s f) -> p t h a s f", t=2, h=2, a=2, s=2)
                    for t in range(2):
                        for h in range(2):
                            src = buf[:, t, h * HD:(h + 1) * HD].rearrange("p (a s f) -> p a s f", a=2, s=2)[:, :, ::-1, :]
                            last = nc.vector.tensor_tensor(rt[:, t, h], src, sin[:, t], ALU.mult)
                    last.then_inc(s_rope, 1)
                    step = 4 * i + (0 if done is s_kr else 2)
                    dve.wait_ge(s_rope, step + 1)
                    v = buf[:, 0:2, :].rearrange("p t (h d) -> p t h d", h=2)
                    cos = cst[:, C_COS:C_COS + 512].rearrange("p (t d) -> p t d", t=2).unsqueeze(2).broadcast_to([P, 2, 2, HD])
                    nc.vector.tensor_tensor(v, v, cos, ALU.mult).then_inc(s_rope, 1)
                    dve.wait_ge(s_rope, step + 2)
                    flat = buf[:, 0:2, :].rearrange("p t d -> p (t d)")
                    nc.vector.tensor_tensor(flat, flat, tmp[:, :], ALU.add).then_inc(done, 1)

                def take(names, buf, banks):
                    def go():
                        for name in names:
                            dve.wait_ge(s_pin[name], i * 16 + 16)
                        for t, b in enumerate(banks):
                            complete(buf[:, t, :], banks, b)
                        dve.wait_ge(s_free[banks[-1]], free_n[banks[-1]].now())
                    return go

                def weights(h):
                    def go():
                        for pair in range(2):
                            dve.wait_ge(s_sc, i * 4 + 2 * h + pair + 1)
                            for m in range(2):
                                w = pair * 384 + (P if m == 0 else 0)
                                last = nc.vector.tensor_tensor(Pm[:, h, 2 * pair + m, :], bank[6 + pair][:, m * N:(m + 1) * N], Dm[:, h, w:w + N], ALU.mult)
                            last.then_inc(s_pm, 1)
                    return go

                def gn_stats(h):
                    def go():
                        dve.wait_ge(s_av, i * 2 + h + 1)
                        for t in range(2):
                            last = nc.vector.bn_stats(bst[:, 2 * h + t, 0, :], bank[6 + h][:, t * HD:(t + 1) * HD])
                        last.then_inc(s_gst, 1)
                        dve.wait_ge(s_bn, 12)
                        dve.wait_ge(s_gst, i * 2 + h + 1)
                        for t in range(2):
                            last = nc.vector.bn_aggr(mv[:, 2 * h + t, :], bst[:, 2 * h + t, 0, :])
                        last.then_inc(s_gag, 1)
                        dve.wait_ge(s_gag, i * 2 + h + 1)
                        nc.vector.tensor_scalar(rs[:, 2 * h:2 * h + 2], mv[:, 2 * h:2 * h + 2, 1], EPS, None, ALU.add).then_inc(s_gnin, 1)
                    return go

                def gn_apply():
                    for h in range(2):
                        dve.wait_ge(s_gnr, i * 2 + h + 1)
                        for t in range(2):
                            n = 2 * h + t
                            last = nc.vector.tensor_scalar(q_sb[:, t, h * HD:(h + 1) * HD], bank[6 + h][:, t * HD:(t + 1) * HD],
                                                           mv[:, n, 0:1], rs[:, n:n + 1], ALU.subtract, ALU.mult)
                        last.then_inc(s_yn, 1)

                def take_g():
                    dve.wait_ge(s_pin["g"], i * 16 + 16)
                    for n in range(2):
                        complete(ch_part(g_sb, n), B23, 2 + n)

                def ada_k(b):
                    ada_sums(ada_acc2[0], "second", b)

                def ada_v(b):
                    dve.wait_ge(s_qr, i + 1)
                    ada_sums(ada_acc2[1], "second", b)

                group(B03, {2: lambda: (prepare(), args(0), start_pool_taps()), 3: lambda: (combine(0), args(1), ada_k(1)),
                            4: lambda: (combine(1), ada_k(2)), 5: lambda: (ada_k(3), taps(0, 2)), 6: lambda: (ada_k(4), taps(2, 6)),
                            7: lambda: (ada_k(5), taps(6, 10)), 8: lambda: (ada_k(6), taps(10, 14)), 9: lambda: (ada_k(7), taps(14, 17)),
                            NP2 + 1: lambda: modulation("gate", i * 8)},
                      take(("k", "kc"), k_sb, B03))
                group(B01, {2: lambda: rotate(k_sb, s_kr), **{j: lambda j=j: taps(12 + j, 13 + j) for j in range(5, 10)}},
                      take(("q",), q_sb, B01))
                group(B03, {2: lambda: rotate(q_sb, s_qr), 3: lambda: (ada_v(1), taps(22, 25)), 4: lambda: (ada_v(2), taps(25, 27)),
                            5: lambda: (weights(0)(), ada_v(3)), 6: lambda: (weights(1)(), ada_v(4)),
                            7: lambda: (ada_v(5), taps(27, 29)), 8: lambda: (ada_v(6), taps(29, TAPS)), 9: lambda: ada_v(7),
                            NP2 + 1: lambda: modulation("gate", i * 8 + 4)},
                      take(("v", "vc"), v_sb, B03))
                group(B23, {2: lambda: (gn_stats(0)(), add_squares(0)()), 3: gn_stats(1), 4: gn_apply, 6: add_squares(1)}, take_g)
            loop(4, SECOND[1][1], e_body, chunks=2, two_step=2, half="second")

            def ln_stats():
                dve.wait_ge(s_yg, 5)
                nc.vector.memset(ones[:, :], 1.0).then_inc(s_one, 1)
                dve.wait_ge(s_lnp, 1)
                nc.vector.tensor_copy(lnt[:, :], bank[6][:, 0:8:2]).then_inc(s_ln, 1)
                dve.wait_ge(s_ln, 1)
                nc.vector.tensor_tensor(lnq[:, :], lnt[:, 0:2], lnt[:, 0:2], ALU.mult).then_inc(s_ln, 1)
                dve.wait_ge(s_ln, 2)
                nc.vector.scalar_tensor_tensor(out=lnt[:, 2:4], in0=lnt[:, 2:4], scalar=EPS, in1=lnq[:, :],
                                               op0=ALU.add, op1=ALU.subtract).then_inc(s_lnvar, 1)

            def ln_diag():
                dve.wait_ge(s_lnr, 1)
                nc.vector.tensor_tensor(diag4[:, :, :], ident.unsqueeze(1).broadcast_to([P, 4, P]),
                                        lnt[:, :].unsqueeze(2).broadcast_to([P, 4, P]), ALU.mult).then_inc(s_lnd, 1)

            def z(g):
                def go():
                    dve.wait_ge(s_lnc, 1)
                    u = Yc[:, 4 * g:4 * g + 4, :]
                    m, r = (lnm[:, n, :].unsqueeze(1).broadcast_to([P, 4, N]) for n in range(2))
                    nc.vector.tensor_tensor(u, u, m, ALU.subtract).then_inc(s_zc, 1)
                    dve.wait_ge(s_zc, g + 1)
                    nc.vector.tensor_tensor(u, u, r, ALU.mult).then_inc(s_z, 1)
                return go

            def split_y(m):
                dve.wait_ge(s_yh, m + 1)
                nc.vector.tensor_tensor(ys[1][:, PK * m:PK * m + PK, :], y_tiles(m),
                                        ys[0][:, PK * m:PK * m + PK, :].bitcast(F32), ALU.subtract).then_inc(s_yl, 1)

            def conv_gate(g, banks):
                def go():
                    if g == 3:
                        for m in range(4):
                            split_y(m)
                    buf = (bb, ab)[g % 2]
                    dve.wait_ge(s_pin[f"c{g % 2}"], 16 * (g // 2 + 1))
                    for n in range(2):
                        complete(ch_part(buf, n), banks, banks[n])
                return go

            def conv_mult(g):
                dve.wait_ge(s_zs, g + 1)
                dve.wait_ge(s_cg, g + 1)
                u = Yc[:, 4 * g:4 * g + 4, :]
                nc.vector.tensor_tensor(u, u, (bb, ab)[g % 2][:, :, :], ALU.mult).then_inc(s_cy, 1)
            for i in range(2):
                n_split.enter(i, 2 * K2)
                enter(i, SECOND[2][1])
                for b in range(4):
                    free_n[b].enter(i, 1)
                for n, banks in enumerate((B01, B23)):
                    g = 2 * i + n
                    extras = {7: z(g)}
                    if g == 0:
                        extras[2], extras[4] = ln_stats, ln_diag
                    else:
                        extras[3] = lambda g=g: conv_mult(g - 1)
                    group(banks, extras, conv_gate(g, banks))
            leave(2)
            for cnt in (n_split, *free_n):
                cnt.leave(2)

            def out_turn(i, first=False, end=False):
                n_split.enter(i, 2 * KT)
                enter(i, SECOND[2][1], NPO)
                for b in range(4):
                    free_n[b].enter(i, 1)
                for n, banks in enumerate((B01, B23)):
                    def gate_diag():
                        v = gp[:, bass.ds(i * 8 + 4 * n, 4)].unsqueeze(2).broadcast_to([P, 4, P])
                        nc.vector.tensor_tensor(diag4[:, :, :], ident.unsqueeze(1).broadcast_to([P, 4, P]), v, ALU.mult).then_inc(s_dg, 1)

                    def gated():
                        dve.wait_ge(s_gbe, i * 2 + n + 1)
                        for t, b in enumerate(banks):
                            dve.wait_ge(s_yq, i * 4 + (2 * n + t + 1))
                            wait_full(banks, b)
                            nc.vector.tensor_tensor(yo[:, t, bass.ds(i * (2 * G) + n * G, G)], bank[b][:, :], gpb[:, :], ALU.mult).then_inc(s_free[b], 1)
                    extras = {}
                    if first and n == 0:
                        extras = {j: (lambda m=j + 2: split_y(m)) for j in range(2, NPO - 2)}
                        extras[2] = lambda: (conv_mult(3), dve.wait_ge(s_cy, 4), split_y(4), gate_diag())
                    else:
                        extras[2] = gate_diag
                    group(banks, extras, gated, NPO, last=end and n == 1)
            out_turn(0, first=True)
            with dve.Fori(1, 3) as i:
                out_turn(i)
            out_turn(3, end=True)

            dve.wait_ge(s_yq, 16)
            nc.vector.tensor_reduce(rs[:, 0:2], ss[:, :, :], AX.X, ALU.add).then_inc(s_fin, 1)
            dve.wait_ge(s_fin, 1)
            nc.vector.tensor_scalar(rs[:, 0:2], rs[:, 0:2], 1.0 / D, EPS, ALU.mult, ALU.add).then_inc(s_var, 1)
            dve.wait_ge(s_frs, 1)
            dve.wait_ge(s_res, 32)
            dve.wait_ge(s_free[1], free_n[1].now())
            dve.wait_ge(s_free[3], free_n[3].now())
            for t in range(2):
                for q in range(4):
                    y = yo[:, t, q * 1024:(q + 1) * 1024]
                    nc.vector.scalar_tensor_tensor(out=y, in0=y, scalar=rs[:, t:t + 1], in1=xres[t][:, q * 1024:(q + 1) * 1024],
                                                   op0=ALU.mult, op1=ALU.add).then_inc(s_o, 1)

        @block.gpsimd
        def _(pool):
            nc.gpsimd.memset(half[:, :], -0.5).then_inc(s_half, 1)
            for h in range(2):
                pool.sem_inc(s_kept[h], 1)
            pool.wait_ge(s_half, 1)
            for t in range(4):
                pool.wait_ge(s_ms, t + 1)
                nc.gpsimd.tensor_tensor(rs[:, t:t + 1], rs[:, t:t + 1], half[:, 0:1], ALU.pow).then_inc(s_rstd, 1)

            free_n = [Count(s_free[b], 1) for b in range(4)]
            kept = [Count(s_pst[h]) for h in range(2)]

            def store(h, to):
                pool.wait_ge(s_half, 1)
                for b in (2 * h, 2 * h + 1):
                    free_n[b].up()
                    pool.wait_ge(s_free[b], free_n[b].now())
                pool.dma_start(to, pst[:, h, :]).then_inc(s_pst[h], 16)
                pool.wait_ge(s_pst[h], kept[h].up(16))
                pool.sem_inc(s_kept[h], 1)

            def loop(turns, kinds, halves, body):
                with pool.Fori(0, turns) as i:
                    for b in range(4):
                        free_n[b].enter(i, uses(kinds, b))
                    for h in range(2):
                        kept[h].enter(i, 16 * halves[h])
                    body(i)
                for cnt in (*free_n, *kept):
                    cnt.leave(turns)

            def slot(t, n):
                return t[bass.ds(n, 1), :, :].rearrange("a p n -> (a p) n")
            loop(4, FIRST[0][1], (2, 2), lambda i: (store(0, slot(part, i + 4)), store(1, slot(part_c, i)),
                                            store(0, slot(part, i + 8)), store(1, slot(part_c, i + 4))))
            loop(2 * LATE_TURNS, FIRST[1][1], (1, 1), lambda i: (store(0, slot(part, i * 2 + 12)), store(1, slot(part, i * 2 + 13))))
            loop(2, FIRST[3][1], (2, 0), lambda i: (store(0, slot(part, i * 2)), store(0, slot(part, i * 2 + 1))))
            pool.wait_ge(s_pst[0], 16 * 20)
            pool.wait_ge(s_pst[1], 16 * 16)
            pool.wait_ge(s_used, 28 * K1)

            def fetch(name, buf, src):
                pool.dma_start(buf, src).then_inc(s_pin[name], 16)

            def flat(t):
                return t.rearrange("p a b -> p (a b)")
            with pool.Fori(0, 4) as i:
                pool.wait_ge(s_half, 1)
                pool.wait_ge(s_u, i + 1)
                fetch("b", flat(bb[:, :, :]), slot(part, i + 20))
                fetch("a", flat(ab[:, :, :]), slot(part, i + 16))
            pool.wait_ge(s_u, 5)
            pool.sem_inc(s_yg, 1)
            with pool.Fori(0, 4) as i:
                pool.wait_ge(s_half, 1)
                pool.wait_ge(s_yg, i + 1)
                fetch("k", flat(k_sb[:, 0:2, :]), slot(part, i + 4))
                fetch("kc", flat(k_sb[:, 2:4, :]), slot(part_c, i))
                fetch("q", flat(q_sb[:, :, :]), slot(part, i))
                pool.wait_ge(s_tap0, i + 1)
                for k in range(1, TAPS):
                    w = w4[:, k, 2:4].unsqueeze(2).broadcast_to([P, 2, N])
                    if k > 1:
                        pool.wait_ge(s_pool_tap, i * 60 + 2 * (k - 1))
                    nc.gpsimd.tensor_tensor(prod[:, :, :], upad2[:, :, k:k + N], w, ALU.mult).then_inc(s_pool_tap, 1)
                    pool.wait_ge(s_pool_tap, i * 60 + 2 * k - 1)
                    nc.gpsimd.tensor_tensor(idle[:, :], half[:, 0:2], half[:, 0:2], ALU.add)
                    y2 = Yc[:, bass.ds(i * 4 + 2, 2), :]
                    nc.gpsimd.tensor_tensor(y2, y2, prod[:, :, :], ALU.add).then_inc(s_pool_tap, 1)
                pool.wait_ge(s_half, 1)
                pool.wait_ge(s_pool_tap, i * 60 + 60)
                fetch("v", flat(v_sb[:, 0:2, :]), slot(part, i + 8))
                fetch("vc", flat(v_sb[:, 2:4, :]), slot(part_c, i + 4))
                pool.wait_ge(s_half, 1)
                pool.wait_ge(s_av, i * 2 + 2)
                fetch("g", flat(g_sb[:, :, :]), slot(part, i + 12))
                for h in range(2):
                    pool.wait_ge(s_gnin, i * 2 + h + 1)
                    nc.gpsimd.tensor_tensor(rs[:, 2 * h:2 * h + 2], rs[:, 2 * h:2 * h + 2], half[:, 0:2], ALU.pow).then_inc(s_gnr, 1)
                pool.wait_ge(s_gs, i + 1)
                pool.wait_ge(s_ye, i * 4 + 5)
                nc.gpsimd.tensor_tensor(y_now[:, :, :], y_now[:, :, :], g_sb[:, :, :], ALU.mult).then_inc(s_gy, 1)
                pool.wait_ge(s_half, 1)
                pool.wait_ge(s_gy, i + 1)
                pool.dma_start(slot(y_ret, i), flat(y_now[:, :, :])).then_inc(s_yst, 16)
                pool.wait_ge(s_yst, i * 16 + 16)
                pool.sem_inc(s_yg, 1)
            pool.wait_ge(s_yg, 5)
            pool.wait_ge(s_mod, 2 * (KT // 4) + 8)
            pool.dma_start(Yr[:, :, :].rearrange("p (n a) b -> p n (a b)", n=4), y_ret.rearrange("n p c -> p n c")).then_inc(s_yin, 16)
            fetch("c0", flat(bb[:, :, :]), slot(part, 24))
            fetch("c1", flat(ab[:, :, :]), slot(part, 25))
            pool.wait_ge(s_lnvar, 1)
            nc.gpsimd.tensor_tensor(lnt[:, 2:4], lnt[:, 2:4], half[:, 0:2], ALU.pow).then_inc(s_lnr, 1)
            for g in range(2):
                pool.wait_ge(s_cy, g + 1)
                fetch(f"c{g}", flat((bb, ab)[g][:, :, :]), slot(part, 26 + g))
            pool.wait_ge(s_var, 1)
            nc.gpsimd.tensor_tensor(rs[:, 0:2], rs[:, 0:2], half[:, 0:2], ALU.pow).then_inc(s_frs, 1)


_INS = ["x", "c", "ctx", "c_ctx", "ada_w", "ada_b", "pre_norm_g", "post_norm_g", "w_in", "ret_log_decay_fwd",
        "ret_log_decay_bwd", "ret_gn_g", "conv_dw_w", "conv_dw_b", "conv_ln_g", "conv_ln_b", "w_out"]


def kernel(**inputs):
    import concourse.bacc as bacc
    from concourse.bass_utils import run_bass_kernel_spmd

    nc = bacc.Bacc("TRN2", target_bir_lowering=False, num_devices=1)
    arrays, args = {}, []
    for name in _INS:
        a = np.ascontiguousarray(inputs[name])
        if name == "c_ctx":
            a = a.reshape(1, D)
        arrays[f"in_{name}"] = a
        args.append(nc.dram_tensor(f"in_{name}", a.shape, mybir.dt.from_np(a.dtype), kind="ExternalInput").ap())
    consts = shape_constants()
    arrays["shape_constants"] = consts
    args.append(nc.dram_tensor("shape_constants", consts.shape, F32, kind="ExternalInput").ap())
    args.append(nc.dram_tensor("out", (1, N, D), F32, kind="ExternalOutput").ap())
    block_kernel(nc, *args)
    r = run_bass_kernel_spmd(nc, [arrays], core_ids=[0])
    return r.results[0]["out"]
```
